# Optimizing a Trainium2 kernel written in Bass

```python
import math
import jax, jax.numpy as jnp
from jax import lax
import numpy as np

D_MODEL = 1024
BATCH = 1
SEQ = 256
DEPTH = 2

N_A_LAYERS = DEPTH // 2
N_B_LAYERS = DEPTH - N_A_LAYERS
PLE_DIM = 256
DN_ALPHA = (2.0 * DEPTH) ** 0.25
DN_BETA = (8.0 * DEPTH) ** -0.25
NORM_EPS = 1e-5

ML_HEADS = 8
ML_QK_DIM = D_MODEL // (2 * ML_HEADS)
ML_V_DIM = D_MODEL // ML_HEADS
ML_CHUNK = 64
ML_Q_END = ML_HEADS * ML_QK_DIM
ML_K_END = 2 * ML_HEADS * ML_QK_DIM
ML_V_END = ML_K_END + ML_HEADS * ML_V_DIM
ML_I_END = ML_V_END + ML_HEADS
ML_F_END = ML_I_END + ML_HEADS
ML_IN_COLS = ML_F_END + D_MODEL

MLA_HEADS = 8
MLA_NOPE_DIM = 128
MLA_ROPE_DIM = 64
MLA_V_DIM = 128
MLA_KV_RANK = 256
MLA_Q_RANK = 384
ROPE_THETA = 10000.0
ATTN_BLOCK = 128

PEER_HEADS = 8
PEER_N_KEYS = 128
PEER_N_EXPERTS = PEER_N_KEYS * PEER_N_KEYS
PEER_KEY_DIM = 256
PEER_HALF = PEER_KEY_DIM // 2
PEER_TOPK = 16
PEER_BLOCK = 128


def layer_norm(x, g, b):
    xf = x.astype(jnp.float32)
    mu = jnp.mean(xf, -1, keepdims=True)
    var = jnp.mean(jnp.square(xf - mu), -1, keepdims=True)
    y = (xf - mu) * lax.rsqrt(var + NORM_EPS)
    return (y * g.astype(jnp.float32) + b.astype(jnp.float32)).astype(x.dtype)

def rms_norm(x, g):
    xf = x.astype(jnp.float32)
    y = xf * lax.rsqrt(jnp.mean(jnp.square(xf), -1, keepdims=True) + NORM_EPS)
    return (y * g.astype(jnp.float32)).astype(x.dtype)

def rope_angles(positions, dim):
    inv_freq = ROPE_THETA ** (-jnp.arange(0, dim, 2, dtype=jnp.float32) / dim)
    ang = positions.astype(jnp.float32)[..., None] * inv_freq
    return jnp.cos(ang), jnp.sin(ang)

def apply_rope(x, cos, sin):
    xf = x.astype(jnp.float32)
    x1, x2 = jnp.split(xf, 2, axis=-1)
    return jnp.concatenate([x1 * cos - x2 * sin, x1 * sin + x2 * cos], -1).astype(x.dtype)

def mlstm_chunk_step(carry, inp):
    C, n, m = carry
    q, k, v, ig, lf = inp
    L = q.shape[2]
    b = jnp.cumsum(lf, axis=-1)
    causal = jnp.tril(jnp.ones((L, L), dtype=bool))
    log_w = jnp.where(causal, b[..., :, None] - b[..., None, :] + ig[..., None, :], -jnp.inf)
    log_inter = b + m[..., None]
    m_t = jnp.maximum(log_inter, jnp.max(log_w, -1))
    w = jnp.exp(log_w - m_t[..., None])
    s_inter = jnp.exp(log_inter - m_t)
    qk = jnp.einsum('bhtd,bhsd->bhts', q, k) * w
    num = jnp.einsum('bhts,bhsv->bhtv', qk, v) + s_inter[..., None] * jnp.einsum('bhtd,bhdv->bhtv', q, C)
    den = jnp.sum(qk, -1) + s_inter * jnp.einsum('bhtd,bhd->bht', q, n)
    h = num / jnp.maximum(jnp.abs(den), jnp.exp(-m_t))[..., None]
    b_last = b[..., -1]
    log_src = b_last[..., None] - b + ig
    m_new = jnp.maximum(b_last + m, jnp.max(log_src, -1))
    w_src = jnp.exp(log_src - m_new[..., None])
    s_old = jnp.exp(b_last + m - m_new)
    C_new = s_old[..., None, None] * C + jnp.einsum('bhs,bhsd,bhsv->bhdv', w_src, k, v)
    n_new = s_old[..., None] * n + jnp.einsum('bhs,bhsd->bhd', w_src, k)
    return (C_new, n_new, m_new), h

def mlstm_mixer(x, w_in, b_if, hn_g, w_out):
    B, S, _ = x.shape
    H, L = ML_HEADS, ML_CHUNK
    nc = S // L
    proj = x @ w_in
    q, k, v = proj[..., :ML_Q_END], proj[..., ML_Q_END:ML_K_END], proj[..., ML_K_END:ML_V_END]
    gi, gf, og = proj[..., ML_V_END:ML_I_END], proj[..., ML_I_END:ML_F_END], proj[..., ML_F_END:]

    def to_chunks(t, d):
        return t.reshape(B, nc, L, H, d).transpose(1, 0, 3, 2, 4).astype(jnp.float32)

    def gate_chunks(t):
        return t.reshape(B, nc, L, H).transpose(1, 0, 3, 2)

    qc = to_chunks(q, ML_QK_DIM)
    kc = to_chunks(k, ML_QK_DIM) * (ML_QK_DIM ** -0.5)
    vc = to_chunks(v, ML_V_DIM)
    b_if = b_if.astype(jnp.float32)
    ig = gate_chunks(gi.astype(jnp.float32) + b_if[0])
    lf = gate_chunks(jax.nn.log_sigmoid(gf.astype(jnp.float32) + b_if[1]))
    init = (jnp.zeros((B, H, ML_QK_DIM, ML_V_DIM), jnp.float32),
            jnp.zeros((B, H, ML_QK_DIM), jnp.float32),
            jnp.zeros((B, H), jnp.float32))
    _, h = lax.scan(mlstm_chunk_step, init, (qc, kc, vc, ig, lf))
    h = h.transpose(1, 0, 3, 2, 4).reshape(B, S, H, ML_V_DIM)
    mu = jnp.mean(h, -1, keepdims=True)
    var = jnp.mean(jnp.square(h - mu), -1, keepdims=True)
    hn = (h - mu) * lax.rsqrt(var + NORM_EPS) * hn_g.astype(jnp.float32).reshape(H, ML_V_DIM)
    out = jax.nn.sigmoid(og.astype(jnp.float32)) * hn.reshape(B, S, H * ML_V_DIM)
    return out.astype(x.dtype) @ w_out

def mla_shared_kv(xs, w_down, kv_norm_g, w_up, cos, sin):
    B, S, _ = xs.shape
    ckr = xs @ w_down
    c_kv = rms_norm(ckr[..., :MLA_KV_RANK], kv_norm_g)
    kv = (c_kv @ w_up).reshape(B, S, MLA_HEADS, MLA_NOPE_DIM + MLA_V_DIM)
    k_nope = kv[..., :MLA_NOPE_DIM].transpose(0, 2, 1, 3)
    v = kv[..., MLA_NOPE_DIM:].transpose(0, 2, 1, 3)
    k_rope = apply_rope(ckr[..., MLA_KV_RANK:], cos, sin)
    return k_nope, k_rope, v

def mla_mixer(x, w_dq, q_norm_g, w_uq, w_out, k_nope, k_rope, v, cos, sin):
    B, S, _ = x.shape
    H = MLA_HEADS
    c_q = rms_norm(x @ w_dq, q_norm_g)
    q = (c_q @ w_uq).reshape(B, S, H, MLA_NOPE_DIM + MLA_ROPE_DIM).transpose(0, 2, 1, 3)
    q_nope = q[..., :MLA_NOPE_DIM]
    q_rope = apply_rope(q[..., MLA_NOPE_DIM:], cos[:, None], sin[:, None])
    nb = S // ATTN_BLOCK

    def blocks(t):
        return t.reshape(B, H, nb, ATTN_BLOCK, t.shape[-1]).transpose(2, 0, 1, 3, 4)

    scale = (MLA_NOPE_DIM + MLA_ROPE_DIM) ** -0.5
    key_pos = jnp.arange(S)

    def attend(args):
        idx, qn, qr = args
        s = jnp.einsum('bhqd,bhkd->bhqk', qn, k_nope) + jnp.einsum('bhqd,bkd->bhqk', qr, k_rope)
        s = s.astype(jnp.float32) * scale
        q_pos = idx * ATTN_BLOCK + jnp.arange(ATTN_BLOCK)
        s = jnp.where(key_pos[None, :] <= q_pos[:, None], s, -jnp.inf)
        p = jax.nn.softmax(s, axis=-1).astype(v.dtype)
        return jnp.einsum('bhqk,bhkd->bhqd', p, v)

    o = lax.map(attend, (jnp.arange(nb), blocks(q_nope), blocks(q_rope)))
    o = o.transpose(1, 0, 3, 2, 4).reshape(B, S, H * MLA_V_DIM)
    return o @ w_out

def peer_ffn(x, w_q, sub_keys, u, v):
    B, S, D = x.shape
    T = B * S
    K = PEER_TOPK
    xt = x.reshape(T, D)
    q = (xt @ w_q).reshape(T, PEER_HEADS, 2, PEER_HALF)
    s = jnp.einsum('thcd,hcnd->thcn', q, sub_keys).astype(jnp.float32)
    s1, i1 = lax.top_k(s[:, :, 0], K)
    s2, i2 = lax.top_k(s[:, :, 1], K)
    cand_s = (s1[..., :, None] + s2[..., None, :]).reshape(T, PEER_HEADS, K * K)
    cand_i = (i1[..., :, None] * PEER_N_KEYS + i2[..., None, :]).reshape(T, PEER_HEADS, K * K)
    top_s, top_pos = lax.top_k(cand_s, K)
    expert_idx = jnp.take_along_axis(cand_i, top_pos, axis=-1)
    gates = jax.nn.softmax(top_s, axis=-1).astype(x.dtype)
    nb = T // PEER_BLOCK

    def expert_block(args):
        xb, eb, gb = args
        ub = jnp.take(u, eb, axis=0)
        act = jax.nn.gelu(jnp.einsum('thkd,td->thk', ub, xb), approximate=False)
        vb = jnp.take(v, eb, axis=0)
        return jnp.einsum('thk,thkd->td', gb * act, vb)

    out = lax.map(expert_block, (xt.reshape(nb, PEER_BLOCK, D),
                                 expert_idx.reshape(nb, PEER_BLOCK, PEER_HEADS, K),
                                 gates.reshape(nb, PEER_BLOCK, PEER_HEADS, K)))
    return out.reshape(B, S, D)

def first_inputs(seed: int = 0) -> dict:
    key = jax.random.key(seed)
    ks = jax.random.split(key, 24)
    D = D_MODEL
    nrm = jax.random.normal
    f32 = jnp.float32
    x = nrm(ks[0], (BATCH, SEQ, D), f32)
    p = nrm(ks[1], (DEPTH, BATCH, SEQ, PLE_DIM), f32)
    positions = jnp.broadcast_to(jnp.arange(SEQ, dtype=jnp.int32), (BATCH, SEQ))
    ln_g = 1.0 + 0.05 * nrm(ks[2], (DEPTH, 2, D), f32)
    ln_b = 0.02 * nrm(ks[3], (DEPTH, 2, D), f32)
    a_w_in = nrm(ks[4], (N_A_LAYERS, D, ML_IN_COLS), f32) * D ** -0.5
    b_i = 0.1 * nrm(ks[5], (N_A_LAYERS, ML_HEADS), f32)
    b_f = jnp.linspace(3.0, 6.0, ML_HEADS, dtype=f32) + 0.1 * nrm(ks[6], (N_A_LAYERS, ML_HEADS), f32)
    a_b_if = jnp.stack([b_i, b_f], axis=1)
    a_hn_g = 1.0 + 0.05 * nrm(ks[7], (N_A_LAYERS, D), f32)
    a_w_out = nrm(ks[8], (N_A_LAYERS, D, D), f32) * (D ** -0.5 * DN_BETA)
    kv_w_down = nrm(ks[9], (D, MLA_KV_RANK + MLA_ROPE_DIM), f32) * D ** -0.5
    kv_norm_g = 1.0 + 0.05 * nrm(ks[10], (MLA_KV_RANK,), f32)
    kv_w_up = nrm(ks[11], (MLA_KV_RANK, MLA_HEADS * (MLA_NOPE_DIM + MLA_V_DIM)), f32) * MLA_KV_RANK ** -0.5
    b_w_dq = nrm(ks[12], (N_B_LAYERS, D, MLA_Q_RANK), f32) * D ** -0.5
    b_q_norm_g = 1.0 + 0.05 * nrm(ks[13], (N_B_LAYERS, MLA_Q_RANK), f32)
    b_w_uq = nrm(ks[14], (N_B_LAYERS, MLA_Q_RANK, MLA_HEADS * (MLA_NOPE_DIM + MLA_ROPE_DIM)), f32) * MLA_Q_RANK ** -0.5
    b_w_out = nrm(ks[15], (N_B_LAYERS, MLA_HEADS * MLA_V_DIM, D), f32) * ((MLA_HEADS * MLA_V_DIM) ** -0.5 * DN_BETA)
    peer_w_q = nrm(ks[16], (DEPTH, D, PEER_HEADS * PEER_KEY_DIM), f32) * D ** -0.5
    peer_sub_keys = nrm(ks[17], (DEPTH, PEER_HEADS, 2, PEER_N_KEYS, PEER_HALF), f32) * PEER_HALF ** -0.5
    peer_u = nrm(ks[18], (DEPTH, PEER_N_EXPERTS, D), f32) * D ** -0.5
    peer_v = nrm(ks[19], (DEPTH, PEER_N_EXPERTS, D), f32) * (DN_BETA * PEER_HEADS ** -0.5)
    ple_w_proj = nrm(ks[20], (DEPTH, PLE_DIM, D), f32) * (0.5 * PLE_DIM ** -0.5)
    ple_w_gate = nrm(ks[21], (DEPTH, D, D), f32) * D ** -0.5
    return {"x": x, "p": p, "positions": positions, "ln_g": ln_g, "ln_b": ln_b,
            "a_w_in": a_w_in, "a_b_if": a_b_if, "a_hn_g": a_hn_g, "a_w_out": a_w_out,
            "kv_w_down": kv_w_down, "kv_norm_g": kv_norm_g, "kv_w_up": kv_w_up,
            "b_w_dq": b_w_dq, "b_q_norm_g": b_q_norm_g, "b_w_uq": b_w_uq, "b_w_out": b_w_out,
            "peer_w_q": peer_w_q, "peer_sub_keys": peer_sub_keys, "peer_u": peer_u, "peer_v": peer_v,
            "ple_w_proj": ple_w_proj, "ple_w_gate": ple_w_gate}

def first_block(x, p, positions, ln_g, ln_b, a_w_in, a_b_if, a_hn_g, a_w_out,
              kv_w_down, kv_norm_g, kv_w_up, b_w_dq, b_q_norm_g, b_w_uq, b_w_out,
              peer_w_q, peer_sub_keys, peer_u, peer_v, ple_w_proj, ple_w_gate):
    cos, sin = rope_angles(positions, MLA_ROPE_DIM)
    shared = None
    for i in range(DEPTH):
        if i < N_A_LAYERS:
            mix = mlstm_mixer(x, a_w_in[i], a_b_if[i], a_hn_g[i], a_w_out[i])
        else:
            j = i - N_A_LAYERS
            if j == 0:
                shared = mla_shared_kv(x, kv_w_down, kv_norm_g, kv_w_up, cos, sin)
            k_nope, k_rope, v = shared
            mix = mla_mixer(x, b_w_dq[j], b_q_norm_g[j], b_w_uq[j], b_w_out[j],
                            k_nope, k_rope, v, cos, sin)
        x = layer_norm(DN_ALPHA * x + mix, ln_g[i, 0], ln_b[i, 0])
        x = layer_norm(DN_ALPHA * x + peer_ffn(x, peer_w_q[i], peer_sub_keys[i], peer_u[i], peer_v[i]),
                       ln_g[i, 1], ln_b[i, 1])
        x = x + jax.nn.sigmoid(x @ ple_w_gate[i]) * (p[i] @ ple_w_proj[i])
    return x


DEPTH_2 = 1

HEAD_DIM = 64
NSA_HEADS = 8
NSA_KV_GROUPS = 2
NSA_REP = NSA_HEADS // NSA_KV_GROUPS
SB_HEADS = 8
CMP_BLOCK = 32
CMP_STRIDE = 16
CMP_HIDDEN = 2 * HEAD_DIM
SEL_BLOCK = 64
SEL_TOPK = 8
WINDOW = 512
Q_BLOCK = 128
SEL_Q_CHUNK = 64
D_FF = -(-8 * D_MODEL // (3 * 256)) * 256
RMS_EPS = 1e-6
NEG_INF = -1e30
FORCE_PRIORITY = 1e4
ATTN_SCALE = 1.0 / math.sqrt(HEAD_DIM)

NSA_Q_DIM = NSA_HEADS * HEAD_DIM
NSA_KV_DIM = 6 * NSA_KV_GROUPS * HEAD_DIM
NSA_GATE_DIM = 3 * NSA_HEADS
SB_QKV_DIM = 3 * SB_HEADS * HEAD_DIM
MERGE_DIM = 2 * D_MODEL
D_IN = NSA_Q_DIM + NSA_KV_DIM + NSA_GATE_DIM + SB_QKV_DIM + MERGE_DIM
IN_SPLITS = (NSA_Q_DIM, NSA_Q_DIM + NSA_KV_DIM, NSA_Q_DIM + NSA_KV_DIM + NSA_GATE_DIM,
             NSA_Q_DIM + NSA_KV_DIM + NSA_GATE_DIM + SB_QKV_DIM)


def rmsnorm(x, g):
    xf = x.astype(jnp.float32)
    y = xf * lax.rsqrt(jnp.mean(xf * xf, axis=-1, keepdims=True) + RMS_EPS)
    return (y * g.astype(jnp.float32)).astype(x.dtype)

def modulate(h, shift, scale):
    return h * (1.0 + scale) + shift

def alibi_slopes():
    i = jnp.arange(1, NSA_HEADS + 1, dtype=jnp.float32)
    return jnp.exp2(-8.0 * i / NSA_HEADS).reshape(NSA_KV_GROUPS, NSA_REP)

def compress(k, pos_emb, w1, w2):
    n_cmp = (k.shape[2] - CMP_BLOCK) // CMP_STRIDE + 1
    idx = jnp.arange(n_cmp)[:, None] * CMP_STRIDE + jnp.arange(CMP_BLOCK)[None, :]
    blocks = k[:, :, idx] + pos_emb
    flat = blocks.reshape(*blocks.shape[:3], CMP_BLOCK * HEAD_DIM)
    return jax.nn.gelu(flat @ w1) @ w2

def nsa_compressed(q, kc, vc, slopes):
    S = q.shape[3]
    n = kc.shape[2]
    t = jnp.arange(S)
    end = jnp.arange(n) * CMP_STRIDE + CMP_BLOCK - 1
    dist = (t[:, None] - end[None, :]).astype(jnp.float32)
    valid = dist >= 0
    s = jnp.einsum('bgrqd,bgnd->bgrqn', q.astype(jnp.float32), kc.astype(jnp.float32)) * ATTN_SCALE
    s = s - slopes[:, :, None, None] * dist
    s = jnp.where(valid, s, NEG_INF)
    p = jax.nn.softmax(s, axis=-1)
    p = jnp.where(valid.any(-1)[:, None], p, 0.0)
    o = jnp.einsum('bgrqn,bgnd->bgrqd', p.astype(vc.dtype), vc)
    return o, p.sum(axis=2)

def nsa_select_indices(p_cmp, S):
    n_cmp = p_cmp.shape[-1]
    n_sel = S // SEL_BLOCK
    c_start = jnp.arange(n_cmp) * CMP_STRIDE
    c_end = c_start + CMP_BLOCK - 1
    s_start = jnp.arange(n_sel) * SEL_BLOCK
    s_end = s_start + SEL_BLOCK - 1
    overlap = ((c_start[:, None] <= s_end[None, :]) & (c_end[:, None] >= s_start[None, :])).astype(jnp.float32)
    p_slc = jnp.einsum('bgqn,nj->bgqj', p_cmp, overlap)
    cur = (jnp.arange(S) // SEL_BLOCK)[:, None]
    j = jnp.arange(n_sel)[None, :]
    valid = j <= cur
    forced = (j == 0) | (j == cur) | (j == cur - 1)
    prio = jnp.where(valid, p_slc, NEG_INF)
    prio = jnp.where(forced & valid, FORCE_PRIORITY, prio)
    _, idx = lax.top_k(prio, min(SEL_TOPK, n_sel))
    return idx

def nsa_selected(q, k, v, idx, slopes):
    B, G, R, S, hd = q.shape
    n = idx.shape[-1]
    kb = k.reshape(B, G, S // SEL_BLOCK, SEL_BLOCK, hd)
    vb = v.reshape(B, G, S // SEL_BLOCK, SEL_BLOCK, hd)
    nc = S // SEL_Q_CHUNK
    q_c = q.reshape(B, G, R, nc, SEL_Q_CHUNK, hd).transpose(3, 0, 1, 2, 4, 5)
    idx_c = idx.reshape(B, G, nc, SEL_Q_CHUNK, n).transpose(2, 0, 1, 3, 4)
    t_c = jnp.arange(S).reshape(nc, SEL_Q_CHUNK)
    bi = jnp.arange(B)[:, None, None, None]
    gi = jnp.arange(G)[None, :, None, None]

    def chunk(args):
        qq, ii, tt = args
        ks = kb[bi, gi, ii]
        vs = vb[bi, gi, ii]
        pos = ii[..., None] * SEL_BLOCK + jnp.arange(SEL_BLOCK)
        dist = (tt[:, None, None] - pos).astype(jnp.float32)
        s = jnp.einsum('bgrqd,bgqnld->bgrqnl', qq.astype(jnp.float32), ks.astype(jnp.float32)) * ATTN_SCALE
        s = s - slopes[:, :, None, None, None] * dist[:, :, None]
        s = jnp.where((dist >= 0)[:, :, None], s, NEG_INF)
        p = jax.nn.softmax(s, axis=(-2, -1))
        return jnp.einsum('bgrqnl,bgqnld->bgrqd', p.astype(v.dtype), vs)

    o = lax.map(chunk, (q_c, idx_c, t_c))
    return o.transpose(1, 2, 3, 0, 4, 5).reshape(B, G, R, S, hd)

def nsa_window(q, k, v, slopes):
    B, G, R, S, hd = q.shape
    kp = jnp.pad(k, ((0, 0), (0, 0), (WINDOW, 0), (0, 0)))
    vp = jnp.pad(v, ((0, 0), (0, 0), (WINDOW, 0), (0, 0)))
    nq = S // Q_BLOCK
    q_c = q.reshape(B, G, R, nq, Q_BLOCK, hd).transpose(3, 0, 1, 2, 4, 5)
    starts = jnp.arange(nq) * Q_BLOCK
    span = WINDOW + Q_BLOCK

    def blk(args):
        qq, q0 = args
        kk = lax.dynamic_slice_in_dim(kp, q0, span, axis=2)
        vv = lax.dynamic_slice_in_dim(vp, q0, span, axis=2)
        t = q0 + jnp.arange(Q_BLOCK)
        s_pos = q0 - WINDOW + jnp.arange(span)
        dist = t[:, None] - s_pos[None, :]
        mask = (dist >= 0) & (dist < WINDOW) & (s_pos[None, :] >= 0)
        s = jnp.einsum('bgrqd,bgkd->bgrqk', qq.astype(jnp.float32), kk.astype(jnp.float32)) * ATTN_SCALE
        s = s - slopes[:, :, None, None] * dist.astype(jnp.float32)
        s = jnp.where(mask, s, NEG_INF)
        p = jax.nn.softmax(s, axis=-1)
        return jnp.einsum('bgrqk,bgkd->bgrqd', p.astype(v.dtype), vv)

    o = lax.map(blk, (q_c, starts))
    return o.transpose(1, 2, 3, 0, 4, 5).reshape(B, G, R, S, hd)

def stick_breaking(q, k, v):
    B, H, S, hd = q.shape
    nq = S // Q_BLOCK
    q_c = q.reshape(B, H, nq, Q_BLOCK, hd).transpose(2, 0, 1, 3, 4)
    starts = jnp.arange(nq) * Q_BLOCK
    kf = k.astype(jnp.float32)
    s_pos = jnp.arange(S)

    def blk(args):
        qq, q0 = args
        t = q0 + jnp.arange(Q_BLOCK)
        mask = s_pos[None, :] < t[:, None]
        z = jnp.einsum('bhqd,bhkd->bhqk', qq.astype(jnp.float32), kf) * ATTN_SCALE
        log_keep = jnp.where(mask, -jax.nn.softplus(z), 0.0)
        later = lax.cumsum(log_keep, axis=3, reverse=True) - log_keep
        a = jnp.where(mask, jnp.exp(jax.nn.log_sigmoid(z) + later), 0.0)
        return jnp.einsum('bhqk,bhkd->bhqd', a.astype(v.dtype), v)

    o = lax.map(blk, (q_c, starts))
    return o.transpose(1, 2, 0, 3, 4).reshape(B, H, S, hd)

def hybrid_mixer(h, w_in, cmp_pos_k, cmp_w1_k, cmp_w2_k, cmp_pos_v, cmp_w1_v, cmp_w2_v,
                 w_proj_a, w_proj_b, w_out):
    B, S, _ = h.shape
    G, R, hd = NSA_KV_GROUPS, NSA_REP, HEAD_DIM
    proj = h @ w_in
    q_a, kv_a, gate_a, qkv_b, merge = jnp.split(proj, IN_SPLITS, axis=-1)

    q_a = q_a.reshape(B, S, G, R, hd).transpose(0, 2, 3, 1, 4)
    kv_a = kv_a.reshape(B, S, 6, G, hd).transpose(2, 0, 3, 1, 4)
    k_cmp, v_cmp, k_sel, v_sel, k_win, v_win = (kv_a[i] for i in range(6))
    g_a = jax.nn.sigmoid(gate_a.reshape(B, S, G, R, 3).transpose(0, 2, 3, 1, 4))
    slopes = alibi_slopes()
    kc = compress(k_cmp, cmp_pos_k, cmp_w1_k, cmp_w2_k)
    vc = compress(v_cmp, cmp_pos_v, cmp_w1_v, cmp_w2_v)
    o_cmp, p_cmp = nsa_compressed(q_a, kc, vc, slopes)
    idx = nsa_select_indices(p_cmp, S)
    o_sel = nsa_selected(q_a, k_sel, v_sel, idx, slopes)
    o_win = nsa_window(q_a, k_win, v_win, slopes)
    o_a = g_a[..., 0:1] * o_cmp + g_a[..., 1:2] * o_sel + g_a[..., 2:3] * o_win
    y_a = o_a.transpose(0, 3, 1, 2, 4).reshape(B, S, NSA_Q_DIM) @ w_proj_a

    qkv_b = qkv_b.reshape(B, S, 3, SB_HEADS, hd).transpose(2, 0, 3, 1, 4)
    o_b = stick_breaking(qkv_b[0], qkv_b[1], qkv_b[2])
    y_b = o_b.transpose(0, 2, 1, 3).reshape(B, S, SB_HEADS * hd) @ w_proj_b

    merge = merge.reshape(B, S, 2, D_MODEL)
    y = jax.nn.sigmoid(merge[:, :, 0]) * y_a + jax.nn.sigmoid(merge[:, :, 1]) * y_b
    return y @ w_out

def swiglu(h, w_gate, w_up, w_down):
    return (jax.nn.silu(h @ w_gate) * (h @ w_up)) @ w_down

def second_inputs(seed: int = 0) -> dict:
    key = jax.random.key(seed)
    ks = jax.random.split(key, 20)

    def dense(k, shape, fan_in):
        return jax.random.normal(k, shape, jnp.float32) * (fan_in ** -0.5)

    def gain(k, shape):
        return 1.0 + 0.05 * jax.random.normal(k, shape, jnp.float32)

    L = DEPTH_2
    cmp_in = CMP_BLOCK * HEAD_DIM
    return {
        "x": jax.random.normal(ks[0], (BATCH, SEQ, D_MODEL), jnp.float32),
        "c": jax.random.normal(ks[1], (BATCH, D_MODEL), jnp.float32),
        "w_ada": dense(ks[2], (L, D_MODEL, 6 * D_MODEL), D_MODEL),
        "b_ada": 0.02 * jax.random.normal(ks[3], (L, 6 * D_MODEL), jnp.float32),
        "norm_mix_g": gain(ks[4], (L, D_MODEL)),
        "w_in": dense(ks[5], (L, D_MODEL, D_IN), D_MODEL),
        "cmp_pos_k": 0.02 * jax.random.normal(ks[6], (L, CMP_BLOCK, HEAD_DIM), jnp.float32),
        "cmp_w1_k": dense(ks[7], (L, cmp_in, CMP_HIDDEN), cmp_in),
        "cmp_w2_k": dense(ks[8], (L, CMP_HIDDEN, HEAD_DIM), CMP_HIDDEN),
        "cmp_pos_v": 0.02 * jax.random.normal(ks[9], (L, CMP_BLOCK, HEAD_DIM), jnp.float32),
        "cmp_w1_v": dense(ks[10], (L, cmp_in, CMP_HIDDEN), cmp_in),
        "cmp_w2_v": dense(ks[11], (L, CMP_HIDDEN, HEAD_DIM), CMP_HIDDEN),
        "w_proj_a": dense(ks[12], (L, NSA_Q_DIM, D_MODEL), NSA_Q_DIM),
        "w_proj_b": dense(ks[13], (L, SB_HEADS * HEAD_DIM, D_MODEL), SB_HEADS * HEAD_DIM),
        "w_out": dense(ks[14], (L, D_MODEL, D_MODEL), D_MODEL),
        "norm_ffn_g": gain(ks[15], (L, D_MODEL)),
        "w_ffn_gate": dense(ks[16], (L, D_MODEL, D_FF), D_MODEL),
        "w_ffn_up": dense(ks[17], (L, D_MODEL, D_FF), D_MODEL),
        "w_ffn_down": dense(ks[18], (L, D_FF, D_MODEL), D_FF),
        "norm_final_g": gain(ks[19], (D_MODEL,)),
    }

def second_block(x, c, w_ada, b_ada, norm_mix_g, w_in, cmp_pos_k, cmp_w1_k, cmp_w2_k,
              cmp_pos_v, cmp_w1_v, cmp_w2_v, w_proj_a, w_proj_b, w_out, norm_ffn_g,
              w_ffn_gate, w_ffn_up, w_ffn_down, norm_final_g):
    for l in range(DEPTH_2):
        mod = jax.nn.silu(c) @ w_ada[l] + b_ada[l]
        sh1, sc1, g1, sh2, sc2, g2 = jnp.split(mod[:, None, :], 6, axis=-1)
        h = modulate(rmsnorm(x, norm_mix_g[l]), sh1, sc1)
        x = x + g1 * hybrid_mixer(h, w_in[l], cmp_pos_k[l], cmp_w1_k[l], cmp_w2_k[l],
                                  cmp_pos_v[l], cmp_w1_v[l], cmp_w2_v[l],
                                  w_proj_a[l], w_proj_b[l], w_out[l])
        h = modulate(rmsnorm(x, norm_ffn_g[l]), sh2, sc2)
        x = x + g2 * swiglu(h, w_ffn_gate[l], w_ffn_up[l], w_ffn_down[l])
    return rmsnorm(x, norm_final_g)


def setup_inputs(seed=0):
    out = dict(first_inputs(seed))
    for name, value in second_inputs(seed + 1).items():
        if name != "x":
            out[name + "_2"] = value
    return out


def reference(
    x, p, positions, ln_g, ln_b, a_w_in, a_b_if, a_hn_g, a_w_out, kv_w_down, kv_norm_g, kv_w_up,
    b_w_dq, b_q_norm_g, b_w_uq, b_w_out, peer_w_q, peer_sub_keys, peer_u, peer_v, ple_w_proj,
    ple_w_gate, c_2, w_ada_2, b_ada_2, norm_mix_g_2, w_in_2, cmp_pos_k_2, cmp_w1_k_2,
    cmp_w2_k_2, cmp_pos_v_2, cmp_w1_v_2, cmp_w2_v_2, w_proj_a_2, w_proj_b_2, w_out_2,
    norm_ffn_g_2, w_ffn_gate_2, w_ffn_up_2, w_ffn_down_2, norm_final_g_2,
):
    x = first_block(
        x, p, positions, ln_g, ln_b, a_w_in, a_b_if, a_hn_g, a_w_out, kv_w_down, kv_norm_g,
        kv_w_up, b_w_dq, b_q_norm_g, b_w_uq, b_w_out, peer_w_q, peer_sub_keys, peer_u, peer_v,
        ple_w_proj, ple_w_gate,
    )
    return second_block(
        x, c_2, w_ada_2, b_ada_2, norm_mix_g_2, w_in_2, cmp_pos_k_2, cmp_w1_k_2, cmp_w2_k_2,
        cmp_pos_v_2, cmp_w1_v_2, cmp_w2_v_2, w_proj_a_2, w_proj_b_2, w_out_2, norm_ffn_g_2,
        w_ffn_gate_2, w_ffn_up_2, w_ffn_down_2, norm_final_g_2,
    )


_drawn_inputs = setup_inputs


def setup_inputs(seed=0):
    import zlib

    import numpy as np

    out = dict(_drawn_inputs(seed))
    spreads = {}
    factors = {'a_hn_g': 3.9,
     'kv_norm_g': 7.589,
     'b_q_norm_g': 8.0,
     'cmp_pos_k_2': 194.782,
     'cmp_pos_v_2': 24.387}
    for name, (base, spread) in spreads.items():
        noise = np.random.default_rng([zlib.crc32(name.encode()), seed]).standard_normal(out[name].shape)
        drawn = base * np.exp(spread * noise) if base else spread * noise
        out[name] = __import__('jax').numpy.asarray(drawn.astype(out[name].dtype))
    for name, factor in factors.items():
        out[name] = (out[name] * factor).astype(out[name].dtype)
    return out
```

```python
import math
from contextlib import ExitStack

import numpy as np
import concourse.bass as bass
from concourse import mybir

F32 = mybir.dt.float32
U32 = mybir.dt.uint32
I32 = mybir.dt.int32
ALU = mybir.AluOpType
ACT = mybir.ActivationFunctionType
AX = mybir.AxisListType.X

P = 128
D = 1024
T = 256
TB = T // P
KC = D // P
DEPTH = 2
ALPHA = (2.0 * DEPTH) ** 0.25
LN_EPS = 1e-5
RMS_EPS = 1e-6
H = 8
QK = D // (2 * H)
A_V, A_G, A_O = 2 * H * QK, 2 * H * QK + D, 2 * H * QK + D + 2 * H
ROPE, RHALF = 64, 32
KV_RANK, Q_RANK = 256, 384
MLA_SCALE = (128 + ROPE) ** -0.5
THETA = 10000.0
PH, NK, TOPK, NEXP = 8, 128, 16, 16384
PAIRS = PH * TOPK
SLOTS = 8
GRP = 2
NG = SLOTS // GRP
ITERS = PAIRS // SLOTS
WOVEN = 5
HD = 64
NCMP, CW = 15, 16
FF = 2816
FC = FF // P
SCALE = 1.0 / math.sqrt(HD)
SLOPES = [2.0 ** (-8.0 * (i + 1) / H) for i in range(H)]
FAR = 1e33
NEG = -1e30
SLOT = 4096
NW = 4


def build(nc, a, out, dbg=None):
    with ExitStack() as ctx:
        program(nc, a, out, ctx, dbg or {})


def program(nc, a, out, ctx, dbg):
    def sb(name, shape, dt=F32):
        return ctx.enter_context(nc.sbuf_tensor(name, shape, dt))

    sems = {}

    def sem(name):
        if name not in sems:
            sems[name] = ctx.enter_context(nc.semaphore(name))
        return sems[name]

    ring = sb("ring", [P, NW, SLOT])
    arena = sb("arena", [P, SLOTS * 2 * D])
    qreg = sb("qreg", [P, 4096])
    sreg = sb("sreg", [P, 4096])
    xt = sb("x_tok", [P, TB, D])
    yt = sb("y_tok", [P, TB, D])
    xT = sb("xT", [P, KC, T])
    lnp = sb("lnp", [P, 2, D])
    ident = sb("ident", [P, P])
    identa = sb("identa", [P, P])
    ones = sb("ones", [P, P])
    upper = sb("upper", [P, P])
    maskT = sb("maskT", [P, 384])
    maskS = sb("maskS", [P, 384])
    keep = sb("keep", [P, 384])
    maskQ = sb("maskQ", [P, 384])
    iota16 = sb("iota16", [P, 16])
    bnst = sb("bnst", [P, 2, 6])
    mv = sb("mv", [P, 2])
    var = sb("var", [P, 16])
    sdv = sb("sdv", [P, 16])
    rstd = sb("rstd", [P, 16])
    psum = [ctx.enter_context(nc.psum_tensor(f"bank{b}", [P, 512], F32)) for b in range(8)]

    def carve(region, parts=P):
        at = [0]

        def take(*shape, p=parts):
            n = int(np.prod(shape))
            v = region[0:p, at[0]:at[0] + n]
            at[0] += n
            assert at[0] <= region.shape[1], (at, region.shape)
            if len(shape) > 1:
                names = "abcd"[:len(shape)]
                v = v.rearrange(f"p ({' '.join(names)}) -> p {' '.join(names)}",
                                **{k: s for k, s in zip(names, shape)})
            return v
        return take

    bank_full = [sem(f"bank_full{b}") for b in range(8)]
    bank_free = [sem(f"bank_free{b}") for b in range(8)]
    slot_loaded = [sem(f"slot_loaded{i}") for i in range(NW)]
    place = {}
    uses = [0] * 8

    def full(eng, name):
        b, k = place[name]
        eng.wait_ge(bank_full[b], k + 1)
        return psum[b]

    def moved(eng, name):
        b, k = place[name]
        eng.wait_ge(bank_free[b], k + 1)

    def free(ins, name):
        ins.then_inc(bank_free[place[name][0]], 1)

    loads = []

    block = ctx.enter_context(nc.Block())

    class Steps:
        def __init__(self, eng, name):
            self.eng, self.sem, self.n = eng, sem(name), 0

        def go(self, ins):
            ins.then_inc(self.sem, 1)
            self.n += 1

        def wait(self):
            self.eng.wait_ge(self.sem, self.n)

        def __call__(self, ins):
            self.go(ins)
            self.wait()

    c = carve(arena)
    A = dict(qT=c(4, T), kT=c(4, T), v=c(TB, H, 129), og=c(TB, D), h=c(TB, H, 128),
             negM=c(H, 384), Pm=c(2, 384), tm=c(2, 384), hT=c(KC, T), g=c(D))
    c = carve(sreg)
    A.update(sel=c(H, P, p=8), ig=c(T, p=8), xf=c(T, p=8), ax=c(T, p=8), ex=c(T, p=8), lf=c(T, p=8),
             B=c(T, p=8), a=c(T, p=8), M=c(T, p=8), nM=c(T, p=8), m=c(T, p=8))
    c = carve(qreg)
    A.update(acol=c(TB, H), enm=c(TB, H), den=c(2, 2), rden=c(2, 2), st=c(TB * H, 6),
             mu=c(16), t1=c(16), t2=c(16), bif=c(2, p=8))
    gath = arena[:, :].rearrange("p (s n) -> p s n", s=SLOTS)
    pq = qreg[:, :].rearrange("p (c t) -> p c t", c=16)
    sc = sreg[:, :].rearrange("p (b c n) -> p b c n", b=TB, c=16)
    c = carve(xT[:, :, :].rearrange("p k t -> p (k t)"))
    v1 = c(16, 16)
    i1 = c(16, 16).bitcast(U32)
    i1f = c(16, 16)
    cand = qreg[:, 0:2048].rearrange("p (h i) -> p h i", h=PH)
    eq = qreg[:, 2048:4096].rearrange("p (h k j) -> p h k j", h=PH, k=16)
    eq2 = qreg[:, 0:2048].rearrange("p (h k j) -> p h k j", h=PH, k=16)
    tsv = c(PH, 16)
    tp = c(PH, 16).bitcast(U32)
    p12 = c(2, PH, 16).bitcast(U32)
    p12f = c(2, PH, 16)
    i12 = c(2, PH, 16)
    eidx = sb("eidx", [P, TB, PAIRS], U32)
    gate = sb("gate", [P, TB, PAIRS])
    gsum = sb("gsum", [P, PH])
    grec = sb("grec", [P, PH])
    idc = sb("idc", [P, SLOTS], U32)
    gcur = sb("gcur", [P, SLOTS])
    dots = sb("dots", [P, SLOTS])
    glu = sb("glu", [P, SLOTS])
    diag = sreg[:, 0:SLOTS * P].rearrange("p (s n) -> p s n", s=SLOTS)
    c = carve(arena)
    M = dict(knT=c(H, T), v=c(TB, D), qnT=c(H, T), oT=c(H, T), krm=c(4, 2, T), ckvT=c(2, T),
             cqT=c(3, T), R=c(2, 2, T), K12=c(2, T), t=c(4, T))
    c = carve(sreg)
    M.update(E=c(3, 384), PT=c(4, 384), ckv=c(KV_RANK), ckv2=c(KV_RANK))
    c = carve(qreg)
    M.update(cq=c(TB, Q_RANK), cg=c(KV_RANK), qg=c(Q_RANK), ang=c(T), cos=c(T), sin=c(T), w1=c(T),
             w2=c(T), w3=c(T), posf=c(T), ssq=c(4), sm=c(2, 8))
    posi = sb("posi", [P, T], I32)
    invf = sb("invf", [P, 1])
    rmax = sb("rmax", [P, 3, 2])
    rsum = sb("rsum", [P, 3, 2])
    rrec = sb("rrec", [P, 3, 2])
    c = carve(arena)
    N = dict(qT=c(4, T), ksT=c(2, T), kwT=c(2, T), vs=c(TB, P), vw=c(TB, P), qbT=c(4, T), kbT=c(4, T),
             vb=c(TB, 512), sgm=c(16, T), oaT=c(4, T), obT=c(4, T), g1=c(D), g2=c(D), sbk=c(4, 384),
             sbp=c(2, 384))
    sbk, sbp = N["sbk"], N["sbp"]
    c = carve(qreg)
    N.update(E=c(3, 384), PT=c(4, 384), bh=c(2, 384), dist=c(384))
    c = carve(sreg)
    N.update(cb=c(TB, H, CW), cE=c(TB, H, CW), cPT=c(T), vcm=c(H, HD), cdist=c(TB, CW), hid=c(2, CW), hidv=c(2, 4, CW),
             kc=c(2, CW), ga=c(TB, 24), w2=c(3, HD), m8=c(8), rv=c(2), cmx=c(TB, H), csm=c(TB, H),
             crc=c(TB, H), cT=c(KC), scT=c(KC), mod=c(4, KC), bada=c(4, KC), ng=c(2, KC), gs=c(2, KC),
             posc=c(2, 32, p=64))
    c = carve(N["sgm"].rearrange("p a b -> p (a b)"), 64)
    ckin = c(4, 32, CW)
    kcv = c(4, T)
    c = carve(arena[:, :])
    F = dict(hid=c(FC, T))

    NX = 8

    @block.tensor
    def _(pe):
        n_open = [0]
        held = set()

        def open_(name):
            b = n_open[0] % 8
            n_open[0] += 1
            k = uses[b]
            uses[b] += 1
            place[name] = (b, k)
            if k:
                pe.wait_ge(bank_free[b], k)
            return psum[b]

        def close(ins, name):
            ins.then_inc(bank_full[place[name][0]], 1)

        def mm(o, l, r, start=True, stop=True):
            return nc.tensor.matmul(o, l, r, start=start, stop=stop)

        nw = [0]

        def take(src, kc, n, p=P):
            i = nw[0]
            nw[0] += 1
            s = i % NW
            rec = dict(kind="w", src=src, slot=s, i=i, kc=kc, n=n, p=p, done=None)
            loads.append(rec)
            pe.wait_ge(slot_loaded[s], 16 * (i // NW + 1))
            v = ring[0:p, s, 0:kc * n].rearrange("p (k n) -> p k n", k=kc)
            return v, rec

        def last_use(rec, name):
            b, k = place[name]
            rec["done"] = (bank_full[b], k + 1)

        def aux(dst, src, key, after=None):
            loads.append(dict(kind="aux", dst=dst, src=src, sem=sem(key), after=after))

        def rows(w, c0, n):
            return w[:, c0:c0 + n].rearrange("(k p) n -> p k n", p=P)

        def featT(name, w, src, cols, kc, rhs=None, m=P):
            o = open_(name)
            for k in range(kc):
                l = w[:, k, cols] if isinstance(cols, slice) else cols(k)
                ins = mm(o[0:m, 0:T], l, src[:, k, :], k == 0, k == kc - 1)
            close(ins, name)

        def tok(name, src, w, tb, n, kc, wk=0, cols=slice(None)):
            o = open_(name)
            for k in range(kc):
                ins = mm(o[:, 0:n], src[:, k, tb * P:(tb + 1) * P], w[:, k, cols], k == 0, k == kc - 1)
            close(ins, name)

        def transposes(name, src, dst_chunks, tbs, ready, base):
            for tb in tbs:
                pe.wait_ge(ready, base + tb + 1)
                for g0 in range(0, dst_chunks, 4):
                    g1 = min(g0 + 4, dst_chunks)
                    nm = f"{name}_{tb}_{g0 // 4}"
                    o = open_(nm)
                    for k in range(g0, g1):
                        ins = nc.tensor.transpose(o[:, (k - g0) * P:(k - g0 + 1) * P],
                                                  src[:, tb, k * P:(k + 1) * P], ident[:, :])
                    close(ins, nm)

        def await_T(name, chunks=KC):
            for tb in range(TB):
                for g in range(-(-chunks // 4)):
                    moved(pe, f"{name}_{tb}_{g}")

        def out_proj(name, srcT, w_dram):
            for half in range(2):
                w, rec = take(rows(w_dram, half * 512, 512), KC, 512)
                for tb in range(TB):
                    tok(f"{name}_{tb}_{half}", srcT, w, tb, 512, KC)
                last_use(rec, f"{name}_{TB - 1}_{half}")

        pe.wait_ge(sem("consts"), 1)

        pe.wait_ge(sem("xT_loaded"), 16)
        win = a["a_w_in"][0]
        w, rec = take(rows(win, A_G, 2 * H), KC, 2 * H)
        featT("gi", w, xT, slice(0, H), KC, m=H)
        featT("gf", w, xT, slice(H, 2 * H), KC, m=H)
        last_use(rec, "gf")
        for nm, c0 in (("q", 0), ("k", H * QK)):
            w, rec = take(rows(win, c0, 512), KC, 512)
            for ch in range(4):
                featT(f"{nm}{ch}", w, xT, slice(ch * P, (ch + 1) * P), KC)
            last_use(rec, f"{nm}3")
        pe.wait_ge(sem("gates"), 1)
        o = open_("acol")
        for tb in range(TB):
            nc.tensor.transpose(o[:, tb * H:tb * H + H], A["a"][:, tb * P:(tb + 1) * P], ident[0:H, 0:H])
            ins = nc.tensor.transpose(o[:, 16 + tb * H:16 + tb * H + H], A["m"][:, tb * P:(tb + 1) * P],
                                      ident[0:H, 0:H])
        close(ins, "acol")
        for j in range(4):
            o = open_(f"nb{j}")
            for e in range(2):
                ins = mm(o[:, e * T:(e + 1) * T], A["sel"][:, 2 * j + e, :], A["nM"][:, :])
            close(ins, f"nb{j}")
        for half in range(2):
            w, rec = take(rows(win, A_V + half * 512, 512), KC, 512)
            for tb in range(TB):
                tok(f"v_{tb}_{half}", xT, w, tb, 512, KC)
            last_use(rec, f"v_1_{half}")

        def mS(h):
            r = slice((h % 2) * 64, (h % 2) * 64 + 64)
            if h % 2 == 0:
                moved(pe, f"q{h // 2}")
                moved(pe, f"k{h // 2}")
            o = open_(f"mS{h}")
            mm(o[:, 0:T], A["kT"][r, h // 2, 0:P], A["qT"][r, h // 2, :])
            close(mm(o[:, T:384], A["kT"][r, h // 2, P:T], A["qT"][r, h // 2, P:T]), f"mS{h}")

        def mO(h):
            moved(pe, f"mS{h}")
            o = open_(f"mO{h}")
            pm = A["Pm"][:, h % 2, :]
            mm(o[:, 0:129], pm[:, 0:P], A["v"][:, 0, h, :])
            mm(o[:, 129:258], pm[:, P:T], A["v"][:, 0, h, :], True, False)
            close(mm(o[:, 129:258], pm[:, T:384], A["v"][:, 1, h, :], False, True), f"mO{h}")

        mS(0)
        mS(1)
        for tb in range(TB):
            for half in range(2):
                moved(pe, f"v_{tb}_{half}")
        pe.wait_ge(sem("v_ones"), 1)
        for h in range(H):
            mO(h)
            if h + 2 < H:
                mS(h + 2)
        for half in range(2):
            w, rec = take(rows(win, A_O + half * 512, 512), KC, 512)
            for tb in range(TB):
                tok(f"og_{tb}_{half}", xT, w, tb, 512, KC)
            last_use(rec, f"og_1_{half}")
        transposes("hT", A["h"].rearrange("p a b c -> p a (b c)"), KC, range(TB), sem("h_ready"), 0)
        await_T("hT")
        aux(lnp[:, :, :], a["lnp"][0, 0], "lnp")
        out_proj("mix0", A["hT"], a["a_w_out"][0])

        def peer(l, xv):
            transposes(f"xT{xv}", xt, KC, range(TB), sem("x_ready"), TB * (xv - 1))
            await_T(f"xT{xv}")
            for j in range(4):
                w, rec = take(rows(a["peer_w_q"][l], j * 512, 512), KC, 512)
                for e in range(4):
                    featT(f"pq{l}_{j * 4 + e}", w, xT, slice(e * P, (e + 1) * P), KC)
                last_use(rec, f"pq{l}_{j * 4 + 3}")
            w, rec = take(a["keysT"][l].unsqueeze(1), 1, 2048)
            for tb in range(TB):
                for j in range(4):
                    nm = f"sc{l}_{tb}_{j}"
                    for e in range(4):
                        if tb == 0:
                            moved(pe, f"pq{l}_{j * 4 + e}")
                    o = open_(nm)
                    for e in range(4):
                        ch = j * 4 + e
                        ins = mm(o[:, e * P:(e + 1) * P], pq[:, ch, tb * P:(tb + 1) * P],
                                 w[:, 0, ch * P:(ch + 1) * P])
                    close(ins, nm)
            last_use(rec, f"sc{l}_1_3")
            aux(lnp[:, :, :], a["lnp"][l, 1], "lnp", (sem("x_ready"), TB * xv))
            for tb in range(TB):
                r = l * TB + tb
                nm = [f"pe{l}_{tb}_{half}" for half in range(2)]
                o = [open_(x) for x in nm]
                if r == 0:
                    pe.sem_inc(sem("row_free"), SLOTS)

                def body(it, first=False):
                    for s in range(SLOTS):
                        pe.wait_ge(sem("diag"), r * PAIRS + it * SLOTS + s + 1)
                        for half in range(2):
                            ins = mm(o[half][:, :], diag[:, s, :],
                                     gath[:, s, D + half * 512:D + half * 512 + 512],
                                     first and s == 0, False)
                        ins.then_inc(sem("row_free"), 1)

                body(0, True)
                with pe.Fori(1, ITERS) as it:
                    body(it)
                for half in range(2):
                    close(mm(o[half][:, :], identa[:, :], xt[:, tb, half * 512:half * 512 + 512], False, True),
                          nm[half])

        def ple(l, xv):
            transposes(f"xT{xv}", xt, KC, range(TB), sem("x_ready"), TB * (xv - 1))
            pT, rp = take(a["pT"][l].rearrange("(k p) t -> p k t", p=P), 2, T)
            wp, rw = take(rows(a["ple_w_proj"][l], 0, D), 2, D)
            await_T(f"xT{xv}")
            for half in range(2):
                w, rec = take(rows(a["ple_w_gate"][l], half * 512, 512), KC, 512)
                for tb in range(TB):
                    tok(f"pg{l}_{tb}_{half}", xT, w, tb, 512, KC)
                    tok(f"pp{l}_{tb}_{half}", pT, wp, tb, 512, 2, cols=slice(half * 512, half * 512 + 512))
                last_use(rec, f"pg{l}_1_{half}")
            last_use(rp, f"pp{l}_1_1")
            last_use(rw, f"pp{l}_1_1")

        peer(0, 1)
        ple(0, 2)

        transposes("xT3", xt, KC, range(TB), sem("x_ready"), TB * 2)
        await_T("xT3")
        wd, rec = take(rows(a["kv_w_down_r"], 0, 512), KC, 512)
        for tb in range(TB):
            tok(f"ckv_{tb}", xT, wd, tb, KV_RANK, KC, cols=slice(0, KV_RANK))
        for e in range(2):
            featT(f"kr{e}", wd, xT, slice(KV_RANK + e * P, KV_RANK + (e + 1) * P), KC)
        last_use(rec, "kr1")
        wq, rec = take(rows(a["b_w_dq"][0], 0, Q_RANK), KC, Q_RANK)
        for tb in range(TB):
            tok(f"cq_{tb}", xT, wq, tb, Q_RANK, KC)
        last_use(rec, "cq_1")
        for tb in range(TB):
            pe.wait_ge(sem("ckv_ready"), tb + 1)
            o = open_(f"ckvT_{tb}_0")
            for k in range(2):
                ins = nc.tensor.transpose(o[:, k * P:(k + 1) * P], (M["ckv"] if tb == 0 else M["ckv2"])[:, k * P:(k + 1) * P], ident[:, :])
            close(ins, f"ckvT_{tb}_0")
        transposes("cqT", M["cq"], 3, range(TB), sem("cq_ready"), 0)
        await_T("ckvT", 2)
        wu, rec = take(rows(a["kv_w_up"], 0, 2048), 2, 2048)
        for h in range(H):
            featT(f"kn{h}", wu, M["ckvT"], slice(h * 256, h * 256 + 128), 2)
        wv = ring[:, rec["slot"], 0:4096].rearrange("p (k h e n) -> p k h e n", k=2, h=H, e=2)
        for half in range(2):
            for tb in range(TB):
                nm = f"kvv_{tb}_{half}"
                o = open_(nm)
                for k in range(2):
                    ins = mm(o[:, :], M["ckvT"][:, k, tb * P:(tb + 1) * P], wv[:, k, half * 4:half * 4 + 4, 1, :],
                             k == 0, k == 1)
                close(ins, nm)
        last_use(rec, "kvv_1_1")
        await_T("cqT", 3)
        for half in range(2):
            w, rec = take(rows(a["b_w_uq_p"], half * 768, 768), 3, 768)
            for j in range(4):
                featT(f"qn{half * 4 + j}", w, M["cqT"], slice(j * P, (j + 1) * P), 3)
            for e in range(2):
                featT(f"qr{half}_{e}", w, M["cqT"], slice((4 + e) * P, (5 + e) * P), 3)
            last_use(rec, f"qr{half}_1")

        def attn_T(nm, E):
            o = open_(nm)
            for j in range(3):
                ins = nc.tensor.transpose(o[:, j * P:(j + 1) * P], E[:, j * P:(j + 1) * P], ident[:, :])
            close(ins, nm)

        def lS(h):
            if h == 0:
                for e in range(H):
                    moved(pe, f"kn{e}")
                    moved(pe, f"qn{e}")
            if h % 4 == 0:
                pe.wait_ge(sem("rope"), 2 + h // 4)
            o = open_(f"lS{h}")
            for tb in range(TB):
                c0, n = tb * P, (tb + 1) * P
                ts = slice(tb * P, (tb + 1) * P)
                mm(o[:, c0:c0 + n], M["qnT"][:, h, ts], M["knT"][:, h, 0:n], True, False)
                for e in range(2):
                    ins = mm(o[:, c0:c0 + n], M["R"][:, h // 4, e, ts], M["krm"][:, h % 4, e, 0:n], False, e == 1)
            close(ins, f"lS{h}")

        def lO(h):
            moved(pe, f"lT{h}")
            if h == 0:
                for tb in range(TB):
                    for half in range(2):
                        moved(pe, f"kvv_{tb}_{half}")
            o = open_(f"lO{h}")
            pt = M["PT"][:, h % 4, :]
            mm(o[:, 0:T], M["v"][:, 0, h * P:(h + 1) * P], pt[:, 0:T], True, False)
            close(mm(o[:, P:T], M["v"][:, 1, h * P:(h + 1) * P], pt[:, T:384], False, True), f"lO{h}")

        lS(0)
        lS(1)
        for h in range(H):
            if h + 2 < H:
                lS(h + 2)
            pe.wait_ge(sem("probs"), h + 1)
            attn_T(f"lT{h}", M["E"][:, h % 3, :])
            if h:
                lO(h - 1)
        lO(H - 1)
        for h in range(H):
            moved(pe, f"lO{h}")
        aux(lnp[:, :, :], a["lnp"][1, 0], "lnp", (sem("x_ready"), TB * 2))
        out_proj("mix1", M["oT"], a["b_w_out"][0])
        peer(1, 4)
        ple(1, 5)

        pe.wait_ge(sem("silu_c"), 1)
        for j in range(12):
            w, rec = take(rows(a["w_ada_2"][0], j * 512, 512), KC, 512)
            part = j // 2
            nm = f"ada{j}"
            o = open_(nm)
            if part in (2, 5):
                for k in range(KC):
                    ins = mm(o[:, :], N["scT"][:, k:k + 1].broadcast_to([P, P]), w[:, k, :], k == 0, k == KC - 1)
            else:
                for e in range(4):
                    for k in range(KC):
                        ins = mm(o[:, e:e + 1], w[:, k, e * P:(e + 1) * P], N["scT"][:, k:k + 1], k == 0, k == KC - 1)
            close(ins, nm)
            last_use(rec, nm)
        transposes("xT6", yt, KC, range(TB), sem("xn_ready"), 0)
        await_T("xT6")
        w_in = a["w_in_2r"]
        w, rec = take(rows(w_in, 0, 512), KC, 512)
        for ch in range(4):
            featT(f"nq{ch}", w, xT, slice(ch * P, (ch + 1) * P), KC)
        last_use(rec, "nq3")
        w, rec = take(rows(w_in, 512, 512), KC, 512)
        wB = w
        for kv in range(2):
            o = open_(f"cmp{kv}")
            for g in range(2):
                for k in range(KC):
                    ins = mm(o[0:HD, g * T:(g + 1) * T], wB[:, k, kv * P + g * HD:kv * P + (g + 1) * HD], xT[:, k, :],
                             k == 0, k == KC - 1)
            close(ins, f"cmp{kv}")

        for g in range(2):
            featT(f"ks{g}", w, xT, slice(256 + g * P, 256 + (g + 1) * P), KC)
        last_use(rec, "ks1")
        w, rec = take(rows(w_in, 1024, 384), KC, 384)
        for g in range(2):
            featT(f"kw{g}", w, xT, slice(g * P, (g + 1) * P), KC)
        for tb in range(TB):
            tok(f"vs{tb}", xT, w, tb, P, KC, cols=slice(2 * P, 3 * P))
        last_use(rec, "vs1")
        w, rec = take(rows(w_in, 1408, 152), KC, 152)
        for tb in range(TB):
            tok(f"vw{tb}", xT, w, tb, 152, KC)
        last_use(rec, "vw1")
        for kv in range(2):
            w, rec = take(a[f"cmp_w1_{'kv'[kv]}_2"][0].rearrange("(l d) m -> d l m", d=HD), 32, P, p=HD)
            if kv == 0:
                pe.wait_ge(sem("ckin_ready"), 1)
            else:
                pe.wait_ge(sem("ckin_ready"), 2)
            nm = f"ch{kv}"
            o = open_(nm)
            for l in range(32):
                ins = mm(o[:, 0:2 * CW], w[:, l, :], ckin[:, 2 * kv:2 * kv + 2, l, :], l == 0, l == 31)
            close(ins, nm)
            last_use(rec, nm)
        moved(pe, "ch0")
        moved(pe, "ch1")
        o = open_("kc")
        close(mm(o[:, 0:2 * CW], N["w2"][:, 0:2, :].rearrange("p a b -> p (a b)"),
                 N["hid"].rearrange("p g n -> p (g n)")), "kc")
        o = open_("vc")
        close(mm(o[:, 0:HD], N["hidv"].rearrange("p g r n -> p (g r n)"), N["w2"][:, 2, :]), "vc")
        moved(pe, "kc")
        for ch in range(4):
            moved(pe, f"nq{ch}")
        for e in range(2):
            o = open_(f"cS{e}")
            r = slice(e * 64, e * 64 + 64)
            for tb in range(TB):
                for i in range(4):
                    ins = mm(o[:, (tb * 4 + i) * CW:(tb * 4 + i + 1) * CW], N["qT"][r, i, tb * P:(tb + 1) * P],
                             N["kc"][r, i // 2, :])
            close(ins, f"cS{e}")

        for nm, c0 in (("bq", 1560), ("bk", 2072)):
            w, rec = take(rows(w_in, c0, 512), KC, 512)
            for ch in range(4):
                featT(f"{nm}{ch}", w, xT, slice(ch * P, (ch + 1) * P), KC)
            last_use(rec, f"{nm}3")
        w, rec = take(rows(w_in, 2584, 512), KC, 512)
        for tb in range(TB):
            tok(f"bv{tb}", xT, w, tb, 512, KC)
        last_use(rec, "bv1")
        pe.wait_ge(sem("cprobs"), 1)
        o = open_("cT")
        for tb in range(TB):
            ins = nc.tensor.transpose(o[:, tb * P:(tb + 1) * P],
                                      N["cE"][:, tb, :, :].rearrange("p h n -> p (h n)"), ident[:, :])
        close(ins, "cT")

        for nm in ("ks0", "ks1", "kw0", "kw1", "vs0", "vs1", "vw0", "vw1", "vc", "cT"):
            moved(pe, nm)

        def nS(i):
            h, win_ = i // 2, i % 2
            kT = N["kwT"] if win_ else N["ksT"]
            r = slice((h % 2) * 64, (h % 2) * 64 + 64)
            o = open_(f"nS{i}")
            for tb in range(TB):
                ins = mm(o[:, tb * P:tb * P + (tb + 1) * P], N["qT"][r, h // 2, tb * P:(tb + 1) * P],
                         kT[r, h // 4, 0:(tb + 1) * P])
            close(ins, f"nS{i}")

        def nO(h):
            moved(pe, f"nT{2 * h}")
            moved(pe, f"nT{2 * h + 1}")
            o = open_(f"nO{h}")
            g = h // 4
            r = slice((h % 2) * 64, (h % 2) * 64 + 64)
            mm(o[r, 0:T], N["vcm"][:, h, :], N["cPT"], True, False)
            for j in range(2):
                vv = (N["vw"] if j else N["vs"])
                pt = N["PT"][:, (2 * h + j) % 4, :]
                mm(o[r, 0:T], vv[:, 0, g * HD:(g + 1) * HD], pt[:, 0:T], False, False)
                ins = mm(o[r, P:T], vv[:, 1, g * HD:(g + 1) * HD], pt[:, T:384], False, j == 1)
            close(ins, f"nO{h}")

        nS(0)
        nS(1)
        for i in range(2 * H):
            if i + 2 < 2 * H:
                nS(i + 2)
            pe.wait_ge(sem("nprobs"), i + 1)
            attn_T(f"nT{i}", N["E"][:, i % 3, :])
            if i % 2 == 0 and i:
                nO(i // 2 - 1)
        nO(H - 1)

        for ch in range(4):
            moved(pe, f"bq{ch}")
            moved(pe, f"bk{ch}")
        for tb in range(TB):
            moved(pe, f"bv{tb}")

        def bS(h):
            r = slice((h % 2) * 64, (h % 2) * 64 + 64)
            o = open_(f"bS{h}")
            mm(o[:, 0:T], N["kbT"][r, h // 2, 0:P], N["qbT"][r, h // 2, :])
            close(mm(o[:, T:384], N["kbT"][r, h // 2, P:T], N["qbT"][r, h // 2, P:T]), f"bS{h}")

        def bL(h):
            pe.wait_ge(sem("keep"), h + 1)
            lk = sbk[:, 2 + h % 2, :]
            o = open_(f"bL{h}")
            mm(o[:, 0:T], upper[:, :], lk[:, 0:T], True, False)
            mm(o[:, P:T], ones[:, :], lk[:, T:384], False, True)
            close(mm(o[:, T:384], upper[:, :], lk[:, T:384]), f"bL{h}")

        def bO(h):
            pe.wait_ge(sem("broken"), h + 1)
            pt = sbp[:, h % 2, :]
            o = open_(f"bO{h}")
            r = slice((h % 2) * 64, (h % 2) * 64 + 64)
            v = [N["vb"][:, b, h * HD:(h + 1) * HD] for b in range(2)]
            mm(o[r, 0:T], v[0], pt[:, 0:T], True, False)
            close(mm(o[r, P:T], v[1], pt[:, T:384], False, True), f"bO{h}")

        bS(0)
        for h in range(H):
            if h + 1 < H:
                bS(h + 1)
            bL(h)
            if h:
                bO(h - 1)
        bO(H - 1)

        for j in range(4):
            w, rec = take(rows(w_in, 3096 + j * 512, 512), KC, 512)
            for e in range(4):
                featT(f"mg{j * 4 + e}", w, xT, slice(e * P, (e + 1) * P), KC)
            last_use(rec, f"mg{j * 4 + 3}")
        wa, ra = take(rows(a["w_proj_a_2"][0], 0, D), 4, D)
        wb, rb = take(rows(a["w_proj_b_2"][0], 0, D), 4, D)
        for h in range(H):
            moved(pe, f"nO{h}")
            moved(pe, f"bO{h}")
        for ch in range(KC):
            featT(f"ya{ch}", wa, N["oaT"], slice(ch * P, (ch + 1) * P), 4)
            featT(f"yb{ch}", wb, N["obT"], slice(ch * P, (ch + 1) * P), 4)
        last_use(ra, f"ya{KC - 1}")
        last_use(rb, f"yb{KC - 1}")
        pe.wait_ge(sem("yT"), KC)
        out_proj("mix2", xT, a["w_out_2"][0])

        transposes("xT7", yt, KC, range(TB), sem("xn_ready"), TB)
        await_T("xT7")
        for j in range(0, FF, 512):
            n = min(512, FF - j)
            wg, r1 = take(rows(a["w_ffn_gate_2"][0], j, n), KC, n)
            wu_, r2 = take(rows(a["w_ffn_up_2"][0], j, n), KC, n)
            for e in range(n // P):
                ch = j // P + e
                featT(f"fg{ch}", wg, xT, slice(e * P, (e + 1) * P), KC)
                featT(f"fu{ch}", wu_, xT, slice(e * P, (e + 1) * P), KC)
            last_use(r1, f"fg{ch}")
            last_use(r2, f"fu{ch}")
        aux(lnp[:, 0, :], a["nfg"], "lnp", (sem("x_ready"), TB * 6))
        pe.wait_ge(sem("hid"), FC)
        names = [(tb, half) for tb in range(TB) for half in range(2)]
        o = {x: open_(f"dn_{x[0]}_{x[1]}") for x in names}
        for j in range(0, FC, 4):
            n = min(4, FC - j)
            w, rec = take(a["w_ffn_down_2"][0][j * P:(j + n) * P, :].rearrange("(k p) n -> p k n", p=P), n, D)
            for x in names:
                for k in range(n):
                    ins = mm(o[x][:, :], F["hid"][:, j + k, x[0] * P:(x[0] + 1) * P],
                             w[:, k, x[1] * 512:x[1] * 512 + 512], j + k == 0, j + k == FC - 1)
                if j + n == FC:
                    close(ins, f"dn_{x[0]}_{x[1]}")
            if j + n < FC:
                ins.then_inc(sem("down_used"), 1)
                rec["done"] = (sem("down_used"), j // 4 + 1)

    @block.sync
    def _(sp):
        sp.dma_start(xT[:, :, :], a["xTin"].rearrange("(k p) t -> p k t", p=P)).then_inc(sem("xT_loaded"), 16)
        first = True
        done_of = {}
        for r in loads:
            if r["kind"] == "w":
                if r["i"] >= NW:
                    s, v = done_of[r["i"] - NW]
                    sp.wait_ge(s, v)
                dst = ring[0:r["p"], r["slot"], 0:r["kc"] * r["n"]].rearrange("p (k n) -> p k n", k=r["kc"])
                sp.dma_start(dst, r["src"]).then_inc(slot_loaded[r["slot"]], 16)
                done_of[r["i"]] = r["done"]
            else:
                if r["after"]:
                    sp.wait_ge(*r["after"])
                sp.dma_start(r["dst"], r["src"]).then_inc(r["sem"], 16)
        for tb in range(TB):
            sp.wait_ge(sem("out_ready"), tb + 1)
            sp.dma_start(out[tb * P:(tb + 1) * P, :], yt[:, tb, :]).then_inc(sem("out_done"), 16)
        sp.wait_ge(sem("out_done"), 16 * TB)

    @block.gpsimd
    def _(pool):
        step = Steps(pool, "pool_step")
        for dst, src in ((xt[:, :, :], a["x"].rearrange("(b p) d -> p b d", p=P)),
                         (A["bif"][:, :], a["bif"]), (A["g"][:, :], a["hng"]),
                         (posi[:, :], a["pos"]), (invf[:, :], a["invf"])):
            pool.dma_start(dst, src).then_inc(sem("small"), 16)
        for t, v in ((ident, 0.0), (ones, 1.0), (upper, 1.0), (maskT, 0.0), (maskS, 0.0), (keep, 1.0), (maskQ, 0.0)):
            step.go(pool.memset(t[:, :], v))
        step.go(pool.memset(A["sel"], 0.0))
        step.wait()

        def select(v, pattern, base, op, fill, ch):
            step.go(pool.affine_select(out=v, in_=v, compare_op=op, fill=fill, base=base, pattern=pattern,
                                       channel_multiplier=ch))
        select(ident[:, :], [[-1, P]], 0, ALU.not_equal, 1.0, 1)
        select(upper[:, :], [[-1, P]], 0, ALU.is_gt, 0.0, 1)
        for c0 in (0, T):
            select(maskT[:, c0:c0 + P], [[1, P]], 0, ALU.is_ge, NEG, -1)
            select(maskS[:, c0:c0 + P], [[1, P]], 0, ALU.is_gt, NEG, -1)
            select(keep[:, c0:c0 + P], [[1, P]], 0, ALU.is_gt, 0.0, -1)
            select(maskQ[:, c0:c0 + P], [[-1, P]], 0, ALU.is_ge, NEG, 1)
        select(A["sel"], [[-1, H], [0, P]], 0, ALU.not_equal, 1.0, 1)
        step.go(pool.iota(iota16[:, :], [[1, 16]], base=0, channel_multiplier=0,
                          allow_small_or_imprecise_dtypes=True))
        step.wait()
        pool.tensor_scalar(identa[:, :], ident[:, :], ALPHA, None, ALU.mult).then_inc(sem("consts"), 1)

        def gathers(l, tb):
            r = l * TB + tb
            pool.wait_ge(sem("experts"), r + 1)
            with pool.Fori(0, ITERS) as it:
                for g in range(NG):
                    pool.wait_ge(sem("row_free"), r * PAIRS + it * SLOTS + (g + 1) * GRP)
                    pool.sem_inc(sem("gather_go"), 1)
                    pool.tensor_copy(idc[:, g * GRP:(g + 1) * GRP],
                                     eidx[:, tb, bass.ds(it * SLOTS + g * GRP, GRP)]).then_inc(sem("idc_set"), 1)
                    pool.wait_ge(sem("idc_set"), (r * ITERS + it) * NG + g + 1)
                    pool.sem_inc(sem("gather_go"), 1)
                    for s in range(g * GRP, (g + 1) * GRP):
                        pool.indirect_dma_start(gath[:, s, :], None, a["uv"],
                                                bass.IndirectOffsetOnAxis(ap=idc[:, s:s + 1], axis=0)
                                                ).then_inc(sem(f"row{s}"), 16)

        for tb in range(TB):
            gathers(0, tb)
        pool.wait_ge(sem("x_ready"), TB * 3)
        pool.dma_start(M["cg"], a["kvg"]).then_inc(sem("mla_par"), 16)
        pool.dma_start(M["qg"], a["qng"]).then_inc(sem("mla_par"), 16)
        for tb in range(TB):
            gathers(1, tb)
        pool.wait_ge(sem("x_ready"), TB * 5)
        for dst, src in ((N["cT"], a["cT"]), (N["bada"], a["badaT"]), (N["ng"], a["ngT"]),
                         (N["posc"], a["posc"]), (N["w2"], a["cmp_w2"]), (N["g1"], a["bg1"]), (N["g2"], a["bg2"])):
            pool.dma_start(dst, src).then_inc(sem("hyb_par"), 16)
        step.go(pool.iota(N["dist"][:, 0:P], [[-1, P]], base=0, channel_multiplier=1,
                          allow_small_or_imprecise_dtypes=True))
        step.go(pool.iota(N["dist"][:, P:384], [[-1, T]], base=P, channel_multiplier=1,
                          allow_small_or_imprecise_dtypes=True))
        for tb in range(TB):
            step.go(pool.iota(N["cdist"][:, tb, :], [[-16, CW]], base=P * tb - 31, channel_multiplier=1,
                              allow_small_or_imprecise_dtypes=True))
        step.go(pool.memset(ckin[:, :, :, :], 0.0))
        step.go(pool.memset(N["m8"], 1.0))
        step.go(pool.memset(N["rv"], 1.0))
        step.wait()
        select(N["dist"][:, 0:P], [[-1, P]], 0, ALU.is_ge, FAR, 1)
        select(N["dist"][:, T:384], [[-1, P]], 0, ALU.is_ge, FAR, 1)
        for tb in range(TB):
            select(N["cdist"][:, tb, :], [[-16, CW]], P * tb - 31, ALU.is_ge, FAR, 1)
        select(N["m8"], [[-16, 8]], 0, ALU.is_ge, 0.0, 1)
        select(N["rv"][:, 0:1], [[0, 1]], -31, ALU.is_ge, 0.0, 1)
        step.wait()
        select(N["m8"], [[16, 8]], 15, ALU.is_ge, 0.0, -1)
        select(N["cdist"][:, 1, CW - 1:CW], [[0, 1]], -1, ALU.is_ge, FAR, 0)
        step.wait()
        for tb in range(TB):
            for h in range(H):
                step.go(pool.tensor_scalar(N["cb"][:, tb, h, :], N["cdist"][:, tb, :], -SLOPES[h], None, ALU.mult))
        step.wait()
        pool.engine_nop().then_inc(sem("hyb_const"), 1)
        for h in range(H):
            if h >= 2:
                pool.wait_ge(sem("bias_used"), h - 1)
            pool.tensor_scalar(N["bh"][:, h % 2, :], N["dist"], -SLOPES[h], None, ALU.mult
                               ).then_inc(sem("bias_ready"), 1)

    @block.scalar
    def _(act):
        step = Steps(act, "act_step")
        nsq = [0]

        def f(o, i, fn, **kw):
            return nc.scalar.activation(o, i, fn, **kw)

        def evac(name, dst, src=None, fn=ACT.Copy, **kw):
            ps = full(act, name)
            free(f(dst, ps[:, 0:T] if src is None else src(ps), fn, **kw), name)

        def sqrt(cols):
            nsq[0] += 1
            act.wait_ge(sem("var_ready"), nsq[0])
            f(sdv[:, 0:cols], var[:, 0:cols], ACT.Sqrt).then_inc(sem("sd_ready"), 1)

        def evac_T(name, dst, chunks=KC):
            for tb in range(TB):
                for g in range(-(-chunks // 4)):
                    n = min(4, chunks - 4 * g)
                    evac(f"{name}_{tb}_{g}", dst[:, 4 * g:4 * g + n, tb * P:(tb + 1) * P],
                         lambda ps, n=n: ps[:, 0:n * P].rearrange("p (k t) -> p k t", k=n))

        act.wait_ge(sem("abs_ready"), 1)
        step(f(A["ex"], A["ax"], ACT.Exp, scale=-1.0))
        f(A["lf"], A["ex"], ACT.Ln, bias=1.0).then_inc(sem("log1p"), 1)
        for ch in range(4):
            evac(f"q{ch}", A["qT"][:, ch, :])
        for ch in range(4):
            evac(f"k{ch}", A["kT"][:, ch, :], scale=QK ** -0.5)
        ps = full(act, "acol")
        step.go(f(A["acol"].rearrange("p b h -> p (b h)"), ps[:, 0:16], ACT.Copy))
        free(f(A["enm"].rearrange("p b h -> p (b h)"), ps[:, 16:32], ACT.Exp, scale=-1.0), "acol")
        for half in range(2):
            for tb in range(TB):
                evac(f"v_{tb}_{half}", A["v"][:, tb, half * 4:half * 4 + 4, 0:128],
                     lambda ps: ps[:, :].rearrange("p (h n) -> p h n", h=4))
        for h in range(H):
            act.wait_ge(sem("m_arg"), h + 1)
            f(A["tm"][:, h % 2, :], A["tm"][:, h % 2, :], ACT.Exp).then_inc(sem("m_exp"), 1)
        for half in range(2):
            for tb in range(TB):
                evac(f"og_{tb}_{half}", A["og"][:, tb, half * 512:half * 512 + 512],
                     lambda ps: ps[:, :], fn=ACT.Sigmoid)
        sqrt(16)
        evac_T("hT", A["hT"])
        for tb in range(TB):
            sqrt(1)

        def peer(l, xv):
            evac_T(f"xT{xv}", xT)
            for ch in range(16):
                evac(f"pq{l}_{ch}", pq[:, ch, :])
            for tb in range(TB):
                for j in range(4):
                    evac(f"sc{l}_{tb}_{j}", sc[:, tb, j * 4:j * 4 + 4, :],
                         lambda ps: ps[:, :].rearrange("p (c n) -> p c n", c=4))
            def gate_exp(tb):
                act.wait_ge(sem("gate_arg"), l * TB + tb + 1)
                f(tsv[:, :, :], tsv[:, :, :], ACT.Exp).then_inc(sem("gate_exp"), 1)

            def gelus(tb, it):
                for g in range(NG):
                    act.wait_ge(sem("dots"), (l * TB + tb) * PAIRS + it * SLOTS + (g + 1) * GRP)
                    f(glu[:, g * GRP:(g + 1) * GRP], dots[:, g * GRP:(g + 1) * GRP], ACT.Gelu
                      ).then_inc(sem("gelu"), 1)

            gate_exp(0)
            for it in range(WOVEN):
                gelus(0, it)
            gate_exp(1)
            with act.Fori(WOVEN, ITERS) as it:
                gelus(0, it)
            sqrt(1)
            with act.Fori(0, ITERS) as it:
                gelus(1, it)
            sqrt(1)

        def ple(l, xv):
            evac_T(f"xT{xv}", xT)
            for half in range(2):
                for tb in range(TB):
                    evac(f"pg{l}_{tb}_{half}", yt[:, tb, half * 512:half * 512 + 512], lambda ps: ps[:, :],
                         fn=ACT.Sigmoid)

        peer(0, 1)
        ple(0, 2)

        evac_T("xT3", xT)
        act.wait_ge(sem("ang_ready"), 1)
        f(M["sin"], M["w1"], ACT.Sin).then_inc(sem("trig"), 1)
        f(M["cos"], M["w2"], ACT.Sin).then_inc(sem("trig"), 1)
        for tb in range(TB):
            evac(f"ckv_{tb}", yt[:, tb, 0:KV_RANK], lambda ps: ps[:, 0:KV_RANK])
        for e in range(2):
            evac(f"kr{e}", M["t"][:, e, :])
        for tb in range(TB):
            evac(f"cq_{tb}", yt[:, tb, 512:512 + Q_RANK], lambda ps: ps[:, 0:Q_RANK])
        sqrt(4)
        evac_T("ckvT", M["ckvT"], 2)
        evac_T("cqT", M["cqT"], 3)
        for h in range(H):
            evac(f"kn{h}", M["knT"][:, h, :])
        for half in range(2):
            for tb in range(TB):
                evac(f"kvv_{tb}_{half}", M["v"][:, tb, half * 512:half * 512 + 512], lambda ps: ps[:, :])
        for half in range(2):
            for j in range(4):
                evac(f"qn{half * 4 + j}", M["qnT"][:, half * 4 + j, :])

        def softmax_exp(i, E, ready, done, pool_of):
            act.wait_ge(sem(ready), i + 1)
            for tb in range(TB):
                c0 = tb * P
                c1 = c0 + (tb + 1) * P
                ins = f(E[:, i % 3, c0:c1], E[:, i % 3, c0:c1], ACT.Exp, bias=rmax[:, i % 3, tb:tb + 1],
                        accum_out=rsum[:, i % 3, tb:tb + 1])
                if tb == 0:
                    step.go(ins)
            ins.then_inc(sem(done), 1)

        def lT(h):
            if h >= 4:
                full(act, f"lO{h - 4}")
            evac(f"lT{h}", M["PT"][:, h % 4, :], lambda ps: ps[:, 0:384])

        for h in range(H):
            softmax_exp(h, M["E"], "l_max", "l_exp", None)
            if h >= 1:
                lT(h - 1)
            if h >= 2:
                evac(f"lO{h - 2}", M["oT"][:, h - 2, :])
        lT(H - 1)
        for h in (H - 2, H - 1):
            evac(f"lO{h}", M["oT"][:, h, :])
        for tb in range(TB):
            sqrt(1)
        peer(1, 4)
        ple(1, 5)

        act.wait_ge(sem("hyb_par"), 16 * 7)
        f(N["scT"], N["cT"], ACT.Silu).then_inc(sem("silu_c"), 1)
        sqrt(2)
        act.wait_ge(sem("mod_ready"), 1)

        def evac_norm(name, j):
            for tb in range(TB):
                for g in range(2):
                    ps = full(act, f"{name}_{tb}_{g}")
                    for e in range(4):
                        k = 4 * g + e
                        ins = f(xT[:, k, tb * P:(tb + 1) * P], ps[:, e * P:(e + 1) * P], ACT.Identity,
                                scale=N["gs"][:, j, k:k + 1], bias=N["mod"][:, 2 * j, k:k + 1])
                        if e < 3:
                            step.go(ins)
                    free(ins, f"{name}_{tb}_{g}")

        evac_norm("xT6", 0)
        for ch in range(4):
            evac(f"nq{ch}", N["qT"][:, ch, :])
        for kv in range(2):
            evac(f"cmp{kv}", kcv[:, 2 * kv:2 * kv + 2, :],
                 lambda ps: ps[0:HD, :].rearrange("p (g t) -> p g t", g=2))
        for g in range(2):
            evac(f"ks{g}", N["ksT"][:, g, :])
        for tb in range(TB):
            evac(f"vs{tb}", N["vs"][:, tb, :], lambda ps: ps[:, 0:P])
        for g in range(2):
            evac(f"kw{g}", N["kwT"][:, g, :])
        for tb in range(TB):
            ps = full(act, f"vw{tb}")
            step.go(f(N["vw"][:, tb, :], ps[:, 0:P], ACT.Copy))
            free(f(N["ga"][:, tb, :], ps[:, P:152], ACT.Sigmoid), f"vw{tb}")
        evac("ch0", N["hid"], lambda ps: ps[:, 0:2 * CW].rearrange("p (g n) -> p g n", g=2), fn=ACT.Gelu_apprx_tanh)
        evac("ch1", N["hidv"], lambda ps: ps[:, 0:2 * CW].rearrange("p (g n) -> p g n", g=2).unsqueeze(2)
             .broadcast_to([P, 2, 4, CW]), fn=ACT.Gelu_apprx_tanh)
        evac("kc", N["kc"], lambda ps: ps[:, 0:2 * CW].rearrange("p (g n) -> p g n", g=2))
        for ch in range(4):
            evac(f"bq{ch}", N["qbT"][:, ch, :])
        for ch in range(4):
            evac(f"bk{ch}", N["kbT"][:, ch, :])
        for tb in range(TB):
            evac(f"bv{tb}", N["vb"][:, tb, :], lambda ps: ps[:, :])
        act.wait_ge(sem("c_arg"), 1)
        f(N["cE"], N["cE"], ACT.Exp).then_inc(sem("c_exp"), 1)
        evac("cT", N["cPT"])

        def nT(i):
            if i >= 4:
                full(act, f"nO{(i - 4) // 2}")
            evac(f"nT{i}", N["PT"][:, i % 4, :], lambda ps: ps[:, 0:384])

        def nO(h):
            r = slice((h % 2) * 64, (h % 2) * 64 + 64)
            evac(f"nO{h}", N["oaT"][r, h // 2, :], lambda ps: ps[r, 0:T])

        for i in range(2 * H):
            softmax_exp(i, N["E"], "n_max", "n_exp", None)
            if i:
                nT(i - 1)
            if i % 2 == 1 and i >= 3:
                nO((i - 3) // 2)
        nT(2 * H - 1)
        nO(H - 1)

        def bo(h):
            r = slice((h % 2) * 64, (h % 2) * 64 + 64)
            evac(f"bO{h}", N["obT"][r, h // 2, :], lambda ps: ps[r, 0:T])

        for h in range(H):
            if h:
                act.wait_ge(sem("keep"), h)
            act.wait_ge(sem("b_min"), h + 1)
            ps = full(act, f"bS{h}")
            step(f(sbk[:, 0, :], ps[:, 0:384], ACT.Abs))
            step(f(sbk[:, 0, :], sbk[:, 0, :], ACT.Exp, scale=-SCALE))
            f(sbk[:, 0, :], sbk[:, 0, :], ACT.Ln, bias=1.0).then_inc(sem("b_log"), 1)
            act.wait_ge(sem("b_arg"), h + 1)
            if h >= 2:
                full(act, f"bO{h - 2}")
            f(sbp[:, h % 2, :], sbk[:, 1, :], ACT.Exp).then_inc(sem("broken"), 1)
            if h:
                bo(h - 1)
        bo(H - 1)
        for ch in range(16):
            evac(f"mg{ch}", N["sgm"][:, ch, :], fn=ACT.Sigmoid)
        sqrt(2)
        evac_norm("xT7", 1)
        for ch in range(FC):
            evac(f"fg{ch}", F["hid"][:, ch, :], fn=ACT.Silu)
        sqrt(2)

    @block.vector
    def _(dve):
        v = nc.vector
        step = Steps(dve, "dve_step")
        nsq = [0]
        nln = [0]

        def inverse_sd(cols):
            nsq[0] += 1
            v.engine_nop().then_inc(sem("var_ready"), 1) if False else None
            dve.wait_ge(sem("sd_ready"), nsq[0])
            step(v.reciprocal(rstd[:, 0:cols], sdv[:, 0:cols]))

        def add_eps(cols, scale, eps):
            v.tensor_scalar(var[:, 0:cols], var[:, 0:cols], scale, eps, ALU.mult, ALU.add
                            ).then_inc(sem("var_ready"), 1)

        def layer_norm(tb, src, frees=()):
            for half in range(2):
                step.go(v.bn_stats(bnst[:, half, :], src[half]))
            step.wait()
            step(v.bn_aggr(mv[:, :], bnst[:, :, :].rearrange("p a b -> p (a b)")))
            v.tensor_scalar(var[:, 0:1], mv[:, 1:2], LN_EPS, None, ALU.add).then_inc(sem("var_ready"), 1)
            inverse_sd(1)
            for half in range(2):
                ins = v.tensor_scalar(yt[:, tb, half * 512:half * 512 + 512], src[half], mv[:, 0:1], rstd[:, 0:1],
                                      ALU.subtract, ALU.mult)
                if frees:
                    free(ins, frees[half])
                    moved(dve, frees[half])
                else:
                    step(ins)
            if tb == 0:
                nln[0] += 1
                dve.wait_ge(sem("lnp"), 16 * nln[0])
            step(v.tensor_tensor(yt[:, tb, :], yt[:, tb, :], lnp[:, 0, :], ALU.mult))
            v.tensor_tensor(xt[:, tb, :], yt[:, tb, :], lnp[:, 1, :], ALU.add).then_inc(sem("x_ready"), 1)

        def residual_norm(name):
            for tb in range(TB):
                for half in range(2):
                    cs = slice(half * 512, half * 512 + 512)
                    ps = full(dve, f"{name}_{tb}_{half}")
                    free(v.scalar_tensor_tensor(yt[:, tb, cs], xt[:, tb, cs], ALPHA, ps[:, :], ALU.mult, ALU.add),
                         f"{name}_{tb}_{half}")
                    moved(dve, f"{name}_{tb}_{half}")
                layer_norm(tb, [yt[:, tb, 0:512], yt[:, tb, 512:1024]])

        dve.wait_ge(sem("small"), 16 * 5)
        v.memset(A["v"][:, :, :, 128:129], 1.0).then_inc(sem("v_ones"), 1)
        ps = full(dve, "gi")
        free(v.tensor_scalar(A["ig"], ps[0:H, 0:T], A["bif"][:, 0:1], None, ALU.add), "gi")
        ps = full(dve, "gf")
        free(v.tensor_scalar(A["xf"], ps[0:H, 0:T], A["bif"][:, 1:2], None, ALU.add), "gf")
        moved(dve, "gi")
        moved(dve, "gf")
        step.go(v.memset(A["B"], 1.0))
        v.scalar_tensor_tensor(A["ax"], A["xf"], -1.0, A["xf"], ALU.mult, ALU.max).then_inc(sem("abs_ready"), 1)
        dve.wait_ge(sem("log1p"), 1)
        step(v.scalar_tensor_tensor(A["ex"], A["xf"], 0.0, A["lf"], ALU.min, ALU.subtract))
        step(v.tensor_tensor_scan(A["m"], A["B"], A["ex"], 0.0, ALU.mult, ALU.add))
        step(v.tensor_tensor(A["a"], A["ig"], A["m"], ALU.subtract))
        step(v.tensor_tensor_scan(A["M"], A["a"], A["a"], 0.0, ALU.max, ALU.max))
        step(v.tensor_tensor(A["m"], A["m"], A["M"], ALU.add))
        v.tensor_scalar(A["nM"], A["M"], -1.0, None, ALU.mult).then_inc(sem("gates"), 1)
        for j in range(4):
            nm = f"nb{j}"
            ps = full(dve, nm)
            for e in range(2):
                step.go(v.tensor_tensor(A["negM"][:, 2 * j + e, 0:T], ps[:, e * T:(e + 1) * T], maskT[:, 0:T], ALU.add))
                ins = v.tensor_tensor(A["negM"][:, 2 * j + e, T:384], ps[:, e * T + P:(e + 1) * T], maskT[:, T:384], ALU.add)
                if e == 0:
                    step.go(ins)
            free(ins, nm)
        moved(dve, "nb3")
        step.wait()
        moved(dve, "acol")

        def m_arg(h):
            step.go(v.tensor_scalar(A["tm"][:, h % 2, 0:T], A["negM"][:, h, 0:T], A["acol"][:, 0, h:h + 1], 0.0,
                                    ALU.add, ALU.min))
            v.tensor_scalar(A["tm"][:, h % 2, T:384], A["negM"][:, h, T:384], A["acol"][:, 1, h:h + 1], 0.0,
                            ALU.add, ALU.min).then_inc(sem("m_arg"), 1)

        def m_fin(h):
            ps = full(dve, f"mO{h}")
            o2 = ps[:, 0:258].rearrange("p (b n) -> p b n", b=2)
            d_ = A["den"][:, h % 2, :]
            r_ = A["rden"][:, h % 2, :]
            step(v.tensor_copy(d_, o2[:, :, 128]))
            step(v.scalar_tensor_tensor(d_, d_, -1.0, d_, ALU.mult, ALU.max))
            step(v.tensor_tensor(d_, d_, A["enm"][:, :, h], ALU.max))
            step(v.reciprocal(r_, d_))
            step.go(v.tensor_scalar(A["h"][:, 0, h, :], o2[:, 0, 0:128], r_[:, 0:1], None, ALU.mult))
            free(v.tensor_scalar(A["h"][:, 1, h, :], o2[:, 1, 0:128], r_[:, 1:2], None, ALU.mult), f"mO{h}")
            moved(dve, f"mO{h}")
            for tb in range(TB):
                step.go(v.bn_stats(A["st"][:, tb * H + h, :], A["h"][:, tb, h, :]))

        m_arg(0)
        m_arg(1)
        for h in range(H):
            dve.wait_ge(sem("m_exp"), h + 1)
            ps = full(dve, f"mS{h}")
            if h >= 2:
                full(dve, f"mO{h - 2}")
            free(v.tensor_tensor(A["Pm"][:, h % 2, :], A["tm"][:, h % 2, :], ps[:, 0:384], ALU.mult), f"mS{h}")
            if h + 2 < H:
                moved(dve, f"mS{h}")
                m_arg(h + 2)
            if h:
                m_fin(h - 1)
        m_fin(H - 1)
        step.wait()
        st = A["st"]
        step.go(v.tensor_tensor(A["mu"], st[:, :, 1], st[:, :, 4], ALU.add))
        step.go(v.tensor_tensor(A["t1"], st[:, :, 1], st[:, :, 4], ALU.subtract))
        step.go(v.tensor_tensor(A["t2"], st[:, :, 2], st[:, :, 5], ALU.add))
        step.wait()
        step.go(v.tensor_scalar(A["mu"], A["mu"], 0.5, None, ALU.mult))
        step.go(v.tensor_tensor(A["t1"], A["t1"], A["t1"], ALU.mult))
        step.wait()
        step.go(v.tensor_scalar(A["t2"], A["t2"], 1.0 / 128, LN_EPS, ALU.mult, ALU.add))
        step.wait()
        v.scalar_tensor_tensor(var[:, 0:16], A["t1"], 0.25, A["t2"], ALU.mult, ALU.add).then_inc(sem("var_ready"), 1)
        inverse_sd(16)
        for tb in range(TB):
            for h in range(H):
                i = tb * H + h
                step.go(v.tensor_scalar(A["h"][:, tb, h, :], A["h"][:, tb, h, :], A["mu"][:, i:i + 1], rstd[:, i:i + 1],
                                        ALU.subtract, ALU.mult))
            step.wait()
            hv = A["h"][:, tb, :, :].rearrange("p h n -> p (h n)")
            step(v.tensor_tensor(hv, hv, A["g"], ALU.mult))
            for half in range(2):
                moved(dve, f"og_{tb}_{half}")
            v.tensor_tensor(hv, hv, A["og"][:, tb, :], ALU.mult).then_inc(sem("h_ready"), 1)
        residual_norm("mix0")

        def top16(vals, idx, scores, n):
            for lo in (0, 8):
                if lo:
                    for i in range(n):
                        step.go(v.match_replace(scores[:, i, :], vals[:, i, 0:8], scores[:, i, :], -3.0e38))
                    step.wait()
                    yield
                for i in range(n):
                    step.go(v.max(vals[:, i, lo:lo + 8], scores[:, i, :]))
                step.wait()
                yield
                for i in range(n):
                    step.go(v.max_index(idx[:, i, lo:lo + 8], vals[:, i, lo:lo + 8], scores[:, i, :]))
                step.wait()
                yield

        def choose(l, tb):
            r = l * TB + tb
            for j in range(4):
                moved(dve, f"sc{l}_{tb}_{j}")
            if tb == 0:
                full(dve, f"sc{l}_1_3")
            yield from top16(v1, i1, sc[:, tb, :, :], 16)
            step.go(v.tensor_copy(i1f[:, :, :], i1[:, :, :]))
            for h in range(PH):
                step.go(v.tensor_tensor(cand[:, h, :].rearrange("p (i j) -> p i j", i=16),
                                        v1[:, 2 * h, :].unsqueeze(2).broadcast_to([P, 16, 16]),
                                        v1[:, 2 * h + 1, :].unsqueeze(1).broadcast_to([P, 16, 16]), ALU.add))
            step.wait()
            yield
            yield from top16(tsv, tp, cand, PH)
            step(v.tensor_copy(gsum[:, :], tsv[:, :, 0]))
            v.tensor_tensor(tsv[:, :, :], tsv[:, :, :], gsum[:, :].unsqueeze(2).broadcast_to([P, PH, 16]),
                            ALU.subtract).then_inc(sem("gate_arg"), 1)
            step.go(v.tensor_scalar(p12[:, 0, :, :], tp[:, :, :], 4, None, ALU.logical_shift_right))
            step.go(v.tensor_scalar(p12[:, 1, :, :], tp[:, :, :], 15, None, ALU.bitwise_and))
            step.wait()
            step(v.tensor_copy(p12f[:, :, :, :].rearrange("p a b c -> p (a b c)"),
                               p12[:, :, :, :].rearrange("p a b c -> p (a b c)")))
            yield
            i4 = i1f[:, :, :].rearrange("p (h c) j -> p h c j", c=2)
            for e, q in ((0, eq), (1, eq2)):
                step(v.tensor_tensor(q, p12f[:, e, :, :].unsqueeze(3).broadcast_to([P, PH, 16, 16]),
                                     iota16[:, :].unsqueeze(1).unsqueeze(1).broadcast_to([P, PH, 16, 16]),
                                     ALU.is_equal))
                yield
                step(v.tensor_tensor(q, q, i4[:, :, e, :].unsqueeze(2).broadcast_to([P, PH, 16, 16]), ALU.mult))
                yield
                step(v.tensor_reduce(i12[:, e, :, :], q, AX, ALU.add))
                yield
            ev = i12[:, 0, :, :].rearrange("p h k -> p (h k)")
            step(v.scalar_tensor_tensor(ev, ev, float(NK), i12[:, 1, :, :].rearrange("p h k -> p (h k)"),
                                        ALU.mult, ALU.add))
            v.tensor_scalar(eidx[:, tb, :], ev, float(l * NEXP), None, ALU.add).then_inc(sem("experts"), 1)

        def gates(l, tb):
            dve.wait_ge(sem("gate_exp"), l * TB + tb + 1)
            step(v.tensor_reduce(gsum[:, :], tsv[:, :, :], AX, ALU.add))
            step(v.reciprocal(grec[:, :], gsum[:, :]))
            step(v.tensor_tensor(gate[:, tb, :].rearrange("p (h k) -> p h k", h=PH), tsv[:, :, :],
                                 grec[:, :].unsqueeze(2).broadcast_to([P, PH, 16]), ALU.mult))

        def experts(l, tb, it):
            r = l * TB + tb
            for g in range(NG):
                for s in range(g * GRP, (g + 1) * GRP):
                    dve.wait_ge(sem(f"row{s}"), (r * ITERS + it + 1) * 16)
                    v.tensor_tensor_reduce(out=gath[:, s, 0:D], in0=gath[:, s, 0:D], in1=xt[:, tb, :], scale=1.0,
                                           scalar=0.0, op0=ALU.mult, op1=ALU.add, accum_out=dots[:, s:s + 1]
                                           ).then_inc(sem("dots"), 1)
                dve.wait_ge(sem("gelu"), (r * ITERS + it) * NG + g + 1)
                if g == 0:
                    dve.sem_inc(sem("gate_go"), 1)
                    v.tensor_copy(gcur[:, :], gate[:, tb, bass.ds(it * SLOTS, SLOTS)]).then_inc(sem("gcur"), 1)
                    dve.wait_ge(sem("gcur"), r * ITERS + it + 1)
                for s in range(g * GRP, (g + 1) * GRP):
                    v.tensor_scalar(diag[:, s, :], ident[:, :], glu[:, s:s + 1], gcur[:, s:s + 1],
                                    ALU.mult, ALU.mult).then_inc(sem("diag"), 1)
                yield

        def peer(l):
            for _ in choose(l, 0):
                pass
            gates(l, 0)
            pieces = choose(l, 1)
            for it in range(WOVEN):
                for _ in experts(l, 0, it):
                    next(pieces, None)
            for _ in pieces:
                pass
            gates(l, 1)
            for tb in range(TB):
                with dve.Fori(WOVEN if tb == 0 else 0, ITERS) as it:
                    for _ in experts(l, tb, it):
                        pass
                nm = [f"pe{l}_{tb}_{half}" for half in range(2)]
                src = [full(dve, x)[:, :] for x in nm]
                layer_norm(tb, src, nm)

        def ple(l):
            for half in range(2):
                for tb in range(TB):
                    cs = slice(half * 512, half * 512 + 512)
                    moved(dve, f"pg{l}_{tb}_{half}")
                    ps = full(dve, f"pp{l}_{tb}_{half}")
                    free(v.tensor_tensor(yt[:, tb, cs], yt[:, tb, cs], ps[:, :], ALU.mult), f"pp{l}_{tb}_{half}")
            for tb in range(TB):
                for half in range(2):
                    moved(dve, f"pp{l}_{tb}_{half}")
                v.tensor_tensor(xt[:, tb, :], xt[:, tb, :], yt[:, tb, :], ALU.add).then_inc(sem("x_ready"), 1)

        peer(0)
        ple(0)

        step(v.tensor_copy(M["posf"], posi[:, :]))
        step(v.tensor_scalar(M["ang"], M["posf"], invf[:, 0:1], None, ALU.mult))
        TWO = 2 * math.pi
        C1 = 6.28125
        C2 = float(np.float32(np.round((TWO - C1) * 2 ** 20) / 2 ** 20))
        C3 = TWO - C1 - C2
        for dst, shift in ((M["w1"], 0.0), (M["w2"], 0.25)):
            step(v.tensor_scalar(M["w3"], M["ang"], 1.0 / TWO, shift, ALU.mult, ALU.add))
            step(v.tensor_scalar(M["w3"], M["w3"], 12582912.0, None, ALU.add))
            step(v.tensor_scalar(M["w3"], M["w3"], -12582912.0, None, ALU.add))
            step(v.scalar_tensor_tensor(dst, M["w3"], -C1, M["ang"], ALU.mult, ALU.add))
            step(v.scalar_tensor_tensor(dst, M["w3"], -C2, dst, ALU.mult, ALU.add))
            step(v.scalar_tensor_tensor(dst, M["w3"], -C3, dst, ALU.mult, ALU.add))
            if shift:
                step(v.tensor_scalar(dst, dst, math.pi / 2, None, ALU.add))
            ins = v.tensor_scalar(dst, dst, 3.1415925, -3.1415925, ALU.min, ALU.max)
            if shift:
                ins.then_inc(sem("ang_ready"), 1)
            else:
                step(ins)
        for tb in range(TB):
            moved(dve, f"ckv_{tb}")
            step.go(v.tensor_tensor_reduce(out=M["oT"][:, tb, :], in0=yt[:, tb, 0:KV_RANK], in1=yt[:, tb, 0:KV_RANK],
                                           scale=1.0, scalar=0.0, op0=ALU.mult, op1=ALU.add,
                                           accum_out=M["ssq"][:, tb:tb + 1]))
            moved(dve, f"cq_{tb}")
            step.go(v.tensor_tensor_reduce(out=M["cq"][:, tb, :], in0=yt[:, tb, 512:512 + Q_RANK],
                                           in1=yt[:, tb, 512:512 + Q_RANK], scale=1.0, scalar=0.0, op0=ALU.mult,
                                           op1=ALU.add, accum_out=M["ssq"][:, 2 + tb:3 + tb]))
        step.wait()
        step.go(v.tensor_scalar(var[:, 0:2], M["ssq"][:, 0:2], 1.0 / KV_RANK, LN_EPS, ALU.mult, ALU.add))
        step.wait()
        v.tensor_scalar(var[:, 2:4], M["ssq"][:, 2:4], 1.0 / Q_RANK, LN_EPS, ALU.mult, ALU.add).then_inc(sem("var_ready"), 1)
        inverse_sd(4)
        dve.wait_ge(sem("mla_par"), 32)
        for tb in range(TB):
            v.scalar_tensor_tensor((M["ckv"] if tb == 0 else M["ckv2"]), yt[:, tb, 0:KV_RANK], rstd[:, tb:tb + 1], M["cg"],
                                   ALU.mult, ALU.mult).then_inc(sem("ckv_ready"), 1)
        for tb in range(TB):
            v.scalar_tensor_tensor(M["cq"][:, tb, :], yt[:, tb, 512:512 + Q_RANK], rstd[:, 2 + tb:3 + tb], M["qg"],
                                   ALU.mult, ALU.mult).then_inc(sem("cq_ready"), 1)
        dve.wait_ge(sem("trig"), 2)

        def rotate(x1, x2, o1, o2, t, names=None):
            step.go(v.tensor_tensor(t[0], x1, M["cos"], ALU.mult))
            step.go(v.tensor_tensor(t[1], x2, M["sin"], ALU.mult))
            step.go(v.tensor_tensor(t[2], x1, M["sin"], ALU.mult))
            ins = v.tensor_tensor(t[3], x2, M["cos"], ALU.mult)
            step.go(ins)
            step.wait()
            step.go(v.tensor_tensor(o1, t[0], t[1], ALU.subtract))
            step.go(v.tensor_tensor(o2, t[2], t[3], ALU.add))
            step.wait()

        moved(dve, "kr0")
        moved(dve, "kr1")
        tt = [M["oT"][:, j, :] for j in range(4)]
        rotate(M["t"][:, 0, :], M["t"][:, 1, :], M["K12"][:, 0, :], M["K12"][:, 1, :], tt)
        step.go(v.memset(M["krm"], 0.0))
        step.wait()
        for j in range(4):
            r = slice(32 * j, 32 * j + 32)
            ins = v.tensor_copy(M["krm"][r, j, :, :], M["K12"][r, :, :])
            if j < 3:
                step.go(ins)
        ins.then_inc(sem("rope"), 1)
        for half in range(2):
            for e in range(2):
                ps = full(dve, f"qr{half}_{e}")
                free(v.tensor_copy(M["t"][:, e, :], ps[:, 0:T]), f"qr{half}_{e}")
                moved(dve, f"qr{half}_{e}")
            rotate(M["t"][:, 0, :], M["t"][:, 1, :], M["R"][:, half, 0, :], M["R"][:, half, 1, :], tt)
            v.tensor_copy(M["w3"][:, 0:1], M["R"][:, half, 1, 0:1]).then_inc(sem("rope"), 1)

        def sm_max(nm, i, E, scale, bias, ready, before):
            ps = full(dve, nm)
            if before:
                full(dve, before)
            free(v.scalar_tensor_tensor(E[:, i % 3, :], ps[:, 0:384], scale, bias, ALU.mult, ALU.add), nm)
            moved(dve, nm)
            step.go(v.tensor_reduce(rmax[:, i % 3, 0:1], E[:, i % 3, 0:P], AX, ALU.max, negate=True))
            v.tensor_reduce(rmax[:, i % 3, 1:2], E[:, i % 3, P:384], AX, ALU.max, negate=True).then_inc(sem(ready), 1)

        def sm_norm(i, E, exp_sem, probs, gcol=None):
            dve.wait_ge(sem(exp_sem), i + 1)
            step(v.reciprocal(rrec[:, i % 3, :], rsum[:, i % 3, :]))
            if gcol is not None:
                step(v.tensor_tensor(rrec[:, i % 3, :], rrec[:, i % 3, :], gcol, ALU.mult))
            step.go(v.tensor_scalar(E[:, i % 3, 0:P], E[:, i % 3, 0:P], rrec[:, i % 3, 0:1], None, ALU.mult))
            v.tensor_scalar(E[:, i % 3, P:384], E[:, i % 3, P:384], rrec[:, i % 3, 1:2], None, ALU.mult
                            ).then_inc(sem(probs), 1)

        for h in range(H):
            sm_max(f"lS{h}", h, M["E"], MLA_SCALE, maskQ[:, :], "l_max", f"lT{h - 3}" if h >= 3 else None)
            if h:
                sm_norm(h - 1, M["E"], "l_exp", "probs")
        sm_norm(H - 1, M["E"], "l_exp", "probs")
        residual_norm("mix1")
        peer(1)
        ple(1)

        def rms_stats():
            for tb in range(TB):
                step.go(v.tensor_tensor_reduce(out=yt[:, tb, :], in0=xt[:, tb, :], in1=xt[:, tb, :], scale=1.0,
                                               scalar=0.0, op0=ALU.mult, op1=ALU.add, accum_out=var[:, tb:tb + 1]))
            step.wait()
            add_eps(2, 1.0 / D, RMS_EPS)
            inverse_sd(2)

        dve.wait_ge(sem("x_ready"), TB * 6)
        rms_stats()
        for tb in range(TB):
            v.tensor_scalar(yt[:, tb, :], xt[:, tb, :], rstd[:, tb:tb + 1], None, ALU.mult).then_inc(sem("xn_ready"), 1)
        dve.wait_ge(sem("hyb_par"), 16 * 7)
        for j in range(12):
            part, hf = j // 2, j % 2
            nm = f"ada{j}"
            ps = full(dve, nm)
            if part in (2, 5):
                g = (N["g1"] if part == 2 else N["g2"])[:, hf * 512:hf * 512 + 512]
                free(v.tensor_tensor(g, ps[:, :], g, ALU.add), nm)
            else:
                q = {0: 0, 1: 1, 3: 2, 4: 3}[part]
                free(v.tensor_tensor(N["mod"][:, q, hf * 4:hf * 4 + 4], ps[:, 0:4], N["bada"][:, q, hf * 4:hf * 4 + 4],
                                     ALU.add), nm)
        for j in range(12):
            moved(dve, f"ada{j}")
        step.go(v.scalar_tensor_tensor(N["gs"][:, 0, :], N["mod"][:, 1, :], 1.0, N["ng"][:, 0, :], ALU.add, ALU.mult))
        v.scalar_tensor_tensor(N["gs"][:, 1, :], N["mod"][:, 3, :], 1.0, N["ng"][:, 1, :], ALU.add, ALU.mult
                               ).then_inc(sem("mod_ready"), 1)
        dve.wait_ge(sem("hyb_const"), 1)
        for kv in range(2):
            moved(dve, f"cmp{kv}")
            for g in range(2):
                i = 2 * kv + g
                base = kcv[:, i, :].rearrange("p (n l) -> p l n", l=16)
                pc = N["posc"][:, kv, :]
                for hf in range(2):
                    ins = v.tensor_tensor(ckin[:, i, hf * 16:hf * 16 + 16, 0:NCMP], base[:, :, hf:hf + NCMP],
                                          pc[:, hf * 16:hf * 16 + 16].unsqueeze(2).broadcast_to([HD, 16, NCMP]), ALU.add)
                    if (g, hf) != (1, 1):
                        step.go(ins)
            ins.then_inc(sem("ckin_ready"), 1)
        ps = full(dve, "vc")
        free(v.tensor_tensor(N["vcm"], ps[:, 0:HD].unsqueeze(1).broadcast_to([P, H, HD]),
                             N["m8"].unsqueeze(2).broadcast_to([P, H, HD]), ALU.mult), "vc")
        cE = N["cE"].rearrange("p b h n -> p (b h) n")
        cmx = N["cmx"].rearrange("p b h -> p (b h)")
        csm = N["csm"].rearrange("p b h -> p (b h)")
        crc = N["crc"].rearrange("p b h -> p (b h)")
        for e in range(2):
            ps = full(dve, f"cS{e}")
            free(v.scalar_tensor_tensor(N["cE"].rearrange("p b (i e) n -> p (b i) e n", e=2)[:, :, e, :],
                                        ps[:, 0:P].rearrange("p (i n) -> p i n", n=CW), SCALE,
                                        N["cb"].rearrange("p b (i e) n -> p (b i) e n", e=2)[:, :, e, :],
                                        ALU.mult, ALU.add), f"cS{e}")
        moved(dve, "cS0")
        moved(dve, "cS1")
        step(v.tensor_reduce(cmx, cE, AX, ALU.max))
        v.tensor_tensor(cE, cE, cmx.unsqueeze(2).broadcast_to([P, 16, CW]), ALU.subtract).then_inc(sem("c_arg"), 1)
        dve.wait_ge(sem("c_exp"), 1)
        step(v.tensor_reduce(csm, cE, AX, ALU.add))
        step(v.reciprocal(crc, csm))
        for tb in range(TB):
            moved(dve, f"vw{tb}")
            ga = N["ga"][:, tb, :].rearrange("p (h e) -> p h e", e=3)
            step(v.scalar_tensor_tensor(N["crc"][:, tb, :], N["crc"][:, tb, :], N["rv"][:, tb:tb + 1], ga[:, :, 0],
                                        ALU.mult, ALU.mult))
        v.tensor_tensor(cE, cE, crc.unsqueeze(2).broadcast_to([P, 16, CW]), ALU.mult).then_inc(sem("cprobs"), 1)

        def gcol(i):
            h, e = i // 2, i % 2
            return N["ga"][:, :, h * 3 + 1 + e]

        for i in range(2 * H):
            h = i // 2
            dve.wait_ge(sem("bias_ready"), h + 1)
            sm_max(f"nS{i}", i, N["E"], SCALE, N["bh"][:, h % 2, :], "n_max", f"nT{i - 3}" if i >= 3 else None)
            if i % 2 == 1:
                v.tensor_copy(mv[:, 0:1], rmax[:, 0, 0:1]).then_inc(sem("bias_used"), 1) if False else None
            if i:
                sm_norm(i - 1, N["E"], "n_exp", "nprobs", gcol(i - 1))
            if i % 2 == 1:
                dve.sem_inc(sem("bias_used"), 1)
        sm_norm(2 * H - 1, N["E"], "n_exp", "nprobs", gcol(2 * H - 1))

        for h in range(H):
            ps = full(dve, f"bS{h}")
            z0, z1, lk = sbk[:, 0, :], sbk[:, 1, :], sbk[:, 2 + h % 2, :]
            if h:
                dve.wait_ge(sem("broken"), h)
            v.tensor_scalar(z1, ps[:, 0:384], SCALE, 0.0, ALU.mult, ALU.min).then_inc(sem("b_min"), 1)
            dve.wait_ge(sem("b_log"), h + 1)
            step(v.tensor_tensor(z1, z1, z0, ALU.subtract))
            if h >= 2:
                full(dve, f"bL{h - 2}")
            free(v.scalar_tensor_tensor(lk, ps[:, 0:384], -SCALE, z1, ALU.mult, ALU.add), f"bS{h}")
            moved(dve, f"bS{h}")
            step.go(v.tensor_tensor(z1, z1, maskS[:, :], ALU.add))
            v.tensor_tensor(lk, lk, keep[:, :], ALU.mult).then_inc(sem("keep"), 1)
            step.wait()
            ps = full(dve, f"bL{h}")
            free(v.tensor_tensor(z1, z1, ps[:, 0:384], ALU.add), f"bL{h}")
            moved(dve, f"bL{h}")
            dve.sem_inc(sem("b_arg"), 1)

        for ch in range(KC):
            moved(dve, f"mg{ch}")
            moved(dve, f"mg{KC + ch}")
            ps = full(dve, f"ya{ch}")
            free(v.tensor_tensor(N["sgm"][:, ch, :], N["sgm"][:, ch, :], ps[:, 0:T], ALU.mult), f"ya{ch}")
            ps = full(dve, f"yb{ch}")
            free(v.tensor_tensor(N["sgm"][:, KC + ch, :], N["sgm"][:, KC + ch, :], ps[:, 0:T], ALU.mult), f"yb{ch}")
            moved(dve, f"ya{ch}")
            moved(dve, f"yb{ch}")
            v.tensor_tensor(xT[:, ch, :], N["sgm"][:, ch, :], N["sgm"][:, KC + ch, :], ALU.add).then_inc(sem("yT"), 1)

        def gated_residual(name, g):
            for tb in range(TB):
                for half in range(2):
                    cs = slice(half * 512, half * 512 + 512)
                    nm = f"{name}_{tb}_{half}"
                    ps = full(dve, nm)
                    free(v.tensor_tensor(yt[:, tb, cs], ps[:, :], g[:, cs], ALU.mult), nm)
                    moved(dve, nm)
                v.tensor_tensor(xt[:, tb, :], xt[:, tb, :], yt[:, tb, :], ALU.add).then_inc(sem("x_ready"), 1)
        gated_residual("mix2", N["g1"])
        dve.wait_ge(sem("x_ready"), TB * 7)
        rms_stats()
        for tb in range(TB):
            v.tensor_scalar(yt[:, tb, :], xt[:, tb, :], rstd[:, tb:tb + 1], None, ALU.mult).then_inc(sem("xn_ready"), 1)
        for ch in range(FC):
            moved(dve, f"fg{ch}")
            ps = full(dve, f"fu{ch}")
            free(v.tensor_tensor(F["hid"][:, ch, :], F["hid"][:, ch, :], ps[:, 0:T], ALU.mult), f"fu{ch}")
            moved(dve, f"fu{ch}")
            dve.sem_inc(sem("hid"), 1)
        gated_residual("dn", N["g2"])
        dve.wait_ge(sem("x_ready"), TB * 8)
        rms_stats()
        dve.wait_ge(sem("lnp"), 16 * 5)
        for tb in range(TB):
            v.scalar_tensor_tensor(yt[:, tb, :], xt[:, tb, :], rstd[:, tb:tb + 1], lnp[:, 0, :], ALU.mult, ALU.mult
                                   ).then_inc(sem("out_ready"), 1)


def layouts(inputs):
    g = {k: np.asarray(v) for k, v in inputs.items()}
    bc = lambda v: np.ascontiguousarray(np.broadcast_to(v, (P,) + v.shape))
    cols = lambda v: np.ascontiguousarray(v.reshape(-1, P).T)
    d = {k: g[k] for k in ("a_w_in", "a_w_out", "kv_w_up", "b_w_dq", "b_w_out", "peer_w_q",
                           "ple_w_proj", "ple_w_gate", "w_ada_2", "cmp_w1_k_2", "cmp_w1_v_2", "w_proj_a_2", "w_proj_b_2", "w_out_2", "w_ffn_gate_2", "w_ffn_up_2",
                           "w_ffn_down_2")}
    w = g["kv_w_down"]
    r1, r2 = w[:, KV_RANK:KV_RANK + RHALF], w[:, KV_RANK + RHALF:]
    d["kv_w_down_r"] = np.concatenate([w[:, :KV_RANK]] + [r1] * 4 + [r2] * 4, axis=1)
    w = g["b_w_uq"][0].reshape(Q_RANK, 2, 4, 192)
    d["b_w_uq_p"] = np.concatenate([w[..., :128].reshape(Q_RANK, 2, 512), w[..., 128:160].reshape(Q_RANK, 2, 128),
                                    w[..., 160:].reshape(Q_RANK, 2, 128)], axis=2).reshape(Q_RANK, 1536)
    w = g["w_in_2"][0]
    twice = lambda c0: [w[:, c0 + j * HD:c0 + (j + 1) * HD] for j in (0, 0, 1, 1)]
    d["w_in_2r"] = np.concatenate([w[:, :768]] + twice(768) + twice(1024) + [w[:, 896:1024], w[:, 1152:]], axis=1)
    d["cmp_w2"] = np.ascontiguousarray(np.stack([g["cmp_w2_k_2"][0]] * 2 + [g["cmp_w2_v_2"][0]], axis=1))
    d["x"] = g["x"][0]
    d["xTin"] = np.ascontiguousarray(g["x"][0].T)
    d["pT"] = np.ascontiguousarray(g["p"][:, 0].transpose(0, 2, 1))
    d["pos"] = bc(g["positions"][0])
    d["invf"] = np.tile((np.float32(THETA) ** (-np.arange(0, ROPE, 2, dtype=np.float32) / np.float32(ROPE))), 4)[:, None].astype(np.float32)
    gb = np.stack([g["ln_g"], g["ln_b"]], axis=2)
    d["lnp"] = np.ascontiguousarray(np.broadcast_to(gb[:, :, None], (DEPTH, 2, P, 2, D)))
    d["hng"] = bc(g["a_hn_g"][0])
    d["bif"] = np.ascontiguousarray(g["a_b_if"][0].T)
    d["kvg"] = bc(g["kv_norm_g"])
    d["qng"] = bc(g["b_q_norm_g"][0])
    d["keysT"] = np.ascontiguousarray(g["peer_sub_keys"].transpose(0, 4, 1, 2, 3).reshape(DEPTH, P, 2048))
    d["uv"] = np.concatenate([g["peer_u"], g["peer_v"]], axis=2).reshape(DEPTH * NEXP, 2 * D)
    d["cT"] = cols(g["c_2"][0])
    b = g["b_ada_2"][0].reshape(6, D)
    d["badaT"] = np.ascontiguousarray(np.stack([cols(b[i]) for i in (0, 1, 3, 4)], axis=1))
    d["bg1"], d["bg2"] = bc(b[2]), bc(b[5])
    d["ngT"] = np.ascontiguousarray(np.stack([cols(g["norm_mix_g_2"][0]), cols(g["norm_ffn_g_2"][0])], axis=1))
    d["nfg"] = bc(g["norm_final_g_2"])
    d["posc"] = np.ascontiguousarray(np.stack([g["cmp_pos_k_2"][0].T, g["cmp_pos_v_2"][0].T], axis=1))
    return d


def kernel(**inputs):
    import concourse.bacc as bacc
    from concourse.bass_utils import run_bass_kernel_spmd as run
    nc = bacc.Bacc("TRN2", target_bir_lowering=False, num_devices=1)
    d = layouts(inputs)
    aps = {k: nc.dram_tensor("in_" + k, v.shape, mybir.dt.from_np(v.dtype), kind="ExternalInput").ap()
           for k, v in d.items()}
    out = nc.dram_tensor("out", (T, D), F32, kind="ExternalOutput").ap()
    build(nc, aps, out)
    r = run(nc, [{"in_" + k: v for k, v in d.items()}], core_ids=[0])
    return r.results[0]["out"].reshape(1, T, D)
```

```python
import math
from contextlib import ExitStack

import numpy as np
import concourse.bass as bass
from concourse import mybir

F32 = mybir.dt.float32
U32 = mybir.dt.uint32
I32 = mybir.dt.int32
ALU = mybir.AluOpType
ACT = mybir.ActivationFunctionType
AX = mybir.AxisListType.X

P = 128
D = 1024
T = 256
TB = T // P
KC = D // P
DEPTH = 2
ALPHA = (2.0 * DEPTH) ** 0.25
LN_EPS = 1e-5
RMS_EPS = 1e-6
H = 8
QK = D // (2 * H)
A_V, A_G, A_O = 2 * H * QK, 2 * H * QK + D, 2 * H * QK + D + 2 * H
ROPE, RHALF = 64, 32
KV_RANK, Q_RANK = 256, 384
MLA_SCALE = (128 + ROPE) ** -0.5
THETA = 10000.0
PH, NK, TOPK, NEXP = 8, 128, 16, 16384
PAIRS = PH * TOPK
SLOTS = 8
GRP = 2
NG = SLOTS // GRP
ITERS = PAIRS // SLOTS
UH = 2
UNITS = PH // UH
UITERS = ITERS // UNITS
UPAIRS = UH * TOPK
SPREAD = 2
WOVEN = 1 + SPREAD * (TB * UNITS - 2)
HD = 64
NCMP, CW = 15, 16
FF = 2816
FC = FF // P
SCALE = 1.0 / math.sqrt(HD)
SLOPES = [2.0 ** (-8.0 * (i + 1) / H) for i in range(H)]
FAR = 1e33
NEG = -1e30
ADA_COLS = (0, 1, 2, 3, 6, 7, 8, 9)
ADA_GATES = (4, 5, 10, 11)
SLOT = 4096
NW = 4


def build(nc, a, out, dbg=None):
    with ExitStack() as ctx:
        program(nc, a, out, ctx, dbg or {})


def program(nc, a, out, ctx, dbg):
    def sb(name, shape, dt=F32):
        return ctx.enter_context(nc.sbuf_tensor(name, shape, dt))

    sems = {}

    def sem(name):
        if name not in sems:
            sems[name] = ctx.enter_context(nc.semaphore(name))
        return sems[name]

    ring = sb("ring", [P, NW, SLOT])
    arena = sb("arena", [P, SLOTS * 2 * D])
    qreg = sb("qreg", [P, 4096])
    sreg = sb("sreg", [P, 4096])
    xt = sb("x_tok", [P, TB, D])
    yt = sb("y_tok", [P, TB, D])
    xT = sb("xT", [P, KC, T])
    lnp = sb("lnp", [P, 2, D])
    ident = sb("ident", [P, P])
    identa = sb("identa", [P, P])
    ones = sb("ones", [P, P])
    upper = sb("upper", [P, P])
    maskT = sb("maskT", [P, 384])
    maskS = sb("maskS", [P, 384])
    keep = sb("keep", [P, 384])
    maskQ = sb("maskQ", [P, 384])
    iota16 = sb("iota16", [P, 16])
    bnst = sb("bnst", [P, 2, 6])
    mv = sb("mv", [P, 2])
    var = sb("var", [P, 16])
    sdv = sb("sdv", [P, 16])
    rstd = sb("rstd", [P, 16])
    psum = [ctx.enter_context(nc.psum_tensor(f"bank{b}", [P, 512], F32)) for b in range(8)]

    def carve(region, parts=P):
        at = [0]

        def take(*shape, p=parts):
            n = int(np.prod(shape))
            v = region[0:p, at[0]:at[0] + n]
            at[0] += n
            assert at[0] <= region.shape[1], (at, region.shape)
            if len(shape) > 1:
                names = "abcd"[:len(shape)]
                v = v.rearrange(f"p ({' '.join(names)}) -> p {' '.join(names)}",
                                **{k: s for k, s in zip(names, shape)})
            return v
        return take

    bank_full = [sem(f"bank_full{b}") for b in range(8)]
    bank_free = [sem(f"bank_free{b}") for b in range(8)]
    slot_loaded = [sem(f"slot_loaded{i}") for i in range(NW)]
    place = {}
    uses = [0] * 8

    def full(eng, name):
        b, k = place[name]
        eng.wait_ge(bank_full[b], k + 1)
        return psum[b]

    def moved(eng, name):
        b, k = place[name]
        eng.wait_ge(bank_free[b], k + 1)

    def free(ins, name):
        ins.then_inc(bank_free[place[name][0]], 1)

    ada_order, ada_at = [], {}
    loads = []

    block = ctx.enter_context(nc.Block())

    class Steps:
        def __init__(self, eng, name):
            self.eng, self.sem, self.n = eng, sem(name), 0

        def go(self, ins):
            ins.then_inc(self.sem, 1)
            self.n += 1

        def wait(self):
            self.eng.wait_ge(self.sem, self.n)

        def __call__(self, ins):
            self.go(ins)
            self.wait()

    c = carve(arena)
    A = dict(qT=c(4, T), kT=c(4, T), v=c(TB, H, 129), og=c(TB, D), h=c(TB, H, 128),
             negM=c(H, 384), Pm=c(2, 384), tm=c(2, 384), hT=c(KC, T), g=c(D))
    c = carve(sreg)
    A.update(sel=c(H, P, p=8), ig=c(T, p=8), xf=c(T, p=8), ax=c(T, p=8), ex=c(T, p=8), lf=c(T, p=8),
             B=c(T, p=8), a=c(T, p=8), M=c(T, p=8), nM=c(T, p=8), m=c(T, p=8))
    c = carve(qreg)
    A.update(acol=c(TB, H), enm=c(TB, H), den=c(2, 2), rden=c(2, 2), st=c(TB * H, 6),
             mu=c(16), t1=c(16), t2=c(16), bif=c(2, p=8))
    gath = arena[:, :].rearrange("p (s n) -> p s n", s=SLOTS)
    pq = qreg[:, :].rearrange("p (c t) -> p c t", c=16)
    sc = sreg[:, :].rearrange("p (b c n) -> p b c n", b=TB, c=16)
    c = carve(yt[:, :, :].rearrange("p b d -> p (b d)"))
    v1 = c(2 * UH, 16)
    i1 = c(2 * UH, 16).bitcast(U32)
    i1f = c(2 * UH, 16)
    tsv = c(UH, 16)
    tp = c(UH, 16).bitcast(U32)
    p12 = c(2, UH, 16).bitcast(U32)
    p12f = c(2, UH, 16)
    i12 = c(2, UH, 16)
    cand = c(UH, 256)
    eq = cand.rearrange("p h (k j) -> p h k j", k=16)
    eidx = sb("eidx", [P, TB, PAIRS], U32)
    gate = sb("gate", [P, TB, PAIRS])
    gsum = sb("gsum", [P, UH])
    grec = sb("grec", [P, UH])
    idc = sb("idc", [P, SLOTS], U32)
    gcur = sb("gcur", [P, SLOTS])
    dots = sb("dots", [P, SLOTS])
    glu = sb("glu", [P, SLOTS])
    diag = (xT[:, :, :].rearrange("p k t -> p (k t)")[:, 0:SLOTS * P]
            .rearrange("p (s n) -> p s n", s=SLOTS))
    c = carve(arena)
    M = dict(knT=c(H, T), v=c(TB, D), qnT=c(H, T), oT=c(H, T), krm=c(4, 2, T), ckvT=c(2, T),
             cqT=c(3, T), R=c(2, 2, T), K12=c(2, T), t=c(4, T))
    c = carve(sreg)
    M.update(E=c(3, 384), PT=c(4, 384), ckv=c(KV_RANK), ckv2=c(KV_RANK))
    c = carve(qreg)
    M.update(cq=c(TB, Q_RANK), cg=c(KV_RANK), qg=c(Q_RANK), ang=c(T), cos=c(T), sin=c(T), w1=c(T),
             w2=c(T), w3=c(T), posf=c(T), ssq=c(4), sm=c(2, 8))
    cT = sb("cT", [P, KC])
    scT = sb("silu_cT", [P, KC])
    adac = sb("ada_columns", [P, 4, KC])
    junk = sb("junk", [P, P])
    posi = sb("posi", [P, T], I32)
    invf = sb("invf", [P, 1])
    rmax = sb("rmax", [P, 3, 2])
    rsum = sb("rsum", [P, 3, 2])
    rrec = sb("rrec", [P, 3, 2])
    c = carve(arena)
    N = dict(qT=c(4, T), ksT=c(2, T), kwT=c(2, T), vs=c(TB, P), vw=c(TB, P), qbT=c(4, T), kbT=c(4, T),
             vb=c(TB, 512), sgm=c(16, T), oaT=c(4, T), obT=c(4, T), g1=c(D), g2=c(D), sbk=c(4, 384),
             sbp=c(2, 384))
    sbk, sbp = N["sbk"], N["sbp"]
    c = carve(qreg)
    N.update(E=c(3, 384), PT=c(4, 384), bh=c(2, 384), dist=c(384))
    c = carve(sreg)
    N.update(cb=c(TB, H, CW), cE=c(TB, H, CW), cPT=c(T), vcm=c(H, HD), cdist=c(TB, CW), hid=c(2, CW), hidv=c(2, 4, CW),
             kc=c(2, CW), ga=c(TB, 24), w2=c(3, HD), m8=c(8), rv=c(2), cmx=c(TB, H), csm=c(TB, H),
             crc=c(TB, H), mod=c(4, KC), bada=c(4, KC), ng=c(2, KC), gs=c(2, KC),
             posc=c(2, 32, p=64))
    c = carve(N["sgm"].rearrange("p a b -> p (a b)"), 64)
    ckin = c(4, 32, CW)
    kcv = c(4, T)
    c = carve(arena[:, :])
    F = dict(hid=c(FC, T))

    NX = 8

    @block.tensor
    def _(pe):
        n_open = [0]
        held = set()

        def open_(name):
            b = n_open[0] % 8
            n_open[0] += 1
            k = uses[b]
            uses[b] += 1
            place[name] = (b, k)
            if k:
                pe.wait_ge(bank_free[b], k)
            return psum[b]

        def close(ins, name):
            ins.then_inc(bank_full[place[name][0]], 1)

        def mm(o, l, r, start=True, stop=True):
            return nc.tensor.matmul(o, l, r, start=start, stop=stop)

        nw = [0]

        def take(src, kc, n, p=P):
            i = nw[0]
            nw[0] += 1
            s = i % NW
            rec = dict(kind="w", src=src, slot=s, i=i, kc=kc, n=n, p=p, done=None)
            loads.append(rec)
            pe.wait_ge(slot_loaded[s], 16 * (i // NW + 1))
            v = ring[0:p, s, 0:kc * n].rearrange("p (k n) -> p k n", k=kc)
            return v, rec

        def last_use(rec, name):
            b, k = place[name]
            rec["done"] = (bank_full[b], k + 1)

        def ada_load(j):
            i = nw[0]
            nw[0] += 1
            rec = dict(kind="w", src=rows(a["w_ada_2"][0], j * 512, 512), slot=i % NW, i=i, kc=KC, n=512, p=P, done=None)
            loads.append(rec)
            ada_order.append(j)
            ada_at[j] = (i % NW, 16 * (i // NW + 1), rec)

        def ada_sum(j):
            slot, _, rec = ada_at[j]
            pe.wait_ge(sem("ada_part"), ada_order.index(j) + 1)
            o = open_(f"ada{j}")
            close(mm(o[:, :], ones[:, :], ring[:, slot, (KC - 1) * 512:KC * 512]), f"ada{j}")
            last_use(rec, f"ada{j}")

        def aux(dst, src, key, after=None):
            loads.append(dict(kind="aux", dst=dst, src=src, sem=sem(key), after=after))

        def rows(w, c0, n):
            return w[:, c0:c0 + n].rearrange("(k p) n -> p k n", p=P)

        def featT(name, w, src, cols, kc, rhs=None, m=P):
            o = open_(name)
            for k in range(kc):
                l = w[:, k, cols] if isinstance(cols, slice) else cols(k)
                ins = mm(o[0:m, 0:T], l, src[:, k, :], k == 0, k == kc - 1)
            close(ins, name)

        def tok(name, src, w, tb, n, kc, wk=0, cols=slice(None)):
            o = open_(name)
            for k in range(kc):
                ins = mm(o[:, 0:n], src[:, k, tb * P:(tb + 1) * P], w[:, k, cols], k == 0, k == kc - 1)
            close(ins, name)

        def transposes(name, src, dst_chunks, tbs, ready, base):
            for tb in tbs:
                pe.wait_ge(ready, base + tb + 1)
                for g0 in range(0, dst_chunks, 4):
                    g1 = min(g0 + 4, dst_chunks)
                    nm = f"{name}_{tb}_{g0 // 4}"
                    o = open_(nm)
                    for k in range(g0, g1):
                        ins = nc.tensor.transpose(o[:, (k - g0) * P:(k - g0 + 1) * P],
                                                  src[:, tb, k * P:(k + 1) * P], ident[:, :])
                    close(ins, nm)

        def await_T(name, chunks=KC):
            for tb in range(TB):
                for g in range(-(-chunks // 4)):
                    moved(pe, f"{name}_{tb}_{g}")

        def out_proj(name, srcT, w_dram, ada=()):
            for half in range(2):
                w, rec = take(rows(w_dram, half * 512, 512), KC, 512)
                if half == 1:
                    for j in ada:
                        ada_load(j)
                for tb in range(TB):
                    tok(f"{name}_{tb}_{half}", srcT, w, tb, 512, KC)
                last_use(rec, f"{name}_{TB - 1}_{half}")
            for j in ada:
                ada_sum(j)

        pe.wait_ge(sem("consts"), 1)

        pe.wait_ge(sem("xT_loaded"), 16)
        win = a["a_w_in"][0]
        w, rec = take(rows(win, A_G, 2 * H), KC, 2 * H)
        featT("gi", w, xT, slice(0, H), KC, m=H)
        featT("gf", w, xT, slice(H, 2 * H), KC, m=H)
        last_use(rec, "gf")
        for nm, c0 in (("q", 0), ("k", H * QK)):
            w, rec = take(rows(win, c0, 512), KC, 512)
            ada_load(ADA_COLS[nm == "k"])
            for ch in range(4):
                featT(f"{nm}{ch}", w, xT, slice(ch * P, (ch + 1) * P), KC)
            last_use(rec, f"{nm}3")
        pe.wait_ge(sem("gates"), 1)
        o = open_("acol")
        for tb in range(TB):
            nc.tensor.transpose(o[:, tb * H:tb * H + H], A["a"][:, tb * P:(tb + 1) * P], ident[0:H, 0:H])
            ins = nc.tensor.transpose(o[:, 16 + tb * H:16 + tb * H + H], A["m"][:, tb * P:(tb + 1) * P],
                                      ident[0:H, 0:H])
        close(ins, "acol")
        for j in range(4):
            o = open_(f"nb{j}")
            for e in range(2):
                ins = mm(o[:, e * T:(e + 1) * T], A["sel"][:, 2 * j + e, :], A["nM"][:, :])
            close(ins, f"nb{j}")
        for half in range(2):
            ada_sum(ADA_COLS[half])
            w, rec = take(rows(win, A_V + half * 512, 512), KC, 512)
            ada_load(ADA_COLS[2 + half])
            for tb in range(TB):
                tok(f"v_{tb}_{half}", xT, w, tb, 512, KC)
            last_use(rec, f"v_1_{half}")
        ada_sum(ADA_COLS[2])

        def mS(h):
            r = slice((h % 2) * 64, (h % 2) * 64 + 64)
            if h % 2 == 0:
                moved(pe, f"q{h // 2}")
                moved(pe, f"k{h // 2}")
            o = open_(f"mS{h}")
            mm(o[:, 0:T], A["kT"][r, h // 2, 0:P], A["qT"][r, h // 2, :])
            close(mm(o[:, T:384], A["kT"][r, h // 2, P:T], A["qT"][r, h // 2, P:T]), f"mS{h}")

        def mO(h):
            moved(pe, f"mS{h}")
            o = open_(f"mO{h}")
            pm = A["Pm"][:, h % 2, :]
            mm(o[:, 0:129], pm[:, 0:P], A["v"][:, 0, h, :])
            mm(o[:, 129:258], pm[:, P:T], A["v"][:, 0, h, :], True, False)
            close(mm(o[:, 129:258], pm[:, T:384], A["v"][:, 1, h, :], False, True), f"mO{h}")

        mS(0)
        mS(1)
        for tb in range(TB):
            for half in range(2):
                moved(pe, f"v_{tb}_{half}")
        pe.wait_ge(sem("v_ones"), 1)
        for h in range(H):
            mO(h)
            if h + 2 < H:
                mS(h + 2)
            if h < 4:
                half, tb = h // TB, h % TB
                if tb == 0:
                    w, rec = take(rows(win, A_O + half * 512, 512), KC, 512)
                tok(f"og_{tb}_{half}", xT, w, tb, 512, KC)
                if tb == TB - 1:
                    last_use(rec, f"og_{tb}_{half}")
            if h == 4:
                ada_sum(ADA_COLS[3])
        transposes("hT", A["h"].rearrange("p a b c -> p a (b c)"), KC, range(TB), sem("h_ready"), 0)
        await_T("hT")
        aux(lnp[:, :, :], a["lnp"][0, 0], "lnp")
        out_proj("mix0", A["hT"], a["a_w_out"][0], ADA_COLS[4:6])

        def peer(l, xv):
            transposes(f"xT{xv}", xt, KC, range(TB), sem("x_ready"), TB * (xv - 1))
            await_T(f"xT{xv}")

            def scores(tb, j):
                if tb == 0:
                    for e in range(4):
                        moved(pe, f"pq{l}_{j * 4 + e}")
                nm = f"sc{l}_{tb}_{j}"
                o = open_(nm)
                for e in range(4):
                    ch = j * 4 + e
                    ins = mm(o[:, e * P:(e + 1) * P], pq[:, ch, tb * P:(tb + 1) * P], wk[:, 0, ch * P:(ch + 1) * P])
                close(ins, nm)

            for j in range(4):
                w, rec = take(rows(a["peer_w_q"][l], j * 512, 512), KC, 512)
                for e in range(4):
                    featT(f"pq{l}_{j * 4 + e}", w, xT, slice(e * P, (e + 1) * P), KC)
                last_use(rec, f"pq{l}_{j * 4 + 3}")
                if j == 0:
                    wk, rk = take(a["keysT"][l].unsqueeze(1), 1, 2048)
                scores(0, j)
            for j in range(4):
                scores(1, j)
            last_use(rk, f"sc{l}_1_3")
            aux(lnp[:, :, :], a["lnp"][l, 1], "lnp", (sem("x_ready"), TB * xv))
            for tb in range(TB):
                r = l * TB + tb
                nm = [f"pe{l}_{tb}_{half}" for half in range(2)]
                o = [open_(x) for x in nm]
                if r == 0:
                    pe.sem_inc(sem("row_free"), SLOTS)

                def body(it, first=False):
                    for s in range(SLOTS):
                        pe.wait_ge(sem("diag"), r * PAIRS + it * SLOTS + s + 1)
                        for half in range(2):
                            ins = mm(o[half][:, :], diag[:, s, :],
                                     gath[:, s, D + half * 512:D + half * 512 + 512],
                                     first and s == 0, False)
                        ins.then_inc(sem("row_free"), 1)

                body(0, True)
                with pe.Fori(1, ITERS) as it:
                    body(it)
                for half in range(2):
                    close(mm(o[half][:, :], identa[:, :], xt[:, tb, half * 512:half * 512 + 512], False, True),
                          nm[half])

        def ple(l, xv):
            transposes(f"xT{xv}", xt, KC, range(TB), sem("x_ready"), TB * (xv - 1))
            pT, rp = take(a["pT"][l].rearrange("(k p) t -> p k t", p=P), 2, T)
            wp, rw = take(rows(a["ple_w_proj"][l], 0, D), 2, D)
            await_T(f"xT{xv}")
            for half in range(2):
                w, rec = take(rows(a["ple_w_gate"][l], half * 512, 512), KC, 512)
                for tb in range(TB):
                    tok(f"pg{l}_{tb}_{half}", xT, w, tb, 512, KC)
                    tok(f"pp{l}_{tb}_{half}", pT, wp, tb, 512, 2, cols=slice(half * 512, half * 512 + 512))
                last_use(rec, f"pg{l}_1_{half}")
            last_use(rp, f"pp{l}_1_1")
            last_use(rw, f"pp{l}_1_1")

        peer(0, 1)
        ple(0, 2)

        transposes("xT3", xt, KC, range(TB), sem("x_ready"), TB * 2)
        await_T("xT3")
        wd, rec = take(rows(a["kv_w_down_r"], 0, 512), KC, 512)
        for tb in range(TB):
            tok(f"ckv_{tb}", xT, wd, tb, KV_RANK, KC, cols=slice(0, KV_RANK))
        for e in range(2):
            featT(f"kr{e}", wd, xT, slice(KV_RANK + e * P, KV_RANK + (e + 1) * P), KC)
        last_use(rec, "kr1")
        wq, rec = take(rows(a["b_w_dq"][0], 0, Q_RANK), KC, Q_RANK)
        for tb in range(TB):
            tok(f"cq_{tb}", xT, wq, tb, Q_RANK, KC)
        last_use(rec, "cq_1")
        for tb in range(TB):
            pe.wait_ge(sem("ckv_ready"), tb + 1)
            o = open_(f"ckvT_{tb}_0")
            for k in range(2):
                ins = nc.tensor.transpose(o[:, k * P:(k + 1) * P], (M["ckv"] if tb == 0 else M["ckv2"])[:, k * P:(k + 1) * P], ident[:, :])
            close(ins, f"ckvT_{tb}_0")
        transposes("cqT", M["cq"], 3, range(TB), sem("cq_ready"), 0)
        await_T("ckvT", 2)
        wu, rec = take(rows(a["kv_w_up"], 0, 2048), 2, 2048)
        for h in range(H):
            featT(f"kn{h}", wu, M["ckvT"], slice(h * 256, h * 256 + 128), 2)
        wv = ring[:, rec["slot"], 0:4096].rearrange("p (k h e n) -> p k h e n", k=2, h=H, e=2)
        for half in range(2):
            for tb in range(TB):
                nm = f"kvv_{tb}_{half}"
                o = open_(nm)
                for k in range(2):
                    ins = mm(o[:, :], M["ckvT"][:, k, tb * P:(tb + 1) * P], wv[:, k, half * 4:half * 4 + 4, 1, :],
                             k == 0, k == 1)
                close(ins, nm)
        last_use(rec, "kvv_1_1")
        await_T("cqT", 3)
        for half in range(2):
            w, rec = take(rows(a["b_w_uq_p"], half * 768, 768), 3, 768)
            for j in range(4):
                featT(f"qn{half * 4 + j}", w, M["cqT"], slice(j * P, (j + 1) * P), 3)
            for e in range(2):
                featT(f"qr{half}_{e}", w, M["cqT"], slice((4 + e) * P, (5 + e) * P), 3)
            last_use(rec, f"qr{half}_1")

        def attn_T(nm, E):
            o = open_(nm)
            for j in range(3):
                ins = nc.tensor.transpose(o[:, j * P:(j + 1) * P], E[:, j * P:(j + 1) * P], ident[:, :])
            close(ins, nm)

        def lS(h):
            if h == 0:
                for e in range(H):
                    moved(pe, f"kn{e}")
                    moved(pe, f"qn{e}")
            if h % 4 == 0:
                pe.wait_ge(sem("rope"), 2 + h // 4)
            o = open_(f"lS{h}")
            for tb in range(TB):
                c0, n = tb * P, (tb + 1) * P
                ts = slice(tb * P, (tb + 1) * P)
                mm(o[:, c0:c0 + n], M["qnT"][:, h, ts], M["knT"][:, h, 0:n], True, False)
                for e in range(2):
                    ins = mm(o[:, c0:c0 + n], M["R"][:, h // 4, e, ts], M["krm"][:, h % 4, e, 0:n], False, e == 1)
            close(ins, f"lS{h}")

        def lO(h):
            moved(pe, f"lT{h}")
            if h == 0:
                for tb in range(TB):
                    for half in range(2):
                        moved(pe, f"kvv_{tb}_{half}")
            o = open_(f"lO{h}")
            pt = M["PT"][:, h % 4, :]
            mm(o[:, 0:T], M["v"][:, 0, h * P:(h + 1) * P], pt[:, 0:T], True, False)
            close(mm(o[:, P:T], M["v"][:, 1, h * P:(h + 1) * P], pt[:, T:384], False, True), f"lO{h}")

        lS(0)
        lS(1)
        for h in range(H):
            if h + 2 < H:
                lS(h + 2)
            pe.wait_ge(sem("probs"), h + 1)
            attn_T(f"lT{h}", M["E"][:, h % 3, :])
            if h:
                lO(h - 1)
        lO(H - 1)
        for h in range(H):
            moved(pe, f"lO{h}")
        aux(lnp[:, :, :], a["lnp"][1, 0], "lnp", (sem("x_ready"), TB * 2))
        out_proj("mix1", M["oT"], a["b_w_out"][0], ADA_COLS[6:8])
        peer(1, 4)
        ple(1, 5)

        transposes("xT6", yt, KC, range(TB), sem("xn_ready"), 0)
        await_T("xT6")
        w_in = a["w_in_2r"]
        w, rec = take(rows(w_in, 0, 512), KC, 512)
        for ch in range(4):
            featT(f"nq{ch}", w, xT, slice(ch * P, (ch + 1) * P), KC)
        last_use(rec, "nq3")
        ada_load(ADA_GATES[0])
        w, rec = take(rows(w_in, 512, 512), KC, 512)
        wB = w
        for kv in range(2):
            o = open_(f"cmp{kv}")
            for g in range(2):
                for k in range(KC):
                    ins = mm(o[0:HD, g * T:(g + 1) * T], wB[:, k, kv * P + g * HD:kv * P + (g + 1) * HD], xT[:, k, :],
                             k == 0, k == KC - 1)
            close(ins, f"cmp{kv}")

        for g in range(2):
            featT(f"ks{g}", w, xT, slice(256 + g * P, 256 + (g + 1) * P), KC)
        last_use(rec, "ks1")
        ada_load(ADA_GATES[1])
        ada_sum(ADA_GATES[0])
        w, rec = take(rows(w_in, 1024, 384), KC, 384)
        for g in range(2):
            featT(f"kw{g}", w, xT, slice(g * P, (g + 1) * P), KC)
        for tb in range(TB):
            tok(f"vs{tb}", xT, w, tb, P, KC, cols=slice(2 * P, 3 * P))
        last_use(rec, "vs1")
        ada_sum(ADA_GATES[1])
        w, rec = take(rows(w_in, 1408, 152), KC, 152)
        for tb in range(TB):
            tok(f"vw{tb}", xT, w, tb, 152, KC)
        last_use(rec, "vw1")
        for kv in range(2):
            w, rec = take(a[f"cmp_w1_{'kv'[kv]}_2"][0].rearrange("(l d) m -> d l m", d=HD), 32, P, p=HD)
            if kv == 0:
                pe.wait_ge(sem("ckin_ready"), 1)
            else:
                pe.wait_ge(sem("ckin_ready"), 2)
            nm = f"ch{kv}"
            o = open_(nm)
            for l in range(32):
                ins = mm(o[:, 0:2 * CW], w[:, l, :], ckin[:, 2 * kv:2 * kv + 2, l, :], l == 0, l == 31)
            close(ins, nm)
            last_use(rec, nm)
        moved(pe, "ch0")
        moved(pe, "ch1")
        o = open_("kc")
        close(mm(o[:, 0:2 * CW], N["w2"][:, 0:2, :].rearrange("p a b -> p (a b)"),
                 N["hid"].rearrange("p g n -> p (g n)")), "kc")
        o = open_("vc")
        close(mm(o[:, 0:HD], N["hidv"].rearrange("p g r n -> p (g r n)"), N["w2"][:, 2, :]), "vc")
        moved(pe, "kc")
        for ch in range(4):
            moved(pe, f"nq{ch}")
        for e in range(2):
            o = open_(f"cS{e}")
            r = slice(e * 64, e * 64 + 64)
            for tb in range(TB):
                for i in range(4):
                    ins = mm(o[:, (tb * 4 + i) * CW:(tb * 4 + i + 1) * CW], N["qT"][r, i, tb * P:(tb + 1) * P],
                             N["kc"][r, i // 2, :])
            close(ins, f"cS{e}")

        for nm, c0 in (("bq", 1560), ("bk", 2072)):
            w, rec = take(rows(w_in, c0, 512), KC, 512)
            ada_load(ADA_GATES[2 + (nm == "bk")])
            for ch in range(4):
                featT(f"{nm}{ch}", w, xT, slice(ch * P, (ch + 1) * P), KC)
            last_use(rec, f"{nm}3")
        w, rec = take(rows(w_in, 2584, 512), KC, 512)
        for tb in range(TB):
            tok(f"bv{tb}", xT, w, tb, 512, KC)
            ada_sum(ADA_GATES[2 + tb])
        last_use(rec, "bv1")
        pe.wait_ge(sem("cprobs"), 1)
        o = open_("cT")
        for tb in range(TB):
            ins = nc.tensor.transpose(o[:, tb * P:(tb + 1) * P],
                                      N["cE"][:, tb, :, :].rearrange("p h n -> p (h n)"), ident[:, :])
        close(ins, "cT")

        for nm in ("ks0", "ks1", "kw0", "kw1", "vs0", "vs1", "vw0", "vw1", "vc", "cT"):
            moved(pe, nm)

        def nS(i):
            h, win_ = i // 2, i % 2
            kT = N["kwT"] if win_ else N["ksT"]
            r = slice((h % 2) * 64, (h % 2) * 64 + 64)
            o = open_(f"nS{i}")
            for tb in range(TB):
                ins = mm(o[:, tb * P:tb * P + (tb + 1) * P], N["qT"][r, h // 2, tb * P:(tb + 1) * P],
                         kT[r, h // 4, 0:(tb + 1) * P])
            close(ins, f"nS{i}")

        def nO(h):
            moved(pe, f"nT{2 * h}")
            moved(pe, f"nT{2 * h + 1}")
            o = open_(f"nO{h}")
            g = h // 4
            r = slice((h % 2) * 64, (h % 2) * 64 + 64)
            mm(o[r, 0:T], N["vcm"][:, h, :], N["cPT"], True, False)
            for j in range(2):
                vv = (N["vw"] if j else N["vs"])
                pt = N["PT"][:, (2 * h + j) % 4, :]
                mm(o[r, 0:T], vv[:, 0, g * HD:(g + 1) * HD], pt[:, 0:T], False, False)
                ins = mm(o[r, P:T], vv[:, 1, g * HD:(g + 1) * HD], pt[:, T:384], False, j == 1)
            close(ins, f"nO{h}")

        for ch in range(4):
            moved(pe, f"bq{ch}")
            moved(pe, f"bk{ch}")
        for tb in range(TB):
            moved(pe, f"bv{tb}")

        def bS(h):
            r = slice((h % 2) * 64, (h % 2) * 64 + 64)
            o = open_(f"bS{h}")
            mm(o[:, 0:T], N["kbT"][r, h // 2, 0:P], N["qbT"][r, h // 2, :])
            close(mm(o[:, T:384], N["kbT"][r, h // 2, P:T], N["qbT"][r, h // 2, P:T]), f"bS{h}")

        def bL(h):
            pe.wait_ge(sem("keep"), h + 1)
            lk = sbk[:, 2 + h % 2, :]
            o = open_(f"bL{h}")
            mm(o[:, 0:T], upper[:, :], lk[:, 0:T], True, False)
            mm(o[:, P:T], ones[:, :], lk[:, T:384], False, True)
            close(mm(o[:, T:384], upper[:, :], lk[:, T:384]), f"bL{h}")

        def bO(h):
            pe.wait_ge(sem("broken"), h + 1)
            pt = sbp[:, h % 2, :]
            o = open_(f"bO{h}")
            r = slice((h % 2) * 64, (h % 2) * 64 + 64)
            v = [N["vb"][:, b, h * HD:(h + 1) * HD] for b in range(2)]
            mm(o[r, 0:T], v[0], pt[:, 0:T], True, False)
            close(mm(o[r, P:T], v[1], pt[:, T:384], False, True), f"bO{h}")

        gate_w = [None]

        def mg(ch):
            if ch % 4 == 0:
                gate_w[0] = take(rows(w_in, 3096 + ch // 4 * 512, 512), KC, 512)
            w, rec = gate_w[0]
            e = ch % 4
            featT(f"mg{ch}", w, xT, slice(e * P, (e + 1) * P), KC)
            if e == 3:
                last_use(rec, f"mg{ch}")

        nS(0)
        nS(1)
        bS(0)
        for h in range(H):
            i = 2 * h
            if h + 1 < H:
                nS(i + 2)
                bS(h + 1)
            mg(i)
            pe.wait_ge(sem("nprobs"), i + 1)
            attn_T(f"nT{i}", N["E"][:, i % 3, :])
            if h:
                nO(h - 1)
            if h + 1 < H:
                nS(i + 3)
            bL(h)
            mg(i + 1)
            pe.wait_ge(sem("nprobs"), i + 2)
            attn_T(f"nT{i + 1}", N["E"][:, (i + 1) % 3, :])
            if h:
                bO(h - 1)
        nO(H - 1)
        bO(H - 1)

        wa, ra = take(rows(a["w_proj_a_2"][0], 0, D), 4, D)
        wb, rb = take(rows(a["w_proj_b_2"][0], 0, D), 4, D)
        for h in range(H):
            moved(pe, f"nO{h}")
            moved(pe, f"bO{h}")
        for ch in range(KC):
            featT(f"ya{ch}", wa, N["oaT"], slice(ch * P, (ch + 1) * P), 4)
            featT(f"yb{ch}", wb, N["obT"], slice(ch * P, (ch + 1) * P), 4)
        last_use(ra, f"ya{KC - 1}")
        last_use(rb, f"yb{KC - 1}")
        pe.wait_ge(sem("yT"), KC)
        out_proj("mix2", xT, a["w_out_2"][0])

        transposes("xT7", yt, KC, range(TB), sem("xn_ready"), TB)
        await_T("xT7")
        for j in range(0, FF, 512):
            n = min(512, FF - j)
            wg, r1 = take(rows(a["w_ffn_gate_2"][0], j, n), KC, n)
            wu_, r2 = take(rows(a["w_ffn_up_2"][0], j, n), KC, n)
            for e in range(n // P):
                ch = j // P + e
                featT(f"fg{ch}", wg, xT, slice(e * P, (e + 1) * P), KC)
                featT(f"fu{ch}", wu_, xT, slice(e * P, (e + 1) * P), KC)
            last_use(r1, f"fg{ch}")
            last_use(r2, f"fu{ch}")
        aux(lnp[:, 0, :], a["nfg"], "lnp", (sem("x_ready"), TB * 6))
        pe.wait_ge(sem("hid"), FC)
        names = [(tb, half) for tb in range(TB) for half in range(2)]
        o = {x: open_(f"dn_{x[0]}_{x[1]}") for x in names}
        for j in range(0, FC, 4):
            n = min(4, FC - j)
            w, rec = take(a["w_ffn_down_2"][0][j * P:(j + n) * P, :].rearrange("(k p) n -> p k n", p=P), n, D)
            for x in names:
                for k in range(n):
                    ins = mm(o[x][:, :], F["hid"][:, j + k, x[0] * P:(x[0] + 1) * P],
                             w[:, k, x[1] * 512:x[1] * 512 + 512], j + k == 0, j + k == FC - 1)
                if j + n == FC:
                    close(ins, f"dn_{x[0]}_{x[1]}")
            if j + n < FC:
                ins.then_inc(sem("down_used"), 1)
                rec["done"] = (sem("down_used"), j // 4 + 1)

    @block.sync
    def _(sp):
        sp.dma_start(xT[:, :, :], a["xTin"].rearrange("(k p) t -> p k t", p=P)).then_inc(sem("xT_loaded"), 16)
        first = True
        done_of = {}
        for r in loads:
            if r["kind"] == "w":
                if r["i"] >= NW:
                    s, v = done_of[r["i"] - NW]
                    sp.wait_ge(s, v)
                dst = ring[0:r["p"], r["slot"], 0:r["kc"] * r["n"]].rearrange("p (k n) -> p k n", k=r["kc"])
                sp.dma_start(dst, r["src"]).then_inc(slot_loaded[r["slot"]], 16)
                done_of[r["i"]] = r["done"]
            else:
                if r["after"]:
                    sp.wait_ge(*r["after"])
                sp.dma_start(r["dst"], r["src"]).then_inc(r["sem"], 16)
        for tb in range(TB):
            sp.wait_ge(sem("out_ready"), tb + 1)
            sp.dma_start(out[tb * P:(tb + 1) * P, :], yt[:, tb, :]).then_inc(sem("out_done"), 16)
        sp.wait_ge(sem("out_done"), 16 * TB)

    @block.gpsimd
    def _(pool):
        step = Steps(pool, "pool_step")
        pool.dma_start(cT[:, :], a["cT"]).then_inc(sem("c_loaded"), 16)
        for dst, src in ((xt[:, :, :], a["x"].rearrange("(b p) d -> p b d", p=P)),
                         (A["bif"][:, :], a["bif"]), (A["g"][:, :], a["hng"]),
                         (posi[:, :], a["pos"]), (invf[:, :], a["invf"])):
            pool.dma_start(dst, src).then_inc(sem("small"), 16)
        for t, v in ((ident, 0.0), (ones, 1.0), (upper, 1.0), (maskT, 0.0), (maskS, 0.0), (keep, 1.0), (maskQ, 0.0)):
            step.go(pool.memset(t[:, :], v))
        step.go(pool.memset(A["sel"], 0.0))
        step.wait()

        def select(v, pattern, base, op, fill, ch):
            step.go(pool.affine_select(out=v, in_=v, compare_op=op, fill=fill, base=base, pattern=pattern,
                                       channel_multiplier=ch))
        select(ident[:, :], [[-1, P]], 0, ALU.not_equal, 1.0, 1)
        select(upper[:, :], [[-1, P]], 0, ALU.is_gt, 0.0, 1)
        for c0 in (0, T):
            select(maskT[:, c0:c0 + P], [[1, P]], 0, ALU.is_ge, NEG, -1)
            select(maskS[:, c0:c0 + P], [[1, P]], 0, ALU.is_gt, NEG, -1)
            select(keep[:, c0:c0 + P], [[1, P]], 0, ALU.is_gt, 0.0, -1)
            select(maskQ[:, c0:c0 + P], [[-1, P]], 0, ALU.is_ge, NEG, 1)
        select(A["sel"], [[-1, H], [0, P]], 0, ALU.not_equal, 1.0, 1)
        step.go(pool.iota(iota16[:, :], [[1, 16]], base=0, channel_multiplier=0,
                          allow_small_or_imprecise_dtypes=True))
        step.wait()
        pool.tensor_scalar(identa[:, :], ident[:, :], ALPHA, None, ALU.mult).then_inc(sem("consts"), 1)

        def gathers(l, tb):
            r = l * TB + tb
            for u in range(UNITS):
                pool.wait_ge(sem("experts"), r * UNITS + u + 1)
                with pool.Fori(u * UITERS, (u + 1) * UITERS) as it:
                    gather_turn(l, tb, it)

        def gather_turn(l, tb, it):
                r = l * TB + tb
                for g in range(NG):
                    pool.wait_ge(sem("row_free"), r * PAIRS + it * SLOTS + (g + 1) * GRP)
                    pool.sem_inc(sem("gather_go"), 1)
                    pool.tensor_copy(idc[:, g * GRP:(g + 1) * GRP],
                                     eidx[:, tb, bass.ds(it * SLOTS + g * GRP, GRP)]).then_inc(sem("idc_set"), 1)
                    pool.wait_ge(sem("idc_set"), (r * ITERS + it) * NG + g + 1)
                    pool.sem_inc(sem("gather_go"), 1)
                    for s in range(g * GRP, (g + 1) * GRP):
                        pool.indirect_dma_start(gath[:, s, :], None, a["uv"],
                                                bass.IndirectOffsetOnAxis(ap=idc[:, s:s + 1], axis=0)
                                                ).then_inc(sem(f"row{s}"), 16)

        for tb in range(TB):
            gathers(0, tb)
        pool.wait_ge(sem("x_ready"), TB * 3)
        pool.dma_start(M["cg"], a["kvg"]).then_inc(sem("mla_par"), 16)
        pool.dma_start(M["qg"], a["qng"]).then_inc(sem("mla_par"), 16)
        for tb in range(TB):
            gathers(1, tb)
        pool.wait_ge(sem("x_ready"), TB * 5)
        for dst, src in ((N["bada"], a["badaT"]), (N["ng"], a["ngT"]),
                         (N["posc"], a["posc"]), (N["w2"], a["cmp_w2"]), (N["g1"], a["bg1"]), (N["g2"], a["bg2"])):
            pool.dma_start(dst, src).then_inc(sem("hyb_par"), 16)
        step.go(pool.iota(N["dist"][:, 0:P], [[-1, P]], base=0, channel_multiplier=1,
                          allow_small_or_imprecise_dtypes=True))
        step.go(pool.iota(N["dist"][:, P:384], [[-1, T]], base=P, channel_multiplier=1,
                          allow_small_or_imprecise_dtypes=True))
        for tb in range(TB):
            step.go(pool.iota(N["cdist"][:, tb, :], [[-16, CW]], base=P * tb - 31, channel_multiplier=1,
                              allow_small_or_imprecise_dtypes=True))
        step.go(pool.memset(ckin[:, :, :, :], 0.0))
        step.go(pool.memset(N["m8"], 1.0))
        step.go(pool.memset(N["rv"], 1.0))
        step.wait()
        select(N["dist"][:, 0:P], [[-1, P]], 0, ALU.is_ge, FAR, 1)
        select(N["dist"][:, T:384], [[-1, P]], 0, ALU.is_ge, FAR, 1)
        for tb in range(TB):
            select(N["cdist"][:, tb, :], [[-16, CW]], P * tb - 31, ALU.is_ge, FAR, 1)
        select(N["m8"], [[-16, 8]], 0, ALU.is_ge, 0.0, 1)
        select(N["rv"][:, 0:1], [[0, 1]], -31, ALU.is_ge, 0.0, 1)
        step.wait()
        select(N["m8"], [[16, 8]], 15, ALU.is_ge, 0.0, -1)
        select(N["cdist"][:, 1, CW - 1:CW], [[0, 1]], -1, ALU.is_ge, FAR, 0)
        step.wait()
        for tb in range(TB):
            for h in range(H):
                step.go(pool.tensor_scalar(N["cb"][:, tb, h, :], N["cdist"][:, tb, :], -SLOPES[h], None, ALU.mult))
        step.wait()
        pool.engine_nop().then_inc(sem("hyb_const"), 1)
        for h in range(H):
            if h >= 2:
                pool.wait_ge(sem("bias_used"), h - 1)
            pool.tensor_scalar(N["bh"][:, h % 2, :], N["dist"], -SLOPES[h], None, ALU.mult
                               ).then_inc(sem("bias_ready"), 1)

    @block.scalar
    def _(act):
        step = Steps(act, "act_step")
        nsq = [0]

        def f(o, i, fn, **kw):
            return nc.scalar.activation(o, i, fn, **kw)

        def evac(name, dst, src=None, fn=ACT.Copy, **kw):
            ps = full(act, name)
            free(f(dst, ps[:, 0:T] if src is None else src(ps), fn, **kw), name)

        def sqrt(cols):
            nsq[0] += 1
            act.wait_ge(sem("var_ready"), nsq[0])
            f(sdv[:, 0:cols], var[:, 0:cols], ACT.Sqrt).then_inc(sem("sd_ready"), 1)

        def evac_T(name, dst, chunks=KC):
            for tb in range(TB):
                for g in range(-(-chunks // 4)):
                    n = min(4, chunks - 4 * g)
                    evac(f"{name}_{tb}_{g}", dst[:, 4 * g:4 * g + n, tb * P:(tb + 1) * P],
                         lambda ps, n=n: ps[:, 0:n * P].rearrange("p (k t) -> p k t", k=n))

        act.wait_ge(sem("c_loaded"), 16)
        f(scT[:, :], cT[:, :], ACT.Silu).then_inc(sem("silu_c"), 1)
        act.wait_ge(sem("abs_ready"), 1)
        step(f(A["ex"], A["ax"], ACT.Exp, scale=-1.0))
        f(A["lf"], A["ex"], ACT.Ln, bias=1.0).then_inc(sem("log1p"), 1)
        for ch in range(4):
            evac(f"q{ch}", A["qT"][:, ch, :])
        for ch in range(4):
            evac(f"k{ch}", A["kT"][:, ch, :], scale=QK ** -0.5)
        ps = full(act, "acol")
        step.go(f(A["acol"].rearrange("p b h -> p (b h)"), ps[:, 0:16], ACT.Copy))
        free(f(A["enm"].rearrange("p b h -> p (b h)"), ps[:, 16:32], ACT.Exp, scale=-1.0), "acol")
        for half in range(2):
            for tb in range(TB):
                evac(f"v_{tb}_{half}", A["v"][:, tb, half * 4:half * 4 + 4, 0:128],
                     lambda ps: ps[:, :].rearrange("p (h n) -> p h n", h=4))
        for h in range(H):
            act.wait_ge(sem("m_arg"), h + 1)
            f(A["tm"][:, h % 2, :], A["tm"][:, h % 2, :], ACT.Exp).then_inc(sem("m_exp"), 1)
            if 1 <= h <= 4:
                half, tb = (h - 1) // TB, (h - 1) % TB
                evac(f"og_{tb}_{half}", A["og"][:, tb, half * 512:half * 512 + 512], lambda ps: ps[:, :])
        for half in range(2):
            moved(act, f"og_1_{half}")
            moved(act, f"og_0_{half}")
        f(A["og"], A["og"], ACT.Sigmoid).then_inc(sem("og_ready"), 1)
        sqrt(16)
        evac_T("hT", A["hT"])
        for tb in range(TB):
            sqrt(1)

        def peer(l, xv):
            evac_T(f"xT{xv}", xT)

            def scores(tb, j):
                evac(f"sc{l}_{tb}_{j}", sc[:, tb, j * 4:j * 4 + 4, :],
                     lambda ps: ps[:, :].rearrange("p (c n) -> p c n", c=4))

            def gate_exp(n):
                act.wait_ge(sem("gate_arg"), l * TB * UNITS + n + 1)
                f(tsv[:, :, :], tsv[:, :, :], ACT.Exp).then_inc(sem("gate_exp"), 1)

            def gelus(tb, it):
                for g in range(NG):
                    act.wait_ge(sem("dots"), (l * TB + tb) * PAIRS + it * SLOTS + (g + 1) * GRP)
                    f(glu[:, g * GRP:(g + 1) * GRP], dots[:, g * GRP:(g + 1) * GRP], ACT.Gelu
                      ).then_inc(sem("gelu"), 1)

            for j in range(4):
                for e in range(4):
                    evac(f"pq{l}_{j * 4 + e}", pq[:, j * 4 + e, :])
                scores(0, j)
                if j == 1:
                    gate_exp(0)
            gate_exp(1)
            for j in range(4):
                scores(1, j)
            gelus(0, 0)
            for n in range(2, TB * UNITS):
                for it in range(1 + SPREAD * (n - 2), 1 + SPREAD * (n - 1)):
                    gelus(0, it)
                gate_exp(n)
            with act.Fori(WOVEN, ITERS) as it:
                gelus(0, it)
            sqrt(1)
            with act.Fori(0, ITERS) as it:
                gelus(1, it)
            sqrt(1)

        def ple(l, xv):
            evac_T(f"xT{xv}", xT)
            for half in range(2):
                for tb in range(TB):
                    evac(f"pg{l}_{tb}_{half}", yt[:, tb, half * 512:half * 512 + 512], lambda ps: ps[:, :],
                         fn=ACT.Sigmoid)

        peer(0, 1)
        ple(0, 2)

        evac_T("xT3", xT)
        act.wait_ge(sem("ang_ready"), 1)
        f(M["sin"], M["w1"], ACT.Sin).then_inc(sem("trig"), 1)
        f(M["cos"], M["w2"], ACT.Sin).then_inc(sem("trig"), 1)
        for tb in range(TB):
            evac(f"ckv_{tb}", yt[:, tb, 0:KV_RANK], lambda ps: ps[:, 0:KV_RANK])
        for e in range(2):
            evac(f"kr{e}", M["t"][:, e, :])
        for tb in range(TB):
            evac(f"cq_{tb}", yt[:, tb, 512:512 + Q_RANK], lambda ps: ps[:, 0:Q_RANK])
        sqrt(4)
        evac_T("ckvT", M["ckvT"], 2)
        evac_T("cqT", M["cqT"], 3)
        for h in range(H):
            evac(f"kn{h}", M["knT"][:, h, :])
        for half in range(2):
            for tb in range(TB):
                evac(f"kvv_{tb}_{half}", M["v"][:, tb, half * 512:half * 512 + 512], lambda ps: ps[:, :])
        for half in range(2):
            for j in range(4):
                evac(f"qn{half * 4 + j}", M["qnT"][:, half * 4 + j, :])

        def softmax_exp(i, E, ready, done, pool_of):
            act.wait_ge(sem(ready), i + 1)
            for tb in range(TB):
                c0 = tb * P
                c1 = c0 + (tb + 1) * P
                ins = f(E[:, i % 3, c0:c1], E[:, i % 3, c0:c1], ACT.Exp, bias=rmax[:, i % 3, tb:tb + 1],
                        accum_out=rsum[:, i % 3, tb:tb + 1])
                if tb == 0:
                    step.go(ins)
            ins.then_inc(sem(done), 1)

        def lT(h):
            if h >= 4:
                full(act, f"lO{h - 4}")
            evac(f"lT{h}", M["PT"][:, h % 4, :], lambda ps: ps[:, 0:384])

        for h in range(H):
            softmax_exp(h, M["E"], "l_max", "l_exp", None)
            if h >= 1:
                lT(h - 1)
            if h >= 2:
                evac(f"lO{h - 2}", M["oT"][:, h - 2, :])
        lT(H - 1)
        for h in (H - 2, H - 1):
            evac(f"lO{h}", M["oT"][:, h, :])
        for tb in range(TB):
            sqrt(1)
        peer(1, 4)
        ple(1, 5)

        sqrt(2)
        act.wait_ge(sem("mod_ready"), 1)

        def evac_norm(name, j):
            for tb in range(TB):
                for g in range(2):
                    ps = full(act, f"{name}_{tb}_{g}")
                    for e in range(4):
                        k = 4 * g + e
                        ins = f(xT[:, k, tb * P:(tb + 1) * P], ps[:, e * P:(e + 1) * P], ACT.Identity,
                                scale=N["gs"][:, j, k:k + 1], bias=N["mod"][:, 2 * j, k:k + 1])
                        if e < 3:
                            step.go(ins)
                    free(ins, f"{name}_{tb}_{g}")

        evac_norm("xT6", 0)
        for ch in range(4):
            evac(f"nq{ch}", N["qT"][:, ch, :])
        for kv in range(2):
            evac(f"cmp{kv}", kcv[:, 2 * kv:2 * kv + 2, :],
                 lambda ps: ps[0:HD, :].rearrange("p (g t) -> p g t", g=2))
        for g in range(2):
            evac(f"ks{g}", N["ksT"][:, g, :])
        for tb in range(TB):
            evac(f"vs{tb}", N["vs"][:, tb, :], lambda ps: ps[:, 0:P])
        for g in range(2):
            evac(f"kw{g}", N["kwT"][:, g, :])
        for tb in range(TB):
            ps = full(act, f"vw{tb}")
            step.go(f(N["vw"][:, tb, :], ps[:, 0:P], ACT.Copy))
            free(f(N["ga"][:, tb, :], ps[:, P:152], ACT.Sigmoid), f"vw{tb}")
        evac("ch0", N["hid"], lambda ps: ps[:, 0:2 * CW].rearrange("p (g n) -> p g n", g=2), fn=ACT.Gelu_apprx_tanh)
        evac("ch1", N["hidv"], lambda ps: ps[:, 0:2 * CW].rearrange("p (g n) -> p g n", g=2).unsqueeze(2)
             .broadcast_to([P, 2, 4, CW]), fn=ACT.Gelu_apprx_tanh)
        evac("kc", N["kc"], lambda ps: ps[:, 0:2 * CW].rearrange("p (g n) -> p g n", g=2))
        for ch in range(4):
            evac(f"bq{ch}", N["qbT"][:, ch, :])
        act.wait_ge(sem("c_arg"), 1)
        f(N["cE"], N["cE"], ACT.Exp).then_inc(sem("c_exp"), 1)
        for ch in range(4):
            evac(f"bk{ch}", N["kbT"][:, ch, :])
        for tb in range(TB):
            evac(f"bv{tb}", N["vb"][:, tb, :], lambda ps: ps[:, :])
        evac("cT", N["cPT"])

        def nT(i):
            if i >= 4:
                full(act, f"nO{(i - 4) // 2}")
            evac(f"nT{i}", N["PT"][:, i % 4, :], lambda ps: ps[:, 0:384])

        def nO(h):
            r = slice((h % 2) * 64, (h % 2) * 64 + 64)
            evac(f"nO{h}", N["oaT"][r, h // 2, :], lambda ps: ps[r, 0:T])

        def bo(h):
            r = slice((h % 2) * 64, (h % 2) * 64 + 64)
            evac(f"bO{h}", N["obT"][r, h // 2, :], lambda ps: ps[r, 0:T])

        def break_logs(h):
            if h:
                act.wait_ge(sem("keep"), h)
            evac(f"bS{h}", sbk[:, 0, :], lambda ps: ps[:, 0:384], scale=SCALE)
            moved(act, f"bS{h}")
            step(f(sbk[:, 1, :], sbk[:, 0, :], ACT.Abs))
            step(f(sbk[:, 1, :], sbk[:, 1, :], ACT.Exp, scale=-1.0))
            f(sbk[:, 1, :], sbk[:, 1, :], ACT.Ln, bias=1.0).then_inc(sem("b_log"), 1)

        def break_exp(h):
            act.wait_ge(sem("b_arg"), h + 1)
            f(sbp[:, h % 2, :], sbp[:, h % 2, :], ACT.Exp).then_inc(sem("broken"), 1)

        def mg(ch):
            evac(f"mg{ch}", N["sgm"][:, ch, :])

        for h in range(H):
            softmax_exp(2 * h, N["E"], "n_max", "n_exp", None)
            break_logs(h)
            if h:
                nT(2 * h - 1)
            if h >= 2:
                bo(h - 2)
            mg(2 * h)
            softmax_exp(2 * h + 1, N["E"], "n_max", "n_exp", None)
            if h:
                break_exp(h - 1)
            nT(2 * h)
            if h:
                nO(h - 1)
            mg(2 * h + 1)
        nT(2 * H - 1)
        break_exp(H - 1)
        bo(H - 2)
        nO(H - 1)
        bo(H - 1)
        for ch in range(16):
            moved(act, f"mg{ch}")
        for j in range(4):
            f(N["sgm"][:, 4 * j:4 * j + 4, :], N["sgm"][:, 4 * j:4 * j + 4, :], ACT.Sigmoid).then_inc(sem("merge_gates"), 1)
        sqrt(2)
        evac_norm("xT7", 1)
        for ch in range(FC):
            evac(f"fg{ch}", F["hid"][:, ch, :], fn=ACT.Silu)
        sqrt(2)

    @block.vector
    def _(dve):
        v = nc.vector
        step = Steps(dve, "dve_step")
        nsq = [0]
        nln = [0]

        def inverse_sd(cols):
            nsq[0] += 1
            dve.wait_ge(sem("sd_ready"), nsq[0])
            step(v.reciprocal(rstd[:, 0:cols], sdv[:, 0:cols]))

        def add_eps(cols, scale, eps):
            v.tensor_scalar(var[:, 0:cols], var[:, 0:cols], scale, eps, ALU.mult, ALU.add
                            ).then_inc(sem("var_ready"), 1)

        def layer_norm(tb, src, frees=()):
            for half in range(2):
                step.go(v.bn_stats(bnst[:, half, :], src[half]))
            step.wait()
            step(v.bn_aggr(mv[:, :], bnst[:, :, :].rearrange("p a b -> p (a b)")))
            v.tensor_scalar(var[:, 0:1], mv[:, 1:2], LN_EPS, None, ALU.add).then_inc(sem("var_ready"), 1)
            inverse_sd(1)
            for half in range(2):
                ins = v.tensor_scalar(yt[:, tb, half * 512:half * 512 + 512], src[half], mv[:, 0:1], rstd[:, 0:1],
                                      ALU.subtract, ALU.mult)
                if frees:
                    free(ins, frees[half])
                    moved(dve, frees[half])
                else:
                    step(ins)
            if tb == 0:
                nln[0] += 1
                dve.wait_ge(sem("lnp"), 16 * nln[0])
            step(v.tensor_tensor(yt[:, tb, :], yt[:, tb, :], lnp[:, 0, :], ALU.mult))
            v.tensor_tensor(xt[:, tb, :], yt[:, tb, :], lnp[:, 1, :], ALU.add).then_inc(sem("x_ready"), 1)

        def residual_norm(name):
            for tb in range(TB):
                for half in range(2):
                    cs = slice(half * 512, half * 512 + 512)
                    ps = full(dve, f"{name}_{tb}_{half}")
                    free(v.scalar_tensor_tensor(yt[:, tb, cs], xt[:, tb, cs], ALPHA, ps[:, :], ALU.mult, ALU.add),
                         f"{name}_{tb}_{half}")
                    moved(dve, f"{name}_{tb}_{half}")
                layer_norm(tb, [yt[:, tb, 0:512], yt[:, tb, 512:1024]])

        def ada_part(j):
            slot, loaded, _ = ada_at[j]
            dve.wait_ge(slot_loaded[slot], loaded)
            w = ring[:, slot, :].rearrange("p (k n) -> p k n", k=KC)
            step(v.tensor_scalar(w[:, 0, :], w[:, 0, :], scT[:, 0:1], None, ALU.mult))
            for k in range(1, KC):
                ins = v.scalar_tensor_tensor(w[:, k, :], w[:, k, :], scT[:, k:k + 1], w[:, k - 1, :], ALU.mult, ALU.add)
                if k < KC - 1:
                    step(ins)
            ins.then_inc(sem("ada_part"), 1)

        def ada_column(j):
            ps = full(dve, f"ada{j}")
            at = ADA_COLS.index(j)
            for e in range(4):
                ins = v.tensor_tensor_reduce(out=junk[:, :], in0=ps[:, e * P:(e + 1) * P], in1=ident[:, :], scale=1.0,
                                             scalar=0.0, op0=ALU.mult, op1=ALU.add,
                                             accum_out=adac[:, at // 2, (at % 2) * 4 + e:(at % 2) * 4 + e + 1])
                if e < 3:
                    step(ins)
            free(ins, f"ada{j}")
            moved(dve, f"ada{j}")

        def ada_gate(j):
            i = ADA_GATES.index(j)
            g = (N["g1"] if i < 2 else N["g2"])[:, (i % 2) * 512:(i % 2) * 512 + 512]
            ps = full(dve, f"ada{j}")
            free(v.tensor_tensor(g, ps[:, :], g, ALU.add), f"ada{j}")
            moved(dve, f"ada{j}")

        dve.wait_ge(sem("small"), 16 * 5)
        v.memset(A["v"][:, :, :, 128:129], 1.0).then_inc(sem("v_ones"), 1)
        ps = full(dve, "gi")
        free(v.tensor_scalar(A["ig"], ps[0:H, 0:T], A["bif"][:, 0:1], None, ALU.add), "gi")
        ps = full(dve, "gf")
        free(v.tensor_scalar(A["xf"], ps[0:H, 0:T], A["bif"][:, 1:2], None, ALU.add), "gf")
        moved(dve, "gi")
        moved(dve, "gf")
        step.go(v.memset(A["B"], 1.0))
        v.scalar_tensor_tensor(A["ax"], A["xf"], -1.0, A["xf"], ALU.mult, ALU.max).then_inc(sem("abs_ready"), 1)
        dve.wait_ge(sem("log1p"), 1)
        step(v.scalar_tensor_tensor(A["ex"], A["xf"], 0.0, A["lf"], ALU.min, ALU.subtract))
        step(v.tensor_tensor_scan(A["m"], A["B"], A["ex"], 0.0, ALU.mult, ALU.add))
        step(v.tensor_tensor(A["a"], A["ig"], A["m"], ALU.subtract))
        step(v.tensor_tensor_scan(A["M"], A["a"], A["a"], 0.0, ALU.max, ALU.max))
        step(v.tensor_tensor(A["m"], A["m"], A["M"], ALU.add))
        v.tensor_scalar(A["nM"], A["M"], -1.0, None, ALU.mult).then_inc(sem("gates"), 1)
        dve.wait_ge(sem("silu_c"), 1)
        ada_part(ADA_COLS[0])
        for j in range(4):
            nm = f"nb{j}"
            ps = full(dve, nm)
            for e in range(2):
                step.go(v.tensor_tensor(A["negM"][:, 2 * j + e, 0:T], ps[:, e * T:(e + 1) * T], maskT[:, 0:T], ALU.add))
                ins = v.tensor_tensor(A["negM"][:, 2 * j + e, T:384], ps[:, e * T + P:(e + 1) * T], maskT[:, T:384], ALU.add)
                if e == 0:
                    step.go(ins)
            free(ins, nm)
        moved(dve, "nb3")
        step.wait()
        moved(dve, "acol")

        def m_arg(h):
            step.go(v.tensor_scalar(A["tm"][:, h % 2, 0:T], A["negM"][:, h, 0:T], A["acol"][:, 0, h:h + 1], 0.0,
                                    ALU.add, ALU.min))
            v.tensor_scalar(A["tm"][:, h % 2, T:384], A["negM"][:, h, T:384], A["acol"][:, 1, h:h + 1], 0.0,
                            ALU.add, ALU.min).then_inc(sem("m_arg"), 1)

        def m_fin(h):
            ps = full(dve, f"mO{h}")
            o2 = ps[:, 0:258].rearrange("p (b n) -> p b n", b=2)
            d_ = A["den"][:, h % 2, :]
            r_ = A["rden"][:, h % 2, :]
            step(v.tensor_copy(d_, o2[:, :, 128]))
            step(v.scalar_tensor_tensor(d_, d_, -1.0, d_, ALU.mult, ALU.max))
            step(v.tensor_tensor(d_, d_, A["enm"][:, :, h], ALU.max))
            step(v.reciprocal(r_, d_))
            step.go(v.tensor_scalar(A["h"][:, 0, h, :], o2[:, 0, 0:128], r_[:, 0:1], None, ALU.mult))
            free(v.tensor_scalar(A["h"][:, 1, h, :], o2[:, 1, 0:128], r_[:, 1:2], None, ALU.mult), f"mO{h}")
            moved(dve, f"mO{h}")
            for tb in range(TB):
                step.go(v.bn_stats(A["st"][:, tb * H + h, :], A["h"][:, tb, h, :]))

        ada_part(ADA_COLS[1])
        ada_column(ADA_COLS[0])
        m_arg(0)
        m_arg(1)
        ada_part(ADA_COLS[2])
        ada_column(ADA_COLS[1])
        for h in range(H):
            dve.wait_ge(sem("m_exp"), h + 1)
            ps = full(dve, f"mS{h}")
            if h >= 2:
                full(dve, f"mO{h - 2}")
            free(v.tensor_tensor(A["Pm"][:, h % 2, :], A["tm"][:, h % 2, :], ps[:, 0:384], ALU.mult), f"mS{h}")
            if h + 2 < H:
                moved(dve, f"mS{h}")
                m_arg(h + 2)
            if h:
                m_fin(h - 1)
            if h == 1:
                ada_column(ADA_COLS[2])
            if h == 2:
                ada_part(ADA_COLS[3])
            if h == 5:
                ada_column(ADA_COLS[3])
        m_fin(H - 1)
        step.wait()
        st = A["st"]
        step.go(v.tensor_tensor(A["mu"], st[:, :, 1], st[:, :, 4], ALU.add))
        step.go(v.tensor_tensor(A["t1"], st[:, :, 1], st[:, :, 4], ALU.subtract))
        step.go(v.tensor_tensor(A["t2"], st[:, :, 2], st[:, :, 5], ALU.add))
        step.wait()
        step.go(v.tensor_scalar(A["mu"], A["mu"], 0.5, None, ALU.mult))
        step.go(v.tensor_tensor(A["t1"], A["t1"], A["t1"], ALU.mult))
        step.wait()
        step.go(v.tensor_scalar(A["t2"], A["t2"], 1.0 / 128, LN_EPS, ALU.mult, ALU.add))
        step.wait()
        v.scalar_tensor_tensor(var[:, 0:16], A["t1"], 0.25, A["t2"], ALU.mult, ALU.add).then_inc(sem("var_ready"), 1)
        inverse_sd(16)
        for tb in range(TB):
            for h in range(H):
                i = tb * H + h
                step.go(v.tensor_scalar(A["h"][:, tb, h, :], A["h"][:, tb, h, :], A["mu"][:, i:i + 1], rstd[:, i:i + 1],
                                        ALU.subtract, ALU.mult))
            step.wait()
            hv = A["h"][:, tb, :, :].rearrange("p h n -> p (h n)")
            step(v.tensor_tensor(hv, hv, A["g"], ALU.mult))
            dve.wait_ge(sem("og_ready"), 1)
            v.tensor_tensor(hv, hv, A["og"][:, tb, :], ALU.mult).then_inc(sem("h_ready"), 1)
        for j in ADA_COLS[4:6]:
            ada_part(j)
        residual_norm("mix0")
        for j in ADA_COLS[4:6]:
            ada_column(j)

        def top16(vals, idx, scores, n):
            for lo in (0, 8):
                if lo:
                    for i in range(n):
                        step.go(v.match_replace(scores[:, i, :], vals[:, i, 0:8], scores[:, i, :], -3.0e38))
                    step.wait()
                    yield
                for i in range(n):
                    step.go(v.max(vals[:, i, lo:lo + 8], scores[:, i, :]))
                step.wait()
                yield
                for i in range(n):
                    step.go(v.max_index(idx[:, i, lo:lo + 8], vals[:, i, lo:lo + 8], scores[:, i, :]))
                step.wait()
                yield

        def choose(l, n):
            tb, u = n // UNITS, n % UNITS
            moved(dve, f"sc{l}_{tb}_{u}")
            yield from top16(v1, i1, sc[:, tb, 2 * UH * u:2 * UH * (u + 1), :], 2 * UH)
            step.go(v.tensor_copy(i1f, i1))
            for h in range(UH):
                step.go(v.tensor_tensor(cand[:, h, :].rearrange("p (i j) -> p i j", i=16),
                                        v1[:, 2 * h, :].unsqueeze(2).broadcast_to([P, 16, 16]),
                                        v1[:, 2 * h + 1, :].unsqueeze(1).broadcast_to([P, 16, 16]), ALU.add))
            step.wait()
            yield
            yield from top16(tsv, tp, cand, UH)
            step.go(v.tensor_scalar(p12[:, 0, :, :], tp[:, :, :], 4, None, ALU.logical_shift_right))
            step.go(v.tensor_scalar(p12[:, 1, :, :], tp[:, :, :], 15, None, ALU.bitwise_and))
            step(v.tensor_copy(gsum[:, :], tsv[:, :, 0]))
            v.tensor_tensor(tsv[:, :, :], tsv[:, :, :], gsum[:, :].unsqueeze(2).broadcast_to([P, UH, 16]),
                            ALU.subtract).then_inc(sem("gate_arg"), 1)
            step(v.tensor_copy(p12f[:, :, :, :].rearrange("p a b c -> p (a b c)"),
                               p12[:, :, :, :].rearrange("p a b c -> p (a b c)")))
            yield
            i4 = i1f[:, :, :].rearrange("p (h c) j -> p h c j", c=2)
            for e in range(2):
                step(v.tensor_tensor(eq, p12f[:, e, :, :].unsqueeze(3).broadcast_to([P, UH, 16, 16]),
                                     iota16[:, :].unsqueeze(1).unsqueeze(1).broadcast_to([P, UH, 16, 16]),
                                     ALU.is_equal))
                step(v.tensor_tensor(eq, eq, i4[:, :, e, :].unsqueeze(2).broadcast_to([P, UH, 16, 16]), ALU.mult))
                step(v.tensor_reduce(i12[:, e, :, :], eq, AX, ALU.add))
                yield
            ev = i12[:, 0, :, :].rearrange("p h k -> p (h k)")
            step(v.scalar_tensor_tensor(ev, ev, float(NK), i12[:, 1, :, :].rearrange("p h k -> p (h k)"),
                                        ALU.mult, ALU.add))
            v.tensor_scalar(eidx[:, tb, u * UPAIRS:(u + 1) * UPAIRS], ev, float(l * NEXP), None, ALU.add
                            ).then_inc(sem("experts"), 1)

        def gates(l, n):
            tb, u = n // UNITS, n % UNITS
            dve.wait_ge(sem("gate_exp"), l * TB * UNITS + n + 1)
            step(v.tensor_reduce(gsum[:, :], tsv[:, :, :], AX, ALU.add))
            step(v.reciprocal(grec[:, :], gsum[:, :]))
            step(v.tensor_tensor(gate[:, tb, u * UPAIRS:(u + 1) * UPAIRS].rearrange("p (h k) -> p h k", h=UH),
                                 tsv[:, :, :], grec[:, :].unsqueeze(2).broadcast_to([P, UH, 16]), ALU.mult))

        def experts(l, tb, it):
            r = l * TB + tb
            for g in range(NG):
                for s in range(g * GRP, (g + 1) * GRP):
                    dve.wait_ge(sem(f"row{s}"), (r * ITERS + it + 1) * 16)
                    v.tensor_tensor_reduce(out=gath[:, s, 0:D], in0=gath[:, s, 0:D], in1=xt[:, tb, :], scale=1.0,
                                           scalar=0.0, op0=ALU.mult, op1=ALU.add, accum_out=dots[:, s:s + 1]
                                           ).then_inc(sem("dots"), 1)
                dve.wait_ge(sem("gelu"), (r * ITERS + it) * NG + g + 1)
                if g == 0:
                    dve.sem_inc(sem("gate_go"), 1)
                    v.tensor_copy(gcur[:, :], gate[:, tb, bass.ds(it * SLOTS, SLOTS)]).then_inc(sem("gcur"), 1)
                    dve.wait_ge(sem("gcur"), r * ITERS + it + 1)
                for s in range(g * GRP, (g + 1) * GRP):
                    v.tensor_scalar(diag[:, s, :], ident[:, :], glu[:, s:s + 1], gcur[:, s:s + 1],
                                    ALU.mult, ALU.mult).then_inc(sem("diag"), 1)
                yield

        def peer(l):
            for _ in choose(l, 0):
                pass
            gates(l, 0)
            for _ in choose(l, 1):
                pass
            full(dve, f"pq{l}_15")
            for _ in experts(l, 0, 0):
                pass
            gates(l, 1)
            for n in range(2, TB * UNITS):
                pieces = choose(l, n)
                for it in range(1 + SPREAD * (n - 2), 1 + SPREAD * (n - 1)):
                    for _ in experts(l, 0, it):
                        for _ in range(3):
                            next(pieces, None)
                for _ in pieces:
                    pass
                gates(l, n)
            for tb in range(TB):
                with dve.Fori(WOVEN if tb == 0 else 0, ITERS) as it:
                    for _ in experts(l, tb, it):
                        pass
                nm = [f"pe{l}_{tb}_{half}" for half in range(2)]
                src = [full(dve, x)[:, :] for x in nm]
                layer_norm(tb, src, nm)

        def ple(l):
            for half in range(2):
                for tb in range(TB):
                    cs = slice(half * 512, half * 512 + 512)
                    moved(dve, f"pg{l}_{tb}_{half}")
                    ps = full(dve, f"pp{l}_{tb}_{half}")
                    free(v.tensor_tensor(yt[:, tb, cs], yt[:, tb, cs], ps[:, :], ALU.mult), f"pp{l}_{tb}_{half}")
            for tb in range(TB):
                for half in range(2):
                    moved(dve, f"pp{l}_{tb}_{half}")
                v.tensor_tensor(xt[:, tb, :], xt[:, tb, :], yt[:, tb, :], ALU.add).then_inc(sem("x_ready"), 1)

        peer(0)
        ple(0)

        step(v.tensor_copy(M["posf"], posi[:, :]))
        step(v.tensor_scalar(M["ang"], M["posf"], invf[:, 0:1], None, ALU.mult))
        TWO = 2 * math.pi
        C1 = 6.28125
        C2 = float(np.float32(np.round((TWO - C1) * 2 ** 20) / 2 ** 20))
        C3 = TWO - C1 - C2
        for dst, shift in ((M["w1"], 0.0), (M["w2"], 0.25)):
            step(v.tensor_scalar(M["w3"], M["ang"], 1.0 / TWO, shift, ALU.mult, ALU.add))
            step(v.tensor_scalar(M["w3"], M["w3"], 12582912.0, None, ALU.add))
            step(v.tensor_scalar(M["w3"], M["w3"], -12582912.0, None, ALU.add))
            step(v.scalar_tensor_tensor(dst, M["w3"], -C1, M["ang"], ALU.mult, ALU.add))
            step(v.scalar_tensor_tensor(dst, M["w3"], -C2, dst, ALU.mult, ALU.add))
            step(v.scalar_tensor_tensor(dst, M["w3"], -C3, dst, ALU.mult, ALU.add))
            if shift:
                step(v.tensor_scalar(dst, dst, math.pi / 2, None, ALU.add))
            ins = v.tensor_scalar(dst, dst, 3.1415925, -3.1415925, ALU.min, ALU.max)
            if shift:
                ins.then_inc(sem("ang_ready"), 1)
            else:
                step(ins)
        for tb in range(TB):
            moved(dve, f"ckv_{tb}")
            step.go(v.tensor_tensor_reduce(out=M["oT"][:, tb, :], in0=yt[:, tb, 0:KV_RANK], in1=yt[:, tb, 0:KV_RANK],
                                           scale=1.0, scalar=0.0, op0=ALU.mult, op1=ALU.add,
                                           accum_out=M["ssq"][:, tb:tb + 1]))
            moved(dve, f"cq_{tb}")
            step.go(v.tensor_tensor_reduce(out=M["cq"][:, tb, :], in0=yt[:, tb, 512:512 + Q_RANK],
                                           in1=yt[:, tb, 512:512 + Q_RANK], scale=1.0, scalar=0.0, op0=ALU.mult,
                                           op1=ALU.add, accum_out=M["ssq"][:, 2 + tb:3 + tb]))
        step.wait()
        step.go(v.tensor_scalar(var[:, 0:2], M["ssq"][:, 0:2], 1.0 / KV_RANK, LN_EPS, ALU.mult, ALU.add))
        step.wait()
        v.tensor_scalar(var[:, 2:4], M["ssq"][:, 2:4], 1.0 / Q_RANK, LN_EPS, ALU.mult, ALU.add).then_inc(sem("var_ready"), 1)
        inverse_sd(4)
        dve.wait_ge(sem("mla_par"), 32)
        for tb in range(TB):
            v.scalar_tensor_tensor((M["ckv"] if tb == 0 else M["ckv2"]), yt[:, tb, 0:KV_RANK], rstd[:, tb:tb + 1], M["cg"],
                                   ALU.mult, ALU.mult).then_inc(sem("ckv_ready"), 1)
        for tb in range(TB):
            v.scalar_tensor_tensor(M["cq"][:, tb, :], yt[:, tb, 512:512 + Q_RANK], rstd[:, 2 + tb:3 + tb], M["qg"],
                                   ALU.mult, ALU.mult).then_inc(sem("cq_ready"), 1)
        dve.wait_ge(sem("trig"), 2)

        def rotate(x1, x2, o1, o2, t, names=None):
            step.go(v.tensor_tensor(t[0], x1, M["cos"], ALU.mult))
            step.go(v.tensor_tensor(t[1], x2, M["sin"], ALU.mult))
            step.go(v.tensor_tensor(t[2], x1, M["sin"], ALU.mult))
            ins = v.tensor_tensor(t[3], x2, M["cos"], ALU.mult)
            step.go(ins)
            step.wait()
            step.go(v.tensor_tensor(o1, t[0], t[1], ALU.subtract))
            step.go(v.tensor_tensor(o2, t[2], t[3], ALU.add))
            step.wait()

        moved(dve, "kr0")
        moved(dve, "kr1")
        tt = [M["oT"][:, j, :] for j in range(4)]
        rotate(M["t"][:, 0, :], M["t"][:, 1, :], M["K12"][:, 0, :], M["K12"][:, 1, :], tt)
        step.go(v.memset(M["krm"], 0.0))
        step.wait()
        for j in range(4):
            r = slice(32 * j, 32 * j + 32)
            ins = v.tensor_copy(M["krm"][r, j, :, :], M["K12"][r, :, :])
            if j < 3:
                step.go(ins)
        ins.then_inc(sem("rope"), 1)
        for half in range(2):
            for e in range(2):
                ps = full(dve, f"qr{half}_{e}")
                free(v.tensor_copy(M["t"][:, e, :], ps[:, 0:T]), f"qr{half}_{e}")
                moved(dve, f"qr{half}_{e}")
            rotate(M["t"][:, 0, :], M["t"][:, 1, :], M["R"][:, half, 0, :], M["R"][:, half, 1, :], tt)
            v.tensor_copy(M["w3"][:, 0:1], M["R"][:, half, 1, 0:1]).then_inc(sem("rope"), 1)

        def sm_max(nm, i, E, scale, bias, ready, before):
            ps = full(dve, nm)
            if before:
                full(dve, before)
            free(v.scalar_tensor_tensor(E[:, i % 3, :], ps[:, 0:384], scale, bias, ALU.mult, ALU.add), nm)
            moved(dve, nm)
            step.go(v.tensor_reduce(rmax[:, i % 3, 0:1], E[:, i % 3, 0:P], AX, ALU.max, negate=True))
            v.tensor_reduce(rmax[:, i % 3, 1:2], E[:, i % 3, P:384], AX, ALU.max, negate=True).then_inc(sem(ready), 1)

        def sm_norm(i, E, exp_sem, probs, gcol=None):
            dve.wait_ge(sem(exp_sem), i + 1)
            step(v.reciprocal(rrec[:, i % 3, :], rsum[:, i % 3, :]))
            if gcol is not None:
                step(v.tensor_tensor(rrec[:, i % 3, :], rrec[:, i % 3, :], gcol, ALU.mult))
            step.go(v.tensor_scalar(E[:, i % 3, 0:P], E[:, i % 3, 0:P], rrec[:, i % 3, 0:1], None, ALU.mult))
            v.tensor_scalar(E[:, i % 3, P:384], E[:, i % 3, P:384], rrec[:, i % 3, 1:2], None, ALU.mult
                            ).then_inc(sem(probs), 1)

        for h in range(H):
            sm_max(f"lS{h}", h, M["E"], MLA_SCALE, maskQ[:, :], "l_max", f"lT{h - 3}" if h >= 3 else None)
            if h:
                sm_norm(h - 1, M["E"], "l_exp", "probs")
        sm_norm(H - 1, M["E"], "l_exp", "probs")
        for j in ADA_COLS[6:8]:
            ada_part(j)
        residual_norm("mix1")
        for j in ADA_COLS[6:8]:
            ada_column(j)
        peer(1)
        ple(1)

        def rms_stats():
            for tb in range(TB):
                step.go(v.tensor_tensor_reduce(out=yt[:, tb, :], in0=xt[:, tb, :], in1=xt[:, tb, :], scale=1.0,
                                               scalar=0.0, op0=ALU.mult, op1=ALU.add, accum_out=var[:, tb:tb + 1]))
            step.wait()
            add_eps(2, 1.0 / D, RMS_EPS)
            inverse_sd(2)

        dve.wait_ge(sem("x_ready"), TB * 6)
        rms_stats()
        for tb in range(TB):
            v.tensor_scalar(yt[:, tb, :], xt[:, tb, :], rstd[:, tb:tb + 1], None, ALU.mult).then_inc(sem("xn_ready"), 1)
        dve.wait_ge(sem("hyb_par"), 16 * 6)
        step(v.tensor_tensor(N["mod"], adac[:, :, :], N["bada"], ALU.add))
        step.go(v.scalar_tensor_tensor(N["gs"][:, 0, :], N["mod"][:, 1, :], 1.0, N["ng"][:, 0, :], ALU.add, ALU.mult))
        v.scalar_tensor_tensor(N["gs"][:, 1, :], N["mod"][:, 3, :], 1.0, N["ng"][:, 1, :], ALU.add, ALU.mult
                               ).then_inc(sem("mod_ready"), 1)
        ada_part(ADA_GATES[0])
        ada_part(ADA_GATES[1])
        for j in ADA_GATES[:2]:
            ada_gate(j)
        dve.wait_ge(sem("hyb_const"), 1)
        for kv in range(2):
            moved(dve, f"cmp{kv}")
            for g in range(2):
                i = 2 * kv + g
                base = kcv[:, i, :].rearrange("p (n l) -> p l n", l=16)
                pc = N["posc"][:, kv, :]
                for hf in range(2):
                    ins = v.tensor_tensor(ckin[:, i, hf * 16:hf * 16 + 16, 0:NCMP], base[:, :, hf:hf + NCMP],
                                          pc[:, hf * 16:hf * 16 + 16].unsqueeze(2).broadcast_to([HD, 16, NCMP]), ALU.add)
                    if (g, hf) != (1, 1):
                        step.go(ins)
            ins.then_inc(sem("ckin_ready"), 1)
        ps = full(dve, "vc")
        free(v.tensor_tensor(N["vcm"], ps[:, 0:HD].unsqueeze(1).broadcast_to([P, H, HD]),
                             N["m8"].unsqueeze(2).broadcast_to([P, H, HD]), ALU.mult), "vc")
        cE = N["cE"].rearrange("p b h n -> p (b h) n")
        cmx = N["cmx"].rearrange("p b h -> p (b h)")
        csm = N["csm"].rearrange("p b h -> p (b h)")
        crc = N["crc"].rearrange("p b h -> p (b h)")
        for e in range(2):
            ps = full(dve, f"cS{e}")
            free(v.scalar_tensor_tensor(N["cE"].rearrange("p b (i e) n -> p (b i) e n", e=2)[:, :, e, :],
                                        ps[:, 0:P].rearrange("p (i n) -> p i n", n=CW), SCALE,
                                        N["cb"].rearrange("p b (i e) n -> p (b i) e n", e=2)[:, :, e, :],
                                        ALU.mult, ALU.add), f"cS{e}")
        moved(dve, "cS0")
        moved(dve, "cS1")
        step(v.tensor_reduce(cmx, cE, AX, ALU.max))
        v.tensor_tensor(cE, cE, cmx.unsqueeze(2).broadcast_to([P, 16, CW]), ALU.subtract).then_inc(sem("c_arg"), 1)
        dve.wait_ge(sem("c_exp"), 1)
        step(v.tensor_reduce(csm, cE, AX, ALU.add))
        step(v.reciprocal(crc, csm))
        for tb in range(TB):
            moved(dve, f"vw{tb}")
            ga = N["ga"][:, tb, :].rearrange("p (h e) -> p h e", e=3)
            step(v.scalar_tensor_tensor(N["crc"][:, tb, :], N["crc"][:, tb, :], N["rv"][:, tb:tb + 1], ga[:, :, 0],
                                        ALU.mult, ALU.mult))
        v.tensor_tensor(cE, cE, crc.unsqueeze(2).broadcast_to([P, 16, CW]), ALU.mult).then_inc(sem("cprobs"), 1)

        for j in ADA_GATES[2:]:
            ada_part(j)
            ada_gate(j)

        def gcol(i):
            h, e = i // 2, i % 2
            return N["ga"][:, :, h * 3 + 1 + e]

        def n_item(i):
            h = i // 2
            dve.wait_ge(sem("bias_ready"), h + 1)
            sm_max(f"nS{i}", i, N["E"], SCALE, N["bh"][:, h % 2, :], "n_max", f"nT{i - 3}" if i >= 3 else None)
            if i % 2 == 1:
                dve.sem_inc(sem("bias_used"), 1)
            if i:
                sm_norm(i - 1, N["E"], "n_exp", "nprobs", gcol(i - 1))

        def break_sums(h):
            z1 = sbp[:, h % 2, :]
            ps = full(dve, f"bL{h}")
            free(v.tensor_tensor(z1, z1, ps[:, 0:384], ALU.add), f"bL{h}")
            moved(dve, f"bL{h}")
            dve.sem_inc(sem("b_arg"), 1)

        def break_keep(h):
            z, z1, lk = sbk[:, 0, :], sbp[:, h % 2, :], sbk[:, 2 + h % 2, :]
            dve.wait_ge(sem("b_log"), h + 1)
            if h >= 2:
                full(dve, f"bO{h - 2}")
            step(v.scalar_tensor_tensor(z1, z, 0.0, sbk[:, 1, :], ALU.min, ALU.subtract))
            step.go(v.scalar_tensor_tensor(lk, z, -1.0, z1, ALU.mult, ALU.add))
            step.wait()
            step.go(v.tensor_tensor(z1, z1, maskS[:, :], ALU.add))
            v.tensor_tensor(lk, lk, keep[:, :], ALU.mult).then_inc(sem("keep"), 1)
            step.wait()

        for h in range(H):
            n_item(2 * h)
            if h:
                break_sums(h - 1)
            n_item(2 * h + 1)
            break_keep(h)
        sm_norm(2 * H - 1, N["E"], "n_exp", "nprobs", gcol(2 * H - 1))
        break_sums(H - 1)

        for ch in range(KC):
            if ch % 4 == 0:
                dve.wait_ge(sem("merge_gates"), 3 + ch // 4)
            ps = full(dve, f"ya{ch}")
            free(v.tensor_tensor(N["sgm"][:, ch, :], N["sgm"][:, ch, :], ps[:, 0:T], ALU.mult), f"ya{ch}")
            ps = full(dve, f"yb{ch}")
            free(v.tensor_tensor(N["sgm"][:, KC + ch, :], N["sgm"][:, KC + ch, :], ps[:, 0:T], ALU.mult), f"yb{ch}")
            moved(dve, f"ya{ch}")
            moved(dve, f"yb{ch}")
            v.tensor_tensor(xT[:, ch, :], N["sgm"][:, ch, :], N["sgm"][:, KC + ch, :], ALU.add).then_inc(sem("yT"), 1)

        def gated_residual(name, g):
            for tb in range(TB):
                for half in range(2):
                    cs = slice(half * 512, half * 512 + 512)
                    nm = f"{name}_{tb}_{half}"
                    ps = full(dve, nm)
                    free(v.tensor_tensor(yt[:, tb, cs], ps[:, :], g[:, cs], ALU.mult), nm)
                    moved(dve, nm)
                v.tensor_tensor(xt[:, tb, :], xt[:, tb, :], yt[:, tb, :], ALU.add).then_inc(sem("x_ready"), 1)
        gated_residual("mix2", N["g1"])
        dve.wait_ge(sem("x_ready"), TB * 7)
        rms_stats()
        for tb in range(TB):
            v.tensor_scalar(yt[:, tb, :], xt[:, tb, :], rstd[:, tb:tb + 1], None, ALU.mult).then_inc(sem("xn_ready"), 1)
        for ch in range(FC):
            moved(dve, f"fg{ch}")
            ps = full(dve, f"fu{ch}")
            free(v.tensor_tensor(F["hid"][:, ch, :], F["hid"][:, ch, :], ps[:, 0:T], ALU.mult), f"fu{ch}")
            moved(dve, f"fu{ch}")
            dve.sem_inc(sem("hid"), 1)
        gated_residual("dn", N["g2"])
        dve.wait_ge(sem("x_ready"), TB * 8)
        rms_stats()
        dve.wait_ge(sem("lnp"), 16 * 5)
        for tb in range(TB):
            v.scalar_tensor_tensor(yt[:, tb, :], xt[:, tb, :], rstd[:, tb:tb + 1], lnp[:, 0, :], ALU.mult, ALU.mult
                                   ).then_inc(sem("out_ready"), 1)


def layouts(inputs):
    g = {k: np.asarray(v) for k, v in inputs.items()}
    bc = lambda v: np.ascontiguousarray(np.broadcast_to(v, (P,) + v.shape))
    cols = lambda v: np.ascontiguousarray(v.reshape(-1, P).T)
    d = {k: g[k] for k in ("a_w_in", "a_w_out", "kv_w_up", "b_w_dq", "b_w_out", "peer_w_q",
                           "ple_w_proj", "ple_w_gate", "w_ada_2", "cmp_w1_k_2", "cmp_w1_v_2", "w_proj_a_2", "w_proj_b_2", "w_out_2", "w_ffn_gate_2", "w_ffn_up_2",
                           "w_ffn_down_2")}
    w = g["kv_w_down"]
    r1, r2 = w[:, KV_RANK:KV_RANK + RHALF], w[:, KV_RANK + RHALF:]
    d["kv_w_down_r"] = np.concatenate([w[:, :KV_RANK]] + [r1] * 4 + [r2] * 4, axis=1)
    w = g["b_w_uq"][0].reshape(Q_RANK, 2, 4, 192)
    d["b_w_uq_p"] = np.concatenate([w[..., :128].reshape(Q_RANK, 2, 512), w[..., 128:160].reshape(Q_RANK, 2, 128),
                                    w[..., 160:].reshape(Q_RANK, 2, 128)], axis=2).reshape(Q_RANK, 1536)
    w = g["w_in_2"][0]
    twice = lambda c0: [w[:, c0 + j * HD:c0 + (j + 1) * HD] for j in (0, 0, 1, 1)]
    d["w_in_2r"] = np.concatenate([w[:, :768]] + twice(768) + twice(1024) + [w[:, 896:1024], w[:, 1152:]], axis=1)
    d["cmp_w2"] = np.ascontiguousarray(np.stack([g["cmp_w2_k_2"][0]] * 2 + [g["cmp_w2_v_2"][0]], axis=1))
    d["x"] = g["x"][0]
    d["xTin"] = np.ascontiguousarray(g["x"][0].T)
    d["pT"] = np.ascontiguousarray(g["p"][:, 0].transpose(0, 2, 1))
    d["pos"] = bc(g["positions"][0])
    d["invf"] = np.tile((np.float32(THETA) ** (-np.arange(0, ROPE, 2, dtype=np.float32) / np.float32(ROPE))), 4)[:, None].astype(np.float32)
    gb = np.stack([g["ln_g"], g["ln_b"]], axis=2)
    d["lnp"] = np.ascontiguousarray(np.broadcast_to(gb[:, :, None], (DEPTH, 2, P, 2, D)))
    d["hng"] = bc(g["a_hn_g"][0])
    d["bif"] = np.ascontiguousarray(g["a_b_if"][0].T)
    d["kvg"] = bc(g["kv_norm_g"])
    d["qng"] = bc(g["b_q_norm_g"][0])
    d["keysT"] = np.ascontiguousarray(g["peer_sub_keys"].transpose(0, 4, 1, 2, 3).reshape(DEPTH, P, 2048))
    d["uv"] = np.concatenate([g["peer_u"], g["peer_v"]], axis=2).reshape(DEPTH * NEXP, 2 * D)
    d["cT"] = cols(g["c_2"][0])
    b = g["b_ada_2"][0].reshape(6, D)
    d["badaT"] = np.ascontiguousarray(np.stack([cols(b[i]) for i in (0, 1, 3, 4)], axis=1))
    d["bg1"], d["bg2"] = bc(b[2]), bc(b[5])
    d["ngT"] = np.ascontiguousarray(np.stack([cols(g["norm_mix_g_2"][0]), cols(g["norm_ffn_g_2"][0])], axis=1))
    d["nfg"] = bc(g["norm_final_g_2"])
    d["posc"] = np.ascontiguousarray(np.stack([g["cmp_pos_k_2"][0].T, g["cmp_pos_v_2"][0].T], axis=1))
    return d


def kernel(**inputs):
    import concourse.bacc as bacc
    from concourse.bass_utils import run_bass_kernel_spmd as run
    nc = bacc.Bacc("TRN2", target_bir_lowering=False, num_devices=1)
    d = layouts(inputs)
    aps = {k: nc.dram_tensor("in_" + k, v.shape, mybir.dt.from_np(v.dtype), kind="ExternalInput").ap()
           for k, v in d.items()}
    out = nc.dram_tensor("out", (T, D), F32, kind="ExternalOutput").ap()
    build(nc, aps, out)
    r = run(nc, [{"in_" + k: v for k, v in d.items()}], core_ids=[0])
    return r.results[0]["out"].reshape(1, T, D)
```

```python
import math
from contextlib import ExitStack

import numpy as np
import concourse.bass as bass
from concourse import mybir

F32 = mybir.dt.float32
U32 = mybir.dt.uint32
I32 = mybir.dt.int32
ALU = mybir.AluOpType
ACT = mybir.ActivationFunctionType
AX = mybir.AxisListType.X

P = 128
D = 1024
T = 256
TB = T // P
KC = D // P
DEPTH = 2
ALPHA = (2.0 * DEPTH) ** 0.25
LN_EPS = 1e-5
RMS_EPS = 1e-6
H = 8
QK = D // (2 * H)
A_V, A_G, A_O = 2 * H * QK, 2 * H * QK + D, 2 * H * QK + D + 2 * H
ROPE, RHALF = 64, 32
KV_RANK, Q_RANK = 256, 384
MLA_SCALE = (128 + ROPE) ** -0.5
THETA = 10000.0
PH, NK, TOPK, NEXP = 8, 128, 16, 16384
PAIRS = PH * TOPK
SLOTS = 8
GRP = 2
NG = SLOTS // GRP
ITERS = PAIRS // SLOTS
UH = 2
UNITS = PH // UH
UITERS = ITERS // UNITS
UPAIRS = UH * TOPK
SPREAD = 2
WOVEN = 1 + SPREAD * (TB * UNITS - 2)
HD = 64
NCMP, CW = 15, 16
FF = 2816
FC = FF // P
SCALE = 1.0 / math.sqrt(HD)
SLOPES = [2.0 ** (-8.0 * (i + 1) / H) for i in range(H)]
FAR = 1e33
NEG = -1e30
ADA_COLS = (0, 1, 2, 3, 6, 7, 8, 9)
ADA_GATES = (4, 5, 10, 11)
SLOT = 4096
NW = 4


def build(nc, a, out, dbg=None):
    with ExitStack() as ctx:
        program(nc, a, out, ctx, dbg or {})


def program(nc, a, out, ctx, dbg):
    def sb(name, shape, dt=F32):
        return ctx.enter_context(nc.sbuf_tensor(name, shape, dt))

    sems = {}

    def sem(name):
        if name not in sems:
            sems[name] = ctx.enter_context(nc.semaphore(name))
        return sems[name]

    ring = sb("ring", [P, NW, SLOT])
    arena = sb("arena", [P, SLOTS * 2 * D])
    qreg = sb("qreg", [P, 4096])
    sreg = sb("sreg", [P, 4096])
    xt = sb("x_tok", [P, TB, D])
    yt = sb("y_tok", [P, TB, D])
    xT = sb("xT", [P, KC, T])
    lnp = sb("lnp", [P, 2, D])
    ident = sb("ident", [P, P])
    identa = sb("identa", [P, P])
    ones = sb("ones", [P, P])
    upper = sb("upper", [P, P])
    maskT = sb("maskT", [P, 384])
    maskS = sb("maskS", [P, 384])
    keep = sb("keep", [P, 384])
    maskQ = sb("maskQ", [P, 384])
    iota16 = sb("iota16", [P, 16])
    bnst = sb("bnst", [P, 2, 6])
    mv = sb("mv", [P, 2])
    var = sb("var", [P, 16])
    sdv = sb("sdv", [P, 16])
    rstd = sb("rstd", [P, 16])
    psum = [ctx.enter_context(nc.psum_tensor(f"bank{b}", [P, 512], F32)) for b in range(8)]

    def carve(region, parts=P):
        at = [0]

        def take(*shape, p=parts):
            n = int(np.prod(shape))
            v = region[0:p, at[0]:at[0] + n]
            at[0] += n
            assert at[0] <= region.shape[1], (at, region.shape)
            if len(shape) > 1:
                names = "abcd"[:len(shape)]
                v = v.rearrange(f"p ({' '.join(names)}) -> p {' '.join(names)}",
                                **{k: s for k, s in zip(names, shape)})
            return v
        return take

    bank_full = [sem(f"bank_full{b}") for b in range(8)]
    bank_free = [sem(f"bank_free{b}") for b in range(8)]
    slot_loaded = [sem(f"slot_loaded{i}") for i in range(NW)]
    place = {}
    uses = [0] * 8

    def full(eng, name):
        b, k = place[name]
        eng.wait_ge(bank_full[b], k + 1)
        return psum[b]

    def moved(eng, name):
        b, k = place[name]
        eng.wait_ge(bank_free[b], k + 1)

    def free(ins, name):
        ins.then_inc(bank_free[place[name][0]], 1)

    ada_order, ada_at = [], {}
    loads = []

    block = ctx.enter_context(nc.Block())

    class Steps:
        def __init__(self, eng, name):
            self.eng, self.sem, self.n = eng, sem(name), 0

        def go(self, ins):
            ins.then_inc(self.sem, 1)
            self.n += 1

        def wait(self):
            self.eng.wait_ge(self.sem, self.n)

        def __call__(self, ins):
            self.go(ins)
            self.wait()

    c = carve(arena)
    A = dict(qT=c(4, T), kT=c(4, T), v=c(TB, H, 129), og=c(TB, D), h=c(TB, H, 128),
             negM=c(H, 384), Pm=c(2, 384), tm=c(2, 384), hT=c(KC, T), g=c(D))
    c = carve(sreg)
    A.update(sel=c(H, P, p=8), ig=c(T, p=8), xf=c(T, p=8), ax=c(T, p=8), ex=c(T, p=8), lf=c(T, p=8),
             B=c(T, p=8), a=c(T, p=8), M=c(T, p=8), nM=c(T, p=8), m=c(T, p=8))
    c = carve(qreg)
    A.update(acol=c(TB, H), enm=c(TB, H), den=c(2, 2), rden=c(2, 2), st=c(TB * H, 6),
             mu=c(16), t1=c(16), t2=c(16), bif=c(2, p=8))
    gath = arena[:, :].rearrange("p (s n) -> p s n", s=SLOTS)
    pq = qreg[:, :].rearrange("p (c t) -> p c t", c=16)
    sc = sreg[:, :].rearrange("p (b c n) -> p b c n", b=TB, c=16)
    c = carve(yt[:, :, :].rearrange("p b d -> p (b d)"))
    v1 = c(2 * UH, 16)
    i1 = c(2 * UH, 16).bitcast(U32)
    i1f = c(2 * UH, 16)
    tsv = c(UH, 16)
    tp = c(UH, 16).bitcast(U32)
    p12 = c(2, UH, 16).bitcast(U32)
    p12f = c(2, UH, 16)
    i12 = c(2, UH, 16)
    cand = c(UH, 256)
    eq = cand.rearrange("p h (k j) -> p h k j", k=16)
    eidx = sb("eidx", [P, TB, PAIRS], U32)
    gate = sb("gate", [P, TB, PAIRS])
    gsum = sb("gsum", [P, UH])
    grec = sb("grec", [P, UH])
    idc = sb("idc", [P, SLOTS], U32)
    gcur = sb("gcur", [P, SLOTS])
    dots = sb("dots", [P, SLOTS])
    glu = sb("glu", [P, SLOTS])
    diag = sreg[:, 0:SLOTS * P].rearrange("p (s n) -> p s n", s=SLOTS)
    c = carve(arena)
    M = dict(knT=c(H, T), v=c(TB, D), qnT=c(H, T), oT=c(H, T), krm=c(4, 2, T), ckvT=c(2, T),
             cqT=c(3, T), R=c(2, 2, T), K12=c(2, T), t=c(4, T))
    c = carve(sreg)
    M.update(E=c(3, 384), PT=c(4, 384), ckv=c(KV_RANK), ckv2=c(KV_RANK))
    c = carve(qreg)
    M.update(cq=c(TB, Q_RANK), cg=c(KV_RANK), qg=c(Q_RANK), ang=c(T), cos=c(T), sin=c(T), w1=c(T),
             w2=c(T), w3=c(T), posf=c(T), ssq=c(4), sm=c(2, 8))
    cT = sb("cT", [P, KC])
    scT = sb("silu_cT", [P, KC])
    adac = sb("ada_columns", [P, 4, KC])
    junk = sb("junk", [P, P])
    posi = sb("posi", [P, T], I32)
    invf = sb("invf", [P, 1])
    rmax = sb("rmax", [P, 3, 2])
    rsum = sb("rsum", [P, 3, 2])
    rrec = sb("rrec", [P, 3, 2])
    c = carve(arena)
    N = dict(qT=c(4, T), ksT=c(2, T), kwT=c(2, T), vs=c(TB, P), vw=c(TB, P), qbT=c(4, T), kbT=c(4, T),
             vb=c(TB, 512), sgm=c(16, T), oaT=c(4, T), obT=c(4, T), g1=c(D), g2=c(D), sbk=c(4, 384),
             sbp=c(2, 384))
    sbk, sbp = N["sbk"], N["sbp"]
    c = carve(qreg)
    N.update(E=c(3, 384), PT=c(4, 384), bh=c(2, 384), dist=c(384))
    c = carve(sreg)
    N.update(cb=c(TB, H, CW), cE=c(TB, H, CW), cPT=c(T), vcm=c(H, HD), cdist=c(TB, CW), hid=c(2, CW), hidv=c(2, 4, CW),
             kc=c(2, CW), ga=c(TB, 24), w2=c(3, HD), m8=c(8), rv=c(2), cmx=c(TB, H), csm=c(TB, H),
             crc=c(TB, H), mod=c(4, KC), bada=c(4, KC), ng=c(2, KC), gs=c(2, KC),
             posc=c(2, 16))
    c = carve(N["sgm"].rearrange("p a b -> p (a b)"))
    ckin = c(2, 16, 2 * CW)
    kcv = c(4, T)
    c = carve(arena[:, :])
    F = dict(hid=c(FC, T))

    @block.tensor
    def _(pe):
        n_open = [0]
        held = set()

        def open_(name):
            while n_open[0] % 8 in held:
                n_open[0] += 1
            b = n_open[0] % 8
            n_open[0] += 1
            k = uses[b]
            uses[b] += 1
            place[name] = (b, k)
            if k:
                pe.wait_ge(bank_free[b], k)
            return psum[b]

        def close(ins, name):
            ins.then_inc(bank_full[place[name][0]], 1)

        def mm(o, l, r, start=True, stop=True):
            return nc.tensor.matmul(o, l, r, start=start, stop=stop)

        nw = [0]

        def take(src, kc, n, p=P):
            i = nw[0]
            nw[0] += 1
            s = i % NW
            rec = dict(kind="w", src=src, slot=s, i=i, kc=kc, n=n, p=p, done=None)
            loads.append(rec)
            pe.wait_ge(slot_loaded[s], 16 * (i // NW + 1))
            v = ring[0:p, s, 0:kc * n].rearrange("p (k n) -> p k n", k=kc)
            return v, rec

        def last_use(rec, name):
            b, k = place[name]
            rec["done"] = (bank_full[b], k + 1)

        def ada_load(j):
            i = nw[0]
            nw[0] += 1
            rec = dict(kind="w", src=rows(a["w_ada_2"][0], j * 512, 512), slot=i % NW, i=i, kc=KC, n=512, p=P, done=None)
            loads.append(rec)
            ada_order.append(j)
            ada_at[j] = (i % NW, 16 * (i // NW + 1), rec)

        def ada_sum(j):
            slot, _, rec = ada_at[j]
            pe.wait_ge(sem("ada_part"), ada_order.index(j) + 1)
            o = open_(f"ada{j}")
            close(mm(o[:, :], ones[:, :], ring[:, slot, (KC - 1) * 512:KC * 512]), f"ada{j}")
            last_use(rec, f"ada{j}")

        def aux(dst, src, key, after=None):
            loads.append(dict(kind="aux", dst=dst, src=src, sem=sem(key), after=after))

        def rows(w, c0, n):
            return w[:, c0:c0 + n].rearrange("(k p) n -> p k n", p=P)

        def featT(name, w, src, cols, kc, rhs=None, m=P):
            o = open_(name)
            for k in range(kc):
                l = w[:, k, cols] if isinstance(cols, slice) else cols(k)
                ins = mm(o[0:m, 0:T], l, src[:, k, :], k == 0, k == kc - 1)
            close(ins, name)

        def tok(name, src, w, tb, n, kc, wk=0, cols=slice(None)):
            o = open_(name)
            for k in range(kc):
                ins = mm(o[:, 0:n], src[:, k, tb * P:(tb + 1) * P], w[:, k, cols], k == 0, k == kc - 1)
            close(ins, name)

        def transposes(name, src, dst_chunks, tbs, ready, base):
            for tb in tbs:
                pe.wait_ge(ready, base + tb + 1)
                for g0 in range(0, dst_chunks, 4):
                    g1 = min(g0 + 4, dst_chunks)
                    nm = f"{name}_{tb}_{g0 // 4}"
                    o = open_(nm)
                    for k in range(g0, g1):
                        ins = nc.tensor.transpose(o[:, (k - g0) * P:(k - g0 + 1) * P],
                                                  src[:, tb, k * P:(k + 1) * P], ident[:, :])
                    close(ins, nm)

        def await_T(name, chunks=KC):
            for tb in range(TB):
                for g in range(-(-chunks // 4)):
                    moved(pe, f"{name}_{tb}_{g}")

        def out_proj(name, srcT, w_dram, ada=()):
            ws = [take(rows(w_dram, half * 512, 512), KC, 512) for half in range(2)]
            for j in ada:
                ada_load(j)
            for tb in range(TB):
                for half in range(2):
                    tok(f"{name}_{tb}_{half}", srcT, ws[half][0], tb, 512, KC)
            for half in range(2):
                last_use(ws[half][1], f"{name}_{TB - 1}_{half}")
            for j in ada:
                ada_sum(j)

        pe.sem_inc(sem("row_free"), SLOTS)
        pe.wait_ge(sem("consts"), 1)

        pe.wait_ge(sem("xT_loaded"), 16)
        win = a["a_w_in"][0]
        w, rec = take(rows(win, A_G, 2 * H), KC, 2 * H)
        featT("gi", w, xT, slice(0, H), KC, m=H)
        featT("gf", w, xT, slice(H, 2 * H), KC, m=H)
        last_use(rec, "gf")
        for nm, c0 in (("q", 0), ("k", H * QK)):
            w, rec = take(rows(win, c0, 512), KC, 512)
            ada_load(ADA_COLS[nm == "k"])
            for ch in range(4):
                featT(f"{nm}{ch}", w, xT, slice(ch * P, (ch + 1) * P), KC)
            last_use(rec, f"{nm}3")
        pe.wait_ge(sem("gates"), 1)
        o = open_("acol")
        for tb in range(TB):
            nc.tensor.transpose(o[:, tb * H:tb * H + H], A["a"][:, tb * P:(tb + 1) * P], ident[0:H, 0:H])
            ins = nc.tensor.transpose(o[:, 16 + tb * H:16 + tb * H + H], A["m"][:, tb * P:(tb + 1) * P],
                                      ident[0:H, 0:H])
        close(ins, "acol")
        for j in range(4):
            o = open_(f"nb{j}")
            for e in range(2):
                ins = mm(o[:, e * T:(e + 1) * T], A["sel"][:, 2 * j + e, :], A["nM"][:, :])
            close(ins, f"nb{j}")
        for half in range(2):
            ada_sum(ADA_COLS[half])
            w, rec = take(rows(win, A_V + half * 512, 512), KC, 512)
            ada_load(ADA_COLS[2 + half])
            for tb in range(TB):
                tok(f"v_{tb}_{half}", xT, w, tb, 512, KC)
            last_use(rec, f"v_1_{half}")
        ada_sum(ADA_COLS[2])

        def mS(h):
            r = slice((h % 2) * 64, (h % 2) * 64 + 64)
            if h % 2 == 0:
                moved(pe, f"q{h // 2}")
                moved(pe, f"k{h // 2}")
            o = open_(f"mS{h}")
            mm(o[:, 0:T], A["kT"][r, h // 2, 0:P], A["qT"][r, h // 2, :])
            close(mm(o[:, T:384], A["kT"][r, h // 2, P:T], A["qT"][r, h // 2, P:T]), f"mS{h}")

        def mO(h):
            moved(pe, f"mS{h}")
            o = open_(f"mO{h}")
            pm = A["Pm"][:, h % 2, :]
            mm(o[:, 0:129], pm[:, 0:P], A["v"][:, 0, h, :])
            mm(o[:, 129:258], pm[:, P:T], A["v"][:, 0, h, :], True, False)
            close(mm(o[:, 129:258], pm[:, T:384], A["v"][:, 1, h, :], False, True), f"mO{h}")

        mS(0)
        mS(1)
        for tb in range(TB):
            for half in range(2):
                moved(pe, f"v_{tb}_{half}")
        pe.wait_ge(sem("v_ones"), 1)
        ow = []
        for h in range(H):
            mO(h)
            if h + 2 < H:
                mS(h + 2)
            if h in (1, 2):
                half = h - 1
                ow.append(take(rows(win, A_O + half * 512, 512), KC, 512))
                tok(f"og_0_{half}", xT, ow[half][0], 0, 512, KC)
            if h == 4:
                ada_sum(ADA_COLS[3])
        for half in range(2):
            tok(f"og_1_{half}", xT, ow[half][0], 1, 512, KC)
            last_use(ow[half][1], f"og_1_{half}")
        transposes("hT", A["h"].rearrange("p a b c -> p a (b c)"), KC, range(TB), sem("h_ready"), 0)
        await_T("hT")
        aux(lnp[:, :, :], a["lnp"][0, 0], "lnp")
        out_proj("mix0", A["hT"], a["a_w_out"][0], ADA_COLS[4:6])

        def peer(l, xv):
            transposes(f"xT{xv}", xt, KC, range(TB), sem("x_ready"), TB * (xv - 1))
            await_T(f"xT{xv}")

            def scores(tb, j):
                if tb == 0:
                    for e in range(4):
                        moved(pe, f"pq{l}_{j * 4 + e}")
                nm = f"sc{l}_{tb}_{j}"
                o = open_(nm)
                for e in range(4):
                    ch = j * 4 + e
                    ins = mm(o[:, e * P:(e + 1) * P], pq[:, ch, tb * P:(tb + 1) * P], wk[:, 0, ch * P:(ch + 1) * P])
                close(ins, nm)

            def start(tb):
                names = [f"pe{l}_{tb}_{half}" for half in range(2)]
                o = [open_(x) for x in names]
                held.update(place[x][0] for x in names)
                return o

            def body(tb, o, it, first=False):
                for s in range(SLOTS):
                    pe.wait_ge(sem("diag"), (l * TB + tb) * PAIRS + it * SLOTS + s + 1)
                    for half in range(2):
                        ins = mm(o[half][:, :], diag[:, s, :], gath[:, s, D + half * 512:D + half * 512 + 512],
                                 first and s == 0, False)
                    ins.then_inc(sem("row_free"), 1)

            for j in range(4):
                w, rec = take(rows(a["peer_w_q"][l], j * 512, 512), KC, 512)
                for e in range(4):
                    featT(f"pq{l}_{j * 4 + e}", w, xT, slice(e * P, (e + 1) * P), KC)
                    if j >= 2 and e == 0:
                        scores(0, j - 1)
                    if j == 3 and e == 1:
                        o = start(0)
                        body(0, o, 0, True)
                last_use(rec, f"pq{l}_{j * 4 + 3}")
                if j == 0:
                    wk, rk = take(a["keysT"][l].unsqueeze(1), 1, 2048)
                    scores(0, 0)
            for tb, j in ((1, 0), (1, 1), (1, 2), (0, 3), (1, 3)):
                scores(tb, j)
            last_use(rk, f"sc{l}_1_3")
            aux(lnp[:, :, :], a["lnp"][l, 1], "lnp", (sem("x_ready"), TB * xv))
            for tb in range(TB):
                if tb == 1:
                    o = start(1)
                    body(1, o, 0, True)
                    ple_T(l, xv, 0)
                    for half in range(2):
                        body(1, o, 1 + half)
                        ple_half(l, 0, half)
                with pe.Fori(1 if tb == 0 else 3, ITERS) as it:
                    body(tb, o, it)
                for half in range(2):
                    nm = f"pe{l}_{tb}_{half}"
                    close(mm(o[half][:, :], identa[:, :], xt[:, tb, half * 512:half * 512 + 512], False, True), nm)
                    held.discard(place[nm][0])

        ple_w = {}

        def ple_T(l, xv, tb):
            transposes(f"xP{l}", xt, KC, [tb], sem("x_ready"), TB * xv + tb)
            if tb == 0:
                ple_w["p"] = take(a["pT_wp"][l].rearrange("(k p) n -> p k n", p=P), 2, T + D)
            for g in range(2):
                moved(pe, f"xP{l}_{tb}_{g}")

        def ple_half(l, tb, half):
            if tb == 0:
                ple_w[half] = take(rows(a["ple_w_gate"][l], half * 512, 512), KC, 512)
            w, rec = ple_w[half]
            wp, rp = ple_w["p"]
            tok(f"pg{l}_{tb}_{half}", xT, w, tb, 512, KC)
            tok(f"pp{l}_{tb}_{half}", wp, wp, tb, 512, 2, cols=slice(T + half * 512, T + half * 512 + 512))
            if tb == 1:
                last_use(rec, f"pg{l}_1_{half}")
                if half == 1:
                    last_use(rp, f"pp{l}_1_1")

        def ple(l, xv):
            ple_T(l, xv, 1)
            for half in range(2):
                ple_half(l, 1, half)

        latent_w = []

        def latent(tb):
            pe.wait_ge(sem("x_ready"), TB + 2 + 2 * tb)
            transposes("xT3", xt, KC, [tb], sem("x_ready"), TB)
            if tb == 0:
                latent_w.extend(take(rows(a["kv_w_down_r"], 0, 512), KC, 512))
            for g in range(2):
                moved(pe, f"xT3_{tb}_{g}")
            tok(f"ckv_{tb}", xT, latent_w[0], tb, KV_RANK, KC, cols=slice(0, KV_RANK))

        peer(0, 1)
        latent(0)
        ple(0, 1)

        latent(1)
        for e in range(2):
            featT(f"kr{e}", latent_w[0], xT, slice(KV_RANK + e * P, KV_RANK + (e + 1) * P), KC)
        last_use(latent_w[1], "kr1")
        wq, rec = take(rows(a["b_w_dq"][0], 0, Q_RANK), KC, Q_RANK)
        for tb in range(TB):
            tok(f"cq_{tb}", xT, wq, tb, Q_RANK, KC)
        last_use(rec, "cq_1")
        for tb in range(TB):
            pe.wait_ge(sem("ckv_ready"), tb + 1)
            o = open_(f"ckvT_{tb}_0")
            for k in range(2):
                ins = nc.tensor.transpose(o[:, k * P:(k + 1) * P], M["ckv" if tb == 0 else "ckv2"][:, k * P:(k + 1) * P], ident[:, :])
            close(ins, f"ckvT_{tb}_0")
        transposes("cqT", M["cq"], 3, range(TB), sem("cq_ready"), 0)
        await_T("ckvT", 2)
        wu, rec = take(rows(a["kv_w_up"], 0, 2048), 2, 2048)
        for h in range(H):
            featT(f"kn{h}", wu, M["ckvT"], slice(h * 256, h * 256 + 128), 2)
        wv = ring[:, rec["slot"], 0:4096].rearrange("p (k h e n) -> p k h e n", k=2, h=H, e=2)
        for half in range(2):
            for tb in range(TB):
                nm = f"kvv_{tb}_{half}"
                o = open_(nm)
                for k in range(2):
                    ins = mm(o[:, :], M["ckvT"][:, k, tb * P:(tb + 1) * P], wv[:, k, half * 4:half * 4 + 4, 1, :],
                             k == 0, k == 1)
                close(ins, nm)
        last_use(rec, "kvv_1_1")
        await_T("cqT", 3)
        for half in range(2):
            w, rec = take(rows(a["b_w_uq_p"], half * 768, 768), 3, 768)
            for j in range(4):
                featT(f"qn{half * 4 + j}", w, M["cqT"], slice(j * P, (j + 1) * P), 3)
            for e in range(2):
                featT(f"qr{half}_{e}", w, M["cqT"], slice((4 + e) * P, (5 + e) * P), 3)
            last_use(rec, f"qr{half}_1")

        def attn_T(nm, E):
            o = open_(nm)
            for j in range(3):
                ins = nc.tensor.transpose(o[:, j * P:(j + 1) * P], E[:, j * P:(j + 1) * P], ident[:, :])
            close(ins, nm)

        def lS(h):
            if h == 0:
                for e in range(H):
                    moved(pe, f"kn{e}")
                    moved(pe, f"qn{e}")
            if h % 4 == 0:
                pe.wait_ge(sem("rope"), 2 + h // 4)
            o = open_(f"lS{h}")
            for tb in range(TB):
                c0, n = tb * P, (tb + 1) * P
                ts = slice(tb * P, (tb + 1) * P)
                mm(o[:, c0:c0 + n], M["qnT"][:, h, ts], M["knT"][:, h, 0:n], True, False)
                for e in range(2):
                    ins = mm(o[:, c0:c0 + n], M["R"][:, h // 4, e, ts], M["krm"][:, h % 4, e, 0:n], False, e == 1)
            close(ins, f"lS{h}")

        def lO(h):
            moved(pe, f"lT{h}")
            if h == 0:
                for tb in range(TB):
                    for half in range(2):
                        moved(pe, f"kvv_{tb}_{half}")
            o = open_(f"lO{h}")
            pt = M["PT"][:, h % 4, :]
            mm(o[:, 0:T], M["v"][:, 0, h * P:(h + 1) * P], pt[:, 0:T], True, False)
            close(mm(o[:, P:T], M["v"][:, 1, h * P:(h + 1) * P], pt[:, T:384], False, True), f"lO{h}")

        lS(0)
        lS(1)
        for h in range(H):
            if h + 2 < H:
                lS(h + 2)
            pe.wait_ge(sem("probs"), h + 1)
            attn_T(f"lT{h}", M["E"][:, h % 3, :])
            if h:
                lO(h - 1)
        lO(H - 1)
        for h in range(H):
            moved(pe, f"lO{h}")
        aux(lnp[:, :, :], a["lnp"][1, 0], "lnp", (sem("x_ready"), TB * 3))
        out_proj("mix1", M["oT"], a["b_w_out"][0], ADA_COLS[6:8])
        peer(1, 4)
        ple(1, 4)

        transposes("xT6", yt, KC, range(TB), sem("xn_ready"), 0)
        await_T("xT6")
        w_in = a["w_in_2r"]
        w, rec = take(rows(w_in, 0, 512), KC, 512)
        for ch in range(4):
            featT(f"nq{ch}", w, xT, slice(ch * P, (ch + 1) * P), KC)
        last_use(rec, "nq3")
        ada_load(ADA_GATES[0])
        w, rec = take(rows(w_in, 512, 512), KC, 512)
        for kv in range(2):
            o = open_(f"cmp{kv}")
            for g in range(2):
                for k in range(KC):
                    ins = mm(o[:, g * T:(g + 1) * T], w[:, k, (2 * kv + g) * P:(2 * kv + g + 1) * P], xT[:, k, :],
                             k == 0, k == KC - 1)
            close(ins, f"cmp{kv}")
        last_use(rec, "cmp1")
        ada_load(ADA_GATES[1])
        ada_sum(ADA_GATES[0])
        w, rec = take(rows(w_in, 1024, 512), KC, 512)
        for i, nm in enumerate(("ks0", "ks1", "kw0", "kw1")):
            featT(nm, w, xT, slice(i * P, (i + 1) * P), KC)
        last_use(rec, "kw1")
        w, rec = take(rows(w_in, 1536, 280), KC, 280)
        for tb in range(TB):
            tok(f"vs{tb}", xT, w, tb, P, KC, cols=slice(0, P))
        ada_sum(ADA_GATES[1])
        for tb in range(TB):
            tok(f"vw{tb}", xT, w, tb, 152, KC, cols=slice(P, P + 152))
        last_use(rec, "vw1")
        for kv in range(2):
            w, rec = take(a[f"cmp_w1_{'kv'[kv]}_2"][0].rearrange("(l p) m -> p l m", p=P), 16, P)
            if kv == 0:
                pe.wait_ge(sem("ckin_ready"), 1)
            else:
                pe.wait_ge(sem("ckin_ready"), 2)
            nm = f"ch{kv}"
            o = open_(nm)
            for l in range(16):
                ins = mm(o[:, 0:2 * CW], w[:, l, :], ckin[:, kv, l, :], l == 0, l == 15)
            close(ins, nm)
            last_use(rec, nm)
        moved(pe, "ch0")
        moved(pe, "ch1")
        o = open_("kc")
        close(mm(o[:, 0:2 * CW], N["w2"][:, 0:2, :].rearrange("p a b -> p (a b)"),
                 N["hid"].rearrange("p g n -> p (g n)")), "kc")
        o = open_("vc")
        close(mm(o[:, 0:HD], N["hidv"].rearrange("p g r n -> p (g r n)"), N["w2"][:, 2, :]), "vc")
        moved(pe, "kc")
        for ch in range(4):
            moved(pe, f"nq{ch}")
        for e in range(2):
            o = open_(f"cS{e}")
            r = slice(e * 64, e * 64 + 64)
            for tb in range(TB):
                for i in range(4):
                    ins = mm(o[:, (tb * 4 + i) * CW:(tb * 4 + i + 1) * CW], N["qT"][r, i, tb * P:(tb + 1) * P],
                             N["kc"][r, i // 2, :])
            close(ins, f"cS{e}")

        for nm, c0 in (("bq", 1816), ("bk", 2328)):
            w, rec = take(rows(w_in, c0, 512), KC, 512)
            ada_load(ADA_GATES[2 + (nm == "bk")])
            for ch in range(4):
                featT(f"{nm}{ch}", w, xT, slice(ch * P, (ch + 1) * P), KC)
            last_use(rec, f"{nm}3")
        w, rec = take(rows(w_in, 2840, 512), KC, 512)
        for tb in range(TB):
            tok(f"bv{tb}", xT, w, tb, 512, KC)
            ada_sum(ADA_GATES[2 + tb])
        last_use(rec, "bv1")
        pe.wait_ge(sem("cprobs"), 1)
        o = open_("cT")
        for tb in range(TB):
            ins = nc.tensor.transpose(o[:, tb * P:(tb + 1) * P],
                                      N["cE"][:, tb, :, :].rearrange("p h n -> p (h n)"), ident[:, :])
        close(ins, "cT")

        for nm in ("ks0", "ks1", "kw0", "kw1", "vs0", "vs1", "vw0", "vw1", "vc", "cT"):
            moved(pe, nm)

        def nS(i):
            h, win_ = i // 2, i % 2
            kT = N["kwT"] if win_ else N["ksT"]
            r = slice((h % 2) * 64, (h % 2) * 64 + 64)
            o = open_(f"nS{i}")
            for tb in range(TB):
                ins = mm(o[:, tb * P:tb * P + (tb + 1) * P], N["qT"][r, h // 2, tb * P:(tb + 1) * P],
                         kT[r, h // 4, 0:(tb + 1) * P])
            close(ins, f"nS{i}")

        def nO(h):
            moved(pe, f"nT{2 * h}")
            moved(pe, f"nT{2 * h + 1}")
            o = open_(f"nO{h}")
            g = h // 4
            r = slice((h % 2) * 64, (h % 2) * 64 + 64)
            mm(o[r, 0:T], N["vcm"][:, h, :], N["cPT"], True, False)
            for j in range(2):
                vv = (N["vw"] if j else N["vs"])
                pt = N["PT"][:, (2 * h + j) % 4, :]
                mm(o[r, 0:T], vv[:, 0, g * HD:(g + 1) * HD], pt[:, 0:T], False, False)
                ins = mm(o[r, P:T], vv[:, 1, g * HD:(g + 1) * HD], pt[:, T:384], False, j == 1)
            close(ins, f"nO{h}")

        for ch in range(4):
            moved(pe, f"bq{ch}")
            moved(pe, f"bk{ch}")
        for tb in range(TB):
            moved(pe, f"bv{tb}")

        def bS(h):
            r = slice((h % 2) * 64, (h % 2) * 64 + 64)
            o = open_(f"bS{h}")
            mm(o[:, 0:T], N["kbT"][r, h // 2, 0:P], N["qbT"][r, h // 2, :])
            close(mm(o[:, T:384], N["kbT"][r, h // 2, P:T], N["qbT"][r, h // 2, P:T]), f"bS{h}")

        def bL(h):
            pe.wait_ge(sem("keep"), h + 1)
            lk = sbk[:, 2 + h % 2, :]
            o = open_(f"bL{h}")
            mm(o[:, 0:T], upper[:, :], lk[:, 0:T], True, False)
            mm(o[:, P:T], ones[:, :], lk[:, T:384], False, True)
            close(mm(o[:, T:384], upper[:, :], lk[:, T:384]), f"bL{h}")

        def bO(h):
            pe.wait_ge(sem("broken"), h + 1)
            pt = sbp[:, h % 2, :]
            o = open_(f"bO{h}")
            r = slice((h % 2) * 64, (h % 2) * 64 + 64)
            v = [N["vb"][:, b, h * HD:(h + 1) * HD] for b in range(2)]
            mm(o[r, 0:T], v[0], pt[:, 0:T], True, False)
            close(mm(o[r, P:T], v[1], pt[:, T:384], False, True), f"bO{h}")

        gate_w = [None]

        def mg(ch):
            if ch % 4 == 0:
                gate_w[0] = take(rows(w_in, 3352 + ch // 4 * 512, 512), KC, 512)
            w, rec = gate_w[0]
            e = ch % 4
            featT(f"mg{ch}", w, xT, slice(e * P, (e + 1) * P), KC)
            if e == 3:
                last_use(rec, f"mg{ch}")

        nS(0)
        nS(1)
        bS(0)
        for h in range(H):
            i = 2 * h
            if h + 1 < H:
                nS(i + 2)
                bS(h + 1)
            mg(i)
            pe.wait_ge(sem("nprobs"), i + 1)
            attn_T(f"nT{i}", N["E"][:, i % 3, :])
            if h:
                nO(h - 1)
            if h + 1 < H:
                nS(i + 3)
            bL(h)
            mg(i + 1)
            pe.wait_ge(sem("nprobs"), i + 2)
            attn_T(f"nT{i + 1}", N["E"][:, (i + 1) % 3, :])
            if h:
                bO(h - 1)
        nO(H - 1)
        bO(H - 1)

        wa, ra = take(rows(a["w_proj_a_2"][0], 0, D), 4, D)
        wb, rb = take(rows(a["w_proj_b_2"][0], 0, D), 4, D)
        for h in range(H):
            moved(pe, f"nO{h}")
            moved(pe, f"bO{h}")
        for ch in range(KC):
            featT(f"ya{ch}", wa, N["oaT"], slice(ch * P, (ch + 1) * P), 4)
            featT(f"yb{ch}", wb, N["obT"], slice(ch * P, (ch + 1) * P), 4)
        last_use(ra, f"ya{KC - 1}")
        last_use(rb, f"yb{KC - 1}")
        pe.wait_ge(sem("yT"), KC)
        out_proj("mix2", xT, a["w_out_2"][0])

        transposes("xT7", yt, KC, range(TB), sem("xn_ready"), TB)
        await_T("xT7")
        for j in range(0, FF, 512):
            n = min(512, FF - j)
            wg, r1 = take(rows(a["w_ffn_gate_2"][0], j, n), KC, n)
            wu_, r2 = take(rows(a["w_ffn_up_2"][0], j, n), KC, n)
            for e in range(n // P):
                ch = j // P + e
                featT(f"fg{ch}", wg, xT, slice(e * P, (e + 1) * P), KC)
                featT(f"fu{ch}", wu_, xT, slice(e * P, (e + 1) * P), KC)
            last_use(r1, f"fg{ch}")
            last_use(r2, f"fu{ch}")
        aux(lnp[:, 0, :], a["nfg"], "lnp", (sem("x_ready"), TB * 6))
        pe.wait_ge(sem("hid"), FC)
        names = [(tb, half) for tb in range(TB) for half in range(2)]
        o = {x: open_(f"dn_{x[0]}_{x[1]}") for x in names}
        for j in range(0, FC, 4):
            n = min(4, FC - j)
            w, rec = take(a["w_ffn_down_2"][0][j * P:(j + n) * P, :].rearrange("(k p) n -> p k n", p=P), n, D)
            for x in names:
                for k in range(n):
                    ins = mm(o[x][:, :], F["hid"][:, j + k, x[0] * P:(x[0] + 1) * P],
                             w[:, k, x[1] * 512:x[1] * 512 + 512], j + k == 0, j + k == FC - 1)
                if j + n == FC:
                    close(ins, f"dn_{x[0]}_{x[1]}")
            if j + n < FC:
                ins.then_inc(sem("down_used"), 1)
                rec["done"] = (sem("down_used"), j // 4 + 1)

    @block.sync
    def _(sp):
        sp.dma_start(xT[:, :, :], a["xTin"].rearrange("(k p) t -> p k t", p=P)).then_inc(sem("xT_loaded"), 16)
        done_of = {}
        for r in loads:
            if r["kind"] == "w":
                if r["i"] >= NW:
                    s, v = done_of[r["i"] - NW]
                    sp.wait_ge(s, v)
                dst = ring[0:r["p"], r["slot"], 0:r["kc"] * r["n"]].rearrange("p (k n) -> p k n", k=r["kc"])
                sp.dma_start(dst, r["src"]).then_inc(slot_loaded[r["slot"]], 16)
                done_of[r["i"]] = r["done"]
            else:
                if r["after"]:
                    sp.wait_ge(*r["after"])
                sp.dma_start(r["dst"], r["src"]).then_inc(r["sem"], 16)
        for tb in range(TB):
            sp.wait_ge(sem("out_ready"), tb + 1)
            sp.dma_start(out[tb * P:(tb + 1) * P, :], yt[:, tb, :]).then_inc(sem("out_done"), 16)
        sp.wait_ge(sem("out_done"), 16 * TB)

    @block.gpsimd
    def _(pool):
        step = Steps(pool, "pool_step")
        pool.dma_start(cT[:, :], a["cT"]).then_inc(sem("c_loaded"), 16)
        pool.dma_start(A["bif"][:, :], a["bif"]).then_inc(sem("bif_loaded"), 16)
        for t, v in ((ident, 0.0), (ones, 1.0), (upper, 1.0), (maskT, 0.0), (maskS, 0.0), (keep, 1.0), (maskQ, 0.0)):
            step.go(pool.memset(t[:, :], v))
        step.go(pool.memset(A["sel"], 0.0))
        step.wait()

        def select(v, pattern, base, op, fill, ch):
            step.go(pool.affine_select(out=v, in_=v, compare_op=op, fill=fill, base=base, pattern=pattern,
                                       channel_multiplier=ch))
        select(ident[:, :], [[-1, P]], 0, ALU.not_equal, 1.0, 1)
        select(upper[:, :], [[-1, P]], 0, ALU.is_gt, 0.0, 1)
        for c0 in (0, T):
            select(maskT[:, c0:c0 + P], [[1, P]], 0, ALU.is_ge, NEG, -1)
            select(maskS[:, c0:c0 + P], [[1, P]], 0, ALU.is_gt, NEG, -1)
            select(keep[:, c0:c0 + P], [[1, P]], 0, ALU.is_gt, 0.0, -1)
            select(maskQ[:, c0:c0 + P], [[-1, P]], 0, ALU.is_ge, NEG, 1)
        select(A["sel"], [[-1, H], [0, P]], 0, ALU.not_equal, 1.0, 1)
        step.go(pool.iota(iota16[:, :], [[1, 16]], base=0, channel_multiplier=0,
                          allow_small_or_imprecise_dtypes=True))
        step.wait()
        pool.tensor_scalar(identa[:, :], ident[:, :], ALPHA, None, ALU.mult).then_inc(sem("consts"), 1)
        pool.wait_ge(sem("gates"), 1)
        for dst, src in ((xt[:, :, :], a["x"].rearrange("(b p) d -> p b d", p=P)), (A["g"][:, :], a["hng"]),
                         (posi[:, :], a["pos"]), (invf[:, :], a["invf"])):
            pool.dma_start(dst, src).then_inc(sem("small"), 16)

        def gathers(l, tb):
            r = l * TB + tb
            for u in range(UNITS):
                pool.wait_ge(sem("experts"), r * UNITS + u + 1)
                with pool.Fori(u * UITERS, (u + 1) * UITERS) as it:
                    gather_turn(l, tb, it)

        def gather_turn(l, tb, it):
            r = l * TB + tb
            for g in range(NG):
                pool.wait_ge(sem("row_free"), r * PAIRS + it * SLOTS + (g + 1) * GRP)
                pool.sem_inc(sem("gather_go"), 1)
                pool.tensor_copy(idc[:, g * GRP:(g + 1) * GRP],
                                 eidx[:, tb, bass.ds(it * SLOTS + g * GRP, GRP)]).then_inc(sem("idc_set"), 1)
                pool.wait_ge(sem("idc_set"), (r * ITERS + it) * NG + g + 1)
                pool.sem_inc(sem("gather_go"), 1)
                for s in range(g * GRP, (g + 1) * GRP):
                    pool.indirect_dma_start(gath[:, s, :], None, a["uv"],
                                            bass.IndirectOffsetOnAxis(ap=idc[:, s:s + 1], axis=0)
                                            ).then_inc(sem(f"row{s}"), 16)

        for tb in range(TB):
            gathers(0, tb)
        pool.wait_ge(sem("x_ready"), TB * 3)
        pool.dma_start(M["cg"], a["kvg"]).then_inc(sem("mla_par"), 16)
        pool.dma_start(M["qg"], a["qng"]).then_inc(sem("mla_par"), 16)
        for tb in range(TB):
            gathers(1, tb)
        pool.wait_ge(sem("x_ready"), TB * 4 + 3)
        for dst, src in ((N["bada"], a["badaT"]), (N["ng"], a["ngT"]),
                         (N["posc"], a["posc"]), (N["w2"], a["cmp_w2"]), (N["g1"], a["bg1"]), (N["g2"], a["bg2"])):
            pool.dma_start(dst, src).then_inc(sem("hyb_par"), 16)
        step.go(pool.iota(N["dist"][:, 0:P], [[-1, P]], base=0, channel_multiplier=1,
                          allow_small_or_imprecise_dtypes=True))
        step.go(pool.iota(N["dist"][:, P:384], [[-1, T]], base=P, channel_multiplier=1,
                          allow_small_or_imprecise_dtypes=True))
        for tb in range(TB):
            step.go(pool.iota(N["cdist"][:, tb, :], [[-16, CW]], base=P * tb - 31, channel_multiplier=1,
                              allow_small_or_imprecise_dtypes=True))
        step.go(pool.memset(ckin[:, :, :, :], 0.0))
        step.go(pool.memset(N["m8"], 1.0))
        step.go(pool.memset(N["rv"], 1.0))
        step.wait()
        select(N["dist"][:, 0:P], [[-1, P]], 0, ALU.is_ge, FAR, 1)
        select(N["dist"][:, T:384], [[-1, P]], 0, ALU.is_ge, FAR, 1)
        for tb in range(TB):
            select(N["cdist"][:, tb, :], [[-16, CW]], P * tb - 31, ALU.is_ge, FAR, 1)
        select(N["m8"], [[-16, 8]], 0, ALU.is_ge, 0.0, 1)
        select(N["rv"][:, 0:1], [[0, 1]], -31, ALU.is_ge, 0.0, 1)
        step.wait()
        select(N["m8"], [[16, 8]], 15, ALU.is_ge, 0.0, -1)
        select(N["cdist"][:, 1, CW - 1:CW], [[0, 1]], -1, ALU.is_ge, FAR, 0)
        step.wait()
        for tb in range(TB):
            for h in range(H):
                step.go(pool.tensor_scalar(N["cb"][:, tb, h, :], N["cdist"][:, tb, :], -SLOPES[h], None, ALU.mult))
        step.wait()
        pool.engine_nop().then_inc(sem("hyb_const"), 1)
        for h in range(H):
            if h >= 2:
                pool.wait_ge(sem("bias_used"), h - 1)
            pool.tensor_scalar(N["bh"][:, h % 2, :], N["dist"], -SLOPES[h], None, ALU.mult
                               ).then_inc(sem("bias_ready"), 1)

    @block.scalar
    def _(act):
        step = Steps(act, "act_step")
        nsq = [0]

        def f(o, i, fn, **kw):
            return nc.scalar.activation(o, i, fn, **kw)

        def evac(name, dst, src=None, fn=ACT.Copy, **kw):
            ps = full(act, name)
            free(f(dst, ps[:, 0:T] if src is None else src(ps), fn, **kw), name)

        def sqrt(cols):
            nsq[0] += 1
            act.wait_ge(sem("var_ready"), nsq[0])
            f(sdv[:, 0:cols], var[:, 0:cols], ACT.Sqrt).then_inc(sem("sd_ready"), 1)

        def evac_T(name, dst, chunks=KC, tbs=range(TB)):
            for tb in tbs:
                for g in range(-(-chunks // 4)):
                    n = min(4, chunks - 4 * g)
                    evac(f"{name}_{tb}_{g}", dst[:, 4 * g:4 * g + n, tb * P:(tb + 1) * P],
                         lambda ps, n=n: ps[:, 0:n * P].rearrange("p (k t) -> p k t", k=n))

        act.wait_ge(sem("c_loaded"), 16)
        f(scT[:, :], cT[:, :], ACT.Silu).then_inc(sem("silu_c"), 1)
        act.wait_ge(sem("abs_ready"), 1)
        step(f(A["ex"], A["ax"], ACT.Exp, scale=-1.0))
        f(A["lf"], A["ex"], ACT.Ln, bias=1.0).then_inc(sem("log1p"), 1)
        for ch in range(4):
            evac(f"q{ch}", A["qT"][:, ch, :])
        for ch in range(4):
            evac(f"k{ch}", A["kT"][:, ch, :], scale=QK ** -0.5)
        ps = full(act, "acol")
        step.go(f(A["acol"].rearrange("p b h -> p (b h)"), ps[:, 0:16], ACT.Copy))
        free(f(A["enm"].rearrange("p b h -> p (b h)"), ps[:, 16:32], ACT.Exp, scale=-1.0), "acol")
        for half in range(2):
            for tb in range(TB):
                evac(f"v_{tb}_{half}", A["v"][:, tb, half * 4:half * 4 + 4, 0:128],
                     lambda ps: ps[:, :].rearrange("p (h n) -> p h n", h=4))
        for h in range(H):
            act.wait_ge(sem("m_arg"), h + 1)
            f(A["tm"][:, h % 2, :], A["tm"][:, h % 2, :], ACT.Exp).then_inc(sem("m_exp"), 1)
            if h in (2, 3):
                evac(f"og_0_{h - 2}", A["og"][:, 0, (h - 2) * 512:(h - 1) * 512], lambda ps: ps[:, :])
        sqrt(16)
        moved(act, "og_0_1")
        f(A["og"][:, 0, :], A["og"][:, 0, :], ACT.Sigmoid).then_inc(sem("og_ready"), 1)
        for half in range(2):
            evac(f"og_1_{half}", A["og"][:, 1, half * 512:half * 512 + 512], lambda ps: ps[:, :], fn=ACT.Sigmoid)
        evac_T("hT", A["hT"])
        for tb in range(TB):
            sqrt(1)

        def peer(l, xv):
            evac_T(f"xT{xv}", xT)

            def scores(tb, j):
                evac(f"sc{l}_{tb}_{j}", sc[:, tb, j * 4:j * 4 + 4, :],
                     lambda ps: ps[:, :].rearrange("p (c n) -> p c n", c=4))

            def gate_exp(n):
                act.wait_ge(sem("gate_arg"), l * TB * UNITS + n + 1)
                f(tsv[:, :, :], tsv[:, :, :], ACT.Exp).then_inc(sem("gate_exp"), 1)

            def gelus(tb, it):
                for g in range(NG):
                    act.wait_ge(sem("dots"), (l * TB + tb) * PAIRS + it * SLOTS + (g + 1) * GRP)
                    f(glu[:, g * GRP:(g + 1) * GRP], dots[:, g * GRP:(g + 1) * GRP], ACT.Gelu
                      ).then_inc(sem("gelu"), 1)

            for j in range(4):
                for e in range(4):
                    evac(f"pq{l}_{j * 4 + e}", pq[:, j * 4 + e, :])
                    if j >= 2 and e == 0:
                        scores(0, j - 1)
                        if j == 2:
                            gate_exp(0)
                    if j == 3 and e == 1:
                        gate_exp(1)
                        gelus(0, 0)
                if j == 0:
                    scores(0, 0)
            for tb, j in ((1, 0), (1, 1), (1, 2), (0, 3), (1, 3)):
                scores(tb, j)
            for n in range(2, TB * UNITS):
                for it in range(1 + SPREAD * (n - 2), 1 + SPREAD * (n - 1)):
                    gelus(0, it)
                gate_exp(n)
            with act.Fori(WOVEN, ITERS) as it:
                gelus(0, it)
            sqrt(1)
            gelus(1, 0)
            evac_T(f"xP{l}", xT, tbs=[0])
            gelus(1, 1)
            for half in range(2):
                gelus(1, 2 + half)
                ple_gate(l, 0, half)
            with act.Fori(4, ITERS) as it:
                gelus(1, it)
            sqrt(1)

        def ple_gate(l, tb, half):
            evac(f"pg{l}_{tb}_{half}", yt[:, tb, half * 512:half * 512 + 512], lambda ps: ps[:, :], fn=ACT.Sigmoid)

        def ple(l):
            evac_T(f"xP{l}", xT, tbs=[1])
            for half in range(2):
                ple_gate(l, 1, half)

        def latent(tb):
            evac_T("xT3", xT, tbs=[tb])
            evac(f"ckv_{tb}", yt[:, tb, 0:KV_RANK], lambda ps: ps[:, 0:KV_RANK])

        peer(0, 1)
        latent(0)
        ple(0)

        latent(1)
        act.wait_ge(sem("ang_ready"), 1)
        f(M["sin"], M["w1"], ACT.Sin).then_inc(sem("trig"), 1)
        f(M["cos"], M["w2"], ACT.Sin).then_inc(sem("trig"), 1)
        for e in range(2):
            evac(f"kr{e}", M["t"][:, e, :])
        for tb in range(TB):
            evac(f"cq_{tb}", yt[:, tb, 512:512 + Q_RANK], lambda ps: ps[:, 0:Q_RANK])
        sqrt(4)
        evac_T("ckvT", M["ckvT"], 2)
        evac_T("cqT", M["cqT"], 3)
        for h in range(H):
            evac(f"kn{h}", M["knT"][:, h, :])
        for half in range(2):
            for tb in range(TB):
                evac(f"kvv_{tb}_{half}", M["v"][:, tb, half * 512:half * 512 + 512], lambda ps: ps[:, :])
        for half in range(2):
            for j in range(4):
                evac(f"qn{half * 4 + j}", M["qnT"][:, half * 4 + j, :])

        def softmax_exp(i, E, ready, done):
            act.wait_ge(sem(ready), i + 1)
            for tb in range(TB):
                c0 = tb * P
                c1 = c0 + (tb + 1) * P
                ins = f(E[:, i % 3, c0:c1], E[:, i % 3, c0:c1], ACT.Exp, bias=rmax[:, i % 3, tb:tb + 1],
                        accum_out=rsum[:, i % 3, tb:tb + 1])
                if tb == 0:
                    step.go(ins)
            ins.then_inc(sem(done), 1)

        def lT(h):
            if h >= 4:
                full(act, f"lO{h - 4}")
            evac(f"lT{h}", M["PT"][:, h % 4, :], lambda ps: ps[:, 0:384])

        for h in range(H):
            softmax_exp(h, M["E"], "l_max", "l_exp")
            if h >= 1:
                lT(h - 1)
            if h >= 2:
                evac(f"lO{h - 2}", M["oT"][:, h - 2, :])
        lT(H - 1)
        for h in (H - 2, H - 1):
            evac(f"lO{h}", M["oT"][:, h, :])
        for tb in range(TB):
            sqrt(1)
        peer(1, 4)
        sqrt(1)
        ple(1)

        sqrt(1)
        act.wait_ge(sem("mod_ready"), 1)

        def evac_norm(name, j):
            for tb in range(TB):
                for g in range(2):
                    ps = full(act, f"{name}_{tb}_{g}")
                    for e in range(4):
                        k = 4 * g + e
                        ins = f(xT[:, k, tb * P:(tb + 1) * P], ps[:, e * P:(e + 1) * P], ACT.Identity,
                                scale=N["gs"][:, j, k:k + 1], bias=N["mod"][:, 2 * j, k:k + 1])
                        if e < 3:
                            step.go(ins)
                    free(ins, f"{name}_{tb}_{g}")

        evac_norm("xT6", 0)
        for ch in range(4):
            evac(f"nq{ch}", N["qT"][:, ch, :])
        for kv in range(2):
            ps = full(act, f"cmp{kv}")[:, :].rearrange("p (g t) -> p g t", g=2)
            step.go(f(kcv[0:HD, 2 * kv:2 * kv + 2, :], ps[0:HD, :, :], ACT.Copy))
            step.wait()
            free(f(kcv[HD:P, 2 * kv:2 * kv + 2, 0:T - 1], ps[HD:P, :, 1:T], ACT.Copy), f"cmp{kv}")
        for g in range(2):
            evac(f"ks{g}", N["ksT"][:, g, :])
        for g in range(2):
            evac(f"kw{g}", N["kwT"][:, g, :])
        for tb in range(TB):
            evac(f"vs{tb}", N["vs"][:, tb, :], lambda ps: ps[:, 0:P])
        for tb in range(TB):
            ps = full(act, f"vw{tb}")
            step.go(f(N["vw"][:, tb, :], ps[:, 0:P], ACT.Copy))
            free(f(N["ga"][:, tb, :], ps[:, P:152], ACT.Sigmoid), f"vw{tb}")
        evac("ch0", N["hid"], lambda ps: ps[:, 0:2 * CW].rearrange("p (g n) -> p g n", g=2), fn=ACT.Gelu_apprx_tanh)
        evac("ch1", N["hidv"], lambda ps: ps[:, 0:2 * CW].rearrange("p (g n) -> p g n", g=2).unsqueeze(2)
             .broadcast_to([P, 2, 4, CW]), fn=ACT.Gelu_apprx_tanh)
        evac("kc", N["kc"], lambda ps: ps[:, 0:2 * CW].rearrange("p (g n) -> p g n", g=2))
        for ch in range(4):
            evac(f"bq{ch}", N["qbT"][:, ch, :])
        act.wait_ge(sem("c_arg"), 1)
        f(N["cE"], N["cE"], ACT.Exp).then_inc(sem("c_exp"), 1)
        for ch in range(4):
            evac(f"bk{ch}", N["kbT"][:, ch, :])
        for tb in range(TB):
            evac(f"bv{tb}", N["vb"][:, tb, :], lambda ps: ps[:, :])
        evac("cT", N["cPT"])

        def nT(i):
            if i >= 4:
                full(act, f"nO{(i - 4) // 2}")
            evac(f"nT{i}", N["PT"][:, i % 4, :], lambda ps: ps[:, 0:384])

        def bo(h):
            r = slice((h % 2) * 64, (h % 2) * 64 + 64)
            evac(f"bO{h}", N["obT"][r, h // 2, :], lambda ps: ps[r, 0:T])

        def break_logs(h):
            if h:
                act.wait_ge(sem("keep"), h)
            evac(f"bS{h}", sbk[:, 0, :], lambda ps: ps[:, 0:384], scale=SCALE)
            moved(act, f"bS{h}")
            step(f(sbk[:, 1, :], sbk[:, 0, :], ACT.Abs))
            step(f(sbk[:, 1, :], sbk[:, 1, :], ACT.Exp, scale=-1.0))
            f(sbk[:, 1, :], sbk[:, 1, :], ACT.Ln, bias=1.0).then_inc(sem("b_log"), 1)

        def break_exp(h):
            act.wait_ge(sem("b_arg"), h + 1)
            f(sbp[:, h % 2, :], sbp[:, h % 2, :], ACT.Exp).then_inc(sem("broken"), 1)

        for h in range(H):
            softmax_exp(2 * h, N["E"], "n_max", "n_exp")
            break_logs(h)
            if h:
                nT(2 * h - 1)
            if h >= 2:
                bo(h - 2)
            softmax_exp(2 * h + 1, N["E"], "n_max", "n_exp")
            if h:
                break_exp(h - 1)
            nT(2 * h)
        nT(2 * H - 1)
        break_exp(H - 1)
        bo(H - 2)
        bo(H - 1)
        for ch in range(16):
            moved(act, f"mg{ch}")
        for j in range(4):
            f(N["sgm"][:, 4 * j:4 * j + 4, :], N["sgm"][:, 4 * j:4 * j + 4, :], ACT.Sigmoid).then_inc(sem("merge_gates"), 1)
        for tb in range(TB):
            sqrt(1)
        evac_norm("xT7", 1)
        for ch in range(FC):
            evac(f"fg{ch}", F["hid"][:, ch, :], fn=ACT.Silu)
        for tb in range(TB):
            sqrt(1)

    @block.vector
    def _(dve):
        v = nc.vector
        step = Steps(dve, "dve_step")
        nsq = [0]
        nln = [0]

        def inverse_sd(cols):
            nsq[0] += 1
            dve.wait_ge(sem("sd_ready"), nsq[0])
            step(v.reciprocal(rstd[:, 0:cols], sdv[:, 0:cols]))

        def add_eps(cols, scale, eps):
            v.tensor_scalar(var[:, 0:cols], var[:, 0:cols], scale, eps, ALU.mult, ALU.add
                            ).then_inc(sem("var_ready"), 1)

        def layer_norm(tb, src, frees=()):
            for half in range(2):
                step.go(v.bn_stats(bnst[:, half, :], src[half]))
            step.wait()
            step(v.bn_aggr(mv[:, :], bnst[:, :, :].rearrange("p a b -> p (a b)")))
            v.tensor_scalar(var[:, 0:1], mv[:, 1:2], LN_EPS, None, ALU.add).then_inc(sem("var_ready"), 1)
            inverse_sd(1)
            for half in range(2):
                ins = v.tensor_scalar(yt[:, tb, half * 512:half * 512 + 512], src[half], mv[:, 0:1], rstd[:, 0:1],
                                      ALU.subtract, ALU.mult)
                if frees:
                    free(ins, frees[half])
                    moved(dve, frees[half])
                else:
                    step(ins)
            if tb == 0:
                nln[0] += 1
                dve.wait_ge(sem("lnp"), 16 * nln[0])
            step(v.tensor_tensor(yt[:, tb, :], yt[:, tb, :], lnp[:, 0, :], ALU.mult))
            v.tensor_tensor(xt[:, tb, :], yt[:, tb, :], lnp[:, 1, :], ALU.add).then_inc(sem("x_ready"), 1)

        def residual_norm(name):
            for tb in range(TB):
                for half in range(2):
                    cs = slice(half * 512, half * 512 + 512)
                    ps = full(dve, f"{name}_{tb}_{half}")
                    free(v.scalar_tensor_tensor(yt[:, tb, cs], xt[:, tb, cs], ALPHA, ps[:, :], ALU.mult, ALU.add),
                         f"{name}_{tb}_{half}")
                    moved(dve, f"{name}_{tb}_{half}")
                layer_norm(tb, [yt[:, tb, 0:512], yt[:, tb, 512:1024]])

        def ada_part(j):
            slot, loaded, _ = ada_at[j]
            dve.wait_ge(slot_loaded[slot], loaded)
            w = ring[:, slot, :].rearrange("p (k n) -> p k n", k=KC)
            step(v.tensor_scalar(w[:, 0, :], w[:, 0, :], scT[:, 0:1], None, ALU.mult))
            for k in range(1, KC):
                ins = v.scalar_tensor_tensor(w[:, k, :], w[:, k, :], scT[:, k:k + 1], w[:, k - 1, :], ALU.mult, ALU.add)
                if k < KC - 1:
                    step(ins)
            ins.then_inc(sem("ada_part"), 1)

        def ada_column(j):
            ps = full(dve, f"ada{j}")
            at = ADA_COLS.index(j)
            for e in range(4):
                ins = v.tensor_tensor_reduce(out=junk[:, :], in0=ps[:, e * P:(e + 1) * P], in1=ident[:, :], scale=1.0,
                                             scalar=0.0, op0=ALU.mult, op1=ALU.add,
                                             accum_out=adac[:, at // 2, (at % 2) * 4 + e:(at % 2) * 4 + e + 1])
                if e < 3:
                    step(ins)
            free(ins, f"ada{j}")
            moved(dve, f"ada{j}")

        def ada_gate(j):
            i = ADA_GATES.index(j)
            g = (N["g1"] if i < 2 else N["g2"])[:, (i % 2) * 512:(i % 2) * 512 + 512]
            ps = full(dve, f"ada{j}")
            free(v.tensor_tensor(g, ps[:, :], g, ALU.add), f"ada{j}")
            moved(dve, f"ada{j}")

        dve.wait_ge(sem("bif_loaded"), 16)
        v.memset(A["v"][:, :, :, 128:129], 1.0).then_inc(sem("v_ones"), 1)
        ps = full(dve, "gi")
        free(v.tensor_scalar(A["ig"], ps[0:H, 0:T], A["bif"][:, 0:1], None, ALU.add), "gi")
        ps = full(dve, "gf")
        free(v.tensor_scalar(A["xf"], ps[0:H, 0:T], A["bif"][:, 1:2], None, ALU.add), "gf")
        moved(dve, "gi")
        moved(dve, "gf")
        step.go(v.memset(A["B"], 1.0))
        v.scalar_tensor_tensor(A["ax"], A["xf"], -1.0, A["xf"], ALU.mult, ALU.max).then_inc(sem("abs_ready"), 1)
        dve.wait_ge(sem("log1p"), 1)
        step(v.scalar_tensor_tensor(A["ex"], A["xf"], 0.0, A["lf"], ALU.min, ALU.subtract))
        step(v.tensor_tensor_scan(A["m"], A["B"], A["ex"], 0.0, ALU.mult, ALU.add))
        step(v.tensor_tensor(A["a"], A["ig"], A["m"], ALU.subtract))
        step(v.tensor_tensor_scan(A["M"], A["a"], A["a"], 0.0, ALU.max, ALU.max))
        step(v.tensor_tensor(A["m"], A["m"], A["M"], ALU.add))
        v.tensor_scalar(A["nM"], A["M"], -1.0, None, ALU.mult).then_inc(sem("gates"), 1)
        dve.wait_ge(sem("silu_c"), 1)
        ada_part(ADA_COLS[0])
        for j in range(4):
            nm = f"nb{j}"
            ps = full(dve, nm)
            for e in range(2):
                step.go(v.tensor_tensor(A["negM"][:, 2 * j + e, 0:T], ps[:, e * T:(e + 1) * T], maskT[:, 0:T], ALU.add))
                ins = v.tensor_tensor(A["negM"][:, 2 * j + e, T:384], ps[:, e * T + P:(e + 1) * T], maskT[:, T:384], ALU.add)
                if e == 0:
                    step.go(ins)
            free(ins, nm)
        moved(dve, "nb3")
        step.wait()
        moved(dve, "acol")

        def m_arg(h):
            step.go(v.tensor_scalar(A["tm"][:, h % 2, 0:T], A["negM"][:, h, 0:T], A["acol"][:, 0, h:h + 1], 0.0,
                                    ALU.add, ALU.min))
            v.tensor_scalar(A["tm"][:, h % 2, T:384], A["negM"][:, h, T:384], A["acol"][:, 1, h:h + 1], 0.0,
                            ALU.add, ALU.min).then_inc(sem("m_arg"), 1)

        def m_fin(h):
            ps = full(dve, f"mO{h}")
            o2 = ps[:, 0:258].rearrange("p (b n) -> p b n", b=2)
            d_ = A["den"][:, h % 2, :]
            r_ = A["rden"][:, h % 2, :]
            step(v.tensor_copy(d_, o2[:, :, 128]))
            step(v.scalar_tensor_tensor(d_, d_, -1.0, d_, ALU.mult, ALU.max))
            step(v.tensor_tensor(d_, d_, A["enm"][:, :, h], ALU.max))
            step(v.reciprocal(r_, d_))
            step.go(v.tensor_scalar(A["h"][:, 0, h, :], o2[:, 0, 0:128], r_[:, 0:1], None, ALU.mult))
            free(v.tensor_scalar(A["h"][:, 1, h, :], o2[:, 1, 0:128], r_[:, 1:2], None, ALU.mult), f"mO{h}")
            moved(dve, f"mO{h}")
            for tb in range(TB):
                step.go(v.bn_stats(A["st"][:, tb * H + h, :], A["h"][:, tb, h, :]))

        ada_part(ADA_COLS[1])
        ada_column(ADA_COLS[0])
        m_arg(0)
        m_arg(1)
        ada_part(ADA_COLS[2])
        ada_column(ADA_COLS[1])
        for h in range(H):
            dve.wait_ge(sem("m_exp"), h + 1)
            ps = full(dve, f"mS{h}")
            if h >= 2:
                full(dve, f"mO{h - 2}")
            free(v.tensor_tensor(A["Pm"][:, h % 2, :], A["tm"][:, h % 2, :], ps[:, 0:384], ALU.mult), f"mS{h}")
            if h + 2 < H:
                moved(dve, f"mS{h}")
                m_arg(h + 2)
            if h:
                m_fin(h - 1)
            if h == 1:
                ada_column(ADA_COLS[2])
            if h == 2:
                ada_part(ADA_COLS[3])
            if h == 5:
                ada_column(ADA_COLS[3])
        m_fin(H - 1)
        step.wait()
        st = A["st"]
        step.go(v.tensor_tensor(A["mu"], st[:, :, 1], st[:, :, 4], ALU.add))
        step.go(v.tensor_tensor(A["t1"], st[:, :, 1], st[:, :, 4], ALU.subtract))
        step.go(v.tensor_tensor(A["t2"], st[:, :, 2], st[:, :, 5], ALU.add))
        step.wait()
        step.go(v.tensor_scalar(A["mu"], A["mu"], 0.5, None, ALU.mult))
        step.go(v.tensor_tensor(A["t1"], A["t1"], A["t1"], ALU.mult))
        step.wait()
        step.go(v.tensor_scalar(A["t2"], A["t2"], 1.0 / 128, LN_EPS, ALU.mult, ALU.add))
        step.wait()
        v.scalar_tensor_tensor(var[:, 0:16], A["t1"], 0.25, A["t2"], ALU.mult, ALU.add).then_inc(sem("var_ready"), 1)
        inverse_sd(16)
        dve.wait_ge(sem("small"), 16 * 4)
        for tb in range(TB):
            for h in range(H):
                i = tb * H + h
                step.go(v.tensor_scalar(A["h"][:, tb, h, :], A["h"][:, tb, h, :], A["mu"][:, i:i + 1], rstd[:, i:i + 1],
                                        ALU.subtract, ALU.mult))
            step.wait()
            hv = A["h"][:, tb, :, :].rearrange("p h n -> p (h n)")
            step(v.tensor_tensor(hv, hv, A["g"], ALU.mult))
            if tb == 0:
                dve.wait_ge(sem("og_ready"), 1)
            else:
                for half in range(2):
                    moved(dve, f"og_1_{half}")
            v.tensor_tensor(hv, hv, A["og"][:, tb, :], ALU.mult).then_inc(sem("h_ready"), 1)
        for j in ADA_COLS[4:6]:
            ada_part(j)
        residual_norm("mix0")
        for j in ADA_COLS[4:6]:
            ada_column(j)

        def top16(vals, idx, scores, n):
            for lo in (0, 8):
                if lo:
                    for i in range(n):
                        step.go(v.match_replace(scores[:, i, :], vals[:, i, 0:8], scores[:, i, :], -3.0e38))
                    step.wait()
                    yield
                for i in range(n):
                    step.go(v.max(vals[:, i, lo:lo + 8], scores[:, i, :]))
                step.wait()
                yield
                for i in range(n):
                    step.go(v.max_index(idx[:, i, lo:lo + 8], vals[:, i, lo:lo + 8], scores[:, i, :]))
                step.wait()
                yield

        def choose(l, n):
            tb, u = n // UNITS, n % UNITS
            moved(dve, f"sc{l}_{tb}_{u}")
            yield from top16(v1, i1, sc[:, tb, 2 * UH * u:2 * UH * (u + 1), :], 2 * UH)
            step.go(v.tensor_copy(i1f, i1))
            for h in range(UH):
                step.go(v.tensor_tensor(cand[:, h, :].rearrange("p (i j) -> p i j", i=16),
                                        v1[:, 2 * h, :].unsqueeze(2).broadcast_to([P, 16, 16]),
                                        v1[:, 2 * h + 1, :].unsqueeze(1).broadcast_to([P, 16, 16]), ALU.add))
            step.wait()
            yield
            yield from top16(tsv, tp, cand, UH)
            step.go(v.tensor_scalar(p12[:, 0, :, :], tp[:, :, :], 4, None, ALU.logical_shift_right))
            step.go(v.tensor_scalar(p12[:, 1, :, :], tp[:, :, :], 15, None, ALU.bitwise_and))
            step(v.tensor_copy(gsum[:, :], tsv[:, :, 0]))
            v.tensor_tensor(tsv[:, :, :], tsv[:, :, :], gsum[:, :].unsqueeze(2).broadcast_to([P, UH, 16]),
                            ALU.subtract).then_inc(sem("gate_arg"), 1)
            step(v.tensor_copy(p12f[:, :, :, :].rearrange("p a b c -> p (a b c)"),
                               p12[:, :, :, :].rearrange("p a b c -> p (a b c)")))
            yield
            i4 = i1f[:, :, :].rearrange("p (h c) j -> p h c j", c=2)
            for e in range(2):
                step(v.tensor_tensor(eq, p12f[:, e, :, :].unsqueeze(3).broadcast_to([P, UH, 16, 16]),
                                     iota16[:, :].unsqueeze(1).unsqueeze(1).broadcast_to([P, UH, 16, 16]),
                                     ALU.is_equal))
                step(v.tensor_tensor(eq, eq, i4[:, :, e, :].unsqueeze(2).broadcast_to([P, UH, 16, 16]), ALU.mult))
                step(v.tensor_reduce(i12[:, e, :, :], eq, AX, ALU.add))
                yield
            ev = i12[:, 0, :, :].rearrange("p h k -> p (h k)")
            step(v.scalar_tensor_tensor(ev, ev, float(NK), i12[:, 1, :, :].rearrange("p h k -> p (h k)"),
                                        ALU.mult, ALU.add))
            v.tensor_scalar(eidx[:, tb, u * UPAIRS:(u + 1) * UPAIRS], ev, float(l * NEXP), None, ALU.add
                            ).then_inc(sem("experts"), 1)

        def gates(l, n):
            tb, u = n // UNITS, n % UNITS
            dve.wait_ge(sem("gate_exp"), l * TB * UNITS + n + 1)
            step(v.tensor_reduce(gsum[:, :], tsv[:, :, :], AX, ALU.add))
            step(v.reciprocal(grec[:, :], gsum[:, :]))
            step(v.tensor_tensor(gate[:, tb, u * UPAIRS:(u + 1) * UPAIRS].rearrange("p (h k) -> p h k", h=UH),
                                 tsv[:, :, :], grec[:, :].unsqueeze(2).broadcast_to([P, UH, 16]), ALU.mult))

        def experts(l, tb, it):
            r = l * TB + tb
            for g in range(NG):
                for s in range(g * GRP, (g + 1) * GRP):
                    dve.wait_ge(sem(f"row{s}"), (r * ITERS + it + 1) * 16)
                    v.tensor_tensor_reduce(out=gath[:, s, 0:D], in0=gath[:, s, 0:D], in1=xt[:, tb, :], scale=1.0,
                                           scalar=0.0, op0=ALU.mult, op1=ALU.add, accum_out=dots[:, s:s + 1]
                                           ).then_inc(sem("dots"), 1)
                dve.wait_ge(sem("gelu"), (r * ITERS + it) * NG + g + 1)
                if g == 0:
                    dve.sem_inc(sem("gate_go"), 1)
                    v.tensor_copy(gcur[:, :], gate[:, tb, bass.ds(it * SLOTS, SLOTS)]).then_inc(sem("gcur"), 1)
                    dve.wait_ge(sem("gcur"), r * ITERS + it + 1)
                for s in range(g * GRP, (g + 1) * GRP):
                    v.tensor_scalar(diag[:, s, :], ident[:, :], glu[:, s:s + 1], gcur[:, s:s + 1],
                                    ALU.mult, ALU.mult).then_inc(sem("diag"), 1)
                yield

        def peer(l):
            for _ in choose(l, 0):
                pass
            gates(l, 0)
            for _ in choose(l, 1):
                pass
            for _ in experts(l, 0, 0):
                pass
            gates(l, 1)
            for n in range(2, TB * UNITS):
                pieces = choose(l, n)
                for it in range(1 + SPREAD * (n - 2), 1 + SPREAD * (n - 1)):
                    for _ in experts(l, 0, it):
                        for _ in range(3):
                            next(pieces, None)
                for _ in pieces:
                    pass
                gates(l, n)
            for tb in range(TB):
                if tb == 1:
                    for it in range(5):
                        for _ in experts(l, 1, it):
                            pass
                        if it >= 3:
                            ple_half(l, 0, it - 3)
                    ple_add(l, 0)
                with dve.Fori(WOVEN if tb == 0 else 5, ITERS) as it:
                    for _ in experts(l, tb, it):
                        pass
                nm = [f"pe{l}_{tb}_{half}" for half in range(2)]
                src = [full(dve, x)[:, :] for x in nm]
                layer_norm(tb, src, nm)

        def ple_half(l, tb, half):
            cs = slice(half * 512, half * 512 + 512)
            moved(dve, f"pg{l}_{tb}_{half}")
            ps = full(dve, f"pp{l}_{tb}_{half}")
            free(v.tensor_tensor(yt[:, tb, cs], yt[:, tb, cs], ps[:, :], ALU.mult), f"pp{l}_{tb}_{half}")

        def ple_add(l, tb):
            for half in range(2):
                moved(dve, f"pp{l}_{tb}_{half}")
            v.tensor_tensor(xt[:, tb, :], xt[:, tb, :], yt[:, tb, :], ALU.add).then_inc(sem("x_ready"), 1)

        def ple(l):
            for half in range(2):
                ple_half(l, 1, half)
            ple_add(l, 1)

        peer(0)
        ple(0)

        step(v.tensor_copy(M["posf"], posi[:, :]))
        step(v.tensor_scalar(M["ang"], M["posf"], invf[:, 0:1], None, ALU.mult))
        TWO = 2 * math.pi
        C1 = 6.28125
        C2 = float(np.float32(np.round((TWO - C1) * 2 ** 20) / 2 ** 20))
        C3 = TWO - C1 - C2
        for dst, shift in ((M["w1"], 0.0), (M["w2"], 0.25)):
            step(v.tensor_scalar(M["w3"], M["ang"], 1.0 / TWO, shift, ALU.mult, ALU.add))
            step(v.tensor_scalar(M["w3"], M["w3"], 12582912.0, None, ALU.add))
            step(v.tensor_scalar(M["w3"], M["w3"], -12582912.0, None, ALU.add))
            step(v.scalar_tensor_tensor(dst, M["w3"], -C1, M["ang"], ALU.mult, ALU.add))
            step(v.scalar_tensor_tensor(dst, M["w3"], -C2, dst, ALU.mult, ALU.add))
            step(v.scalar_tensor_tensor(dst, M["w3"], -C3, dst, ALU.mult, ALU.add))
            if shift:
                step(v.tensor_scalar(dst, dst, math.pi / 2, None, ALU.add))
            ins = v.tensor_scalar(dst, dst, 3.1415925, -3.1415925, ALU.min, ALU.max)
            if shift:
                ins.then_inc(sem("ang_ready"), 1)
            else:
                step(ins)
        for tb in range(TB):
            moved(dve, f"ckv_{tb}")
            step.go(v.tensor_tensor_reduce(out=M["oT"][:, tb, :], in0=yt[:, tb, 0:KV_RANK], in1=yt[:, tb, 0:KV_RANK],
                                           scale=1.0, scalar=0.0, op0=ALU.mult, op1=ALU.add,
                                           accum_out=M["ssq"][:, tb:tb + 1]))
            moved(dve, f"cq_{tb}")
            step.go(v.tensor_tensor_reduce(out=M["cq"][:, tb, :], in0=yt[:, tb, 512:512 + Q_RANK],
                                           in1=yt[:, tb, 512:512 + Q_RANK], scale=1.0, scalar=0.0, op0=ALU.mult,
                                           op1=ALU.add, accum_out=M["ssq"][:, 2 + tb:3 + tb]))
        step.wait()
        step.go(v.tensor_scalar(var[:, 0:2], M["ssq"][:, 0:2], 1.0 / KV_RANK, LN_EPS, ALU.mult, ALU.add))
        step.wait()
        v.tensor_scalar(var[:, 2:4], M["ssq"][:, 2:4], 1.0 / Q_RANK, LN_EPS, ALU.mult, ALU.add).then_inc(sem("var_ready"), 1)
        inverse_sd(4)
        dve.wait_ge(sem("mla_par"), 32)
        for tb in range(TB):
            v.scalar_tensor_tensor(M["ckv" if tb == 0 else "ckv2"], yt[:, tb, 0:KV_RANK], rstd[:, tb:tb + 1], M["cg"],
                                   ALU.mult, ALU.mult).then_inc(sem("ckv_ready"), 1)
        for tb in range(TB):
            v.scalar_tensor_tensor(M["cq"][:, tb, :], yt[:, tb, 512:512 + Q_RANK], rstd[:, 2 + tb:3 + tb], M["qg"],
                                   ALU.mult, ALU.mult).then_inc(sem("cq_ready"), 1)
        dve.wait_ge(sem("trig"), 2)

        def rotate(x1, x2, o1, o2, t, names=None):
            step.go(v.tensor_tensor(t[0], x1, M["cos"], ALU.mult))
            step.go(v.tensor_tensor(t[1], x2, M["sin"], ALU.mult))
            step.go(v.tensor_tensor(t[2], x1, M["sin"], ALU.mult))
            ins = v.tensor_tensor(t[3], x2, M["cos"], ALU.mult)
            step.go(ins)
            step.wait()
            step.go(v.tensor_tensor(o1, t[0], t[1], ALU.subtract))
            step.go(v.tensor_tensor(o2, t[2], t[3], ALU.add))
            step.wait()

        moved(dve, "kr0")
        moved(dve, "kr1")
        tt = [M["oT"][:, j, :] for j in range(4)]
        rotate(M["t"][:, 0, :], M["t"][:, 1, :], M["K12"][:, 0, :], M["K12"][:, 1, :], tt)
        step.go(v.memset(M["krm"], 0.0))
        step.wait()
        for j in range(4):
            r = slice(32 * j, 32 * j + 32)
            ins = v.tensor_copy(M["krm"][r, j, :, :], M["K12"][r, :, :])
            if j < 3:
                step.go(ins)
        ins.then_inc(sem("rope"), 1)
        for half in range(2):
            for e in range(2):
                ps = full(dve, f"qr{half}_{e}")
                free(v.tensor_copy(M["t"][:, e, :], ps[:, 0:T]), f"qr{half}_{e}")
                moved(dve, f"qr{half}_{e}")
            rotate(M["t"][:, 0, :], M["t"][:, 1, :], M["R"][:, half, 0, :], M["R"][:, half, 1, :], tt)
            v.tensor_copy(M["w3"][:, 0:1], M["R"][:, half, 1, 0:1]).then_inc(sem("rope"), 1)

        def sm_max(nm, i, E, scale, bias, ready, before):
            ps = full(dve, nm)
            if before:
                full(dve, before)
            free(v.scalar_tensor_tensor(E[:, i % 3, :], ps[:, 0:384], scale, bias, ALU.mult, ALU.add), nm)
            moved(dve, nm)
            step.go(v.tensor_reduce(rmax[:, i % 3, 0:1], E[:, i % 3, 0:P], AX, ALU.max, negate=True))
            v.tensor_reduce(rmax[:, i % 3, 1:2], E[:, i % 3, P:384], AX, ALU.max, negate=True).then_inc(sem(ready), 1)

        def sm_norm(i, E, exp_sem, probs, gcol=None):
            dve.wait_ge(sem(exp_sem), i + 1)
            step(v.reciprocal(rrec[:, i % 3, :], rsum[:, i % 3, :]))
            if gcol is not None:
                step(v.tensor_tensor(rrec[:, i % 3, :], rrec[:, i % 3, :], gcol, ALU.mult))
            step.go(v.tensor_scalar(E[:, i % 3, 0:P], E[:, i % 3, 0:P], rrec[:, i % 3, 0:1], None, ALU.mult))
            v.tensor_scalar(E[:, i % 3, P:384], E[:, i % 3, P:384], rrec[:, i % 3, 1:2], None, ALU.mult
                            ).then_inc(sem(probs), 1)

        for h in range(H):
            sm_max(f"lS{h}", h, M["E"], MLA_SCALE, maskQ[:, :], "l_max", f"lT{h - 3}" if h >= 3 else None)
            if h:
                sm_norm(h - 1, M["E"], "l_exp", "probs")
        sm_norm(H - 1, M["E"], "l_exp", "probs")
        for j in ADA_COLS[6:8]:
            ada_part(j)
        residual_norm("mix1")
        for j in ADA_COLS[6:8]:
            ada_column(j)
        peer(1)

        def rms_rstd(tb):
            step(v.tensor_tensor_reduce(out=yt[:, tb, :], in0=xt[:, tb, :], in1=xt[:, tb, :], scale=1.0,
                                        scalar=0.0, op0=ALU.mult, op1=ALU.add, accum_out=var[:, 0:1]))
            add_eps(1, 1.0 / D, RMS_EPS)
            inverse_sd(1)

        def rms_norm(tb):
            rms_rstd(tb)
            v.tensor_scalar(yt[:, tb, :], xt[:, tb, :], rstd[:, 0:1], None, ALU.mult).then_inc(sem("xn_ready"), 1)

        rms_norm(0)
        ple(1)
        dve.wait_ge(sem("x_ready"), TB * 6)
        rms_norm(1)
        dve.wait_ge(sem("hyb_par"), 16 * 6)
        step(v.tensor_tensor(N["mod"], adac[:, :, :], N["bada"], ALU.add))
        step.go(v.scalar_tensor_tensor(N["gs"][:, 0, :], N["mod"][:, 1, :], 1.0, N["ng"][:, 0, :], ALU.add, ALU.mult))
        v.scalar_tensor_tensor(N["gs"][:, 1, :], N["mod"][:, 3, :], 1.0, N["ng"][:, 1, :], ALU.add, ALU.mult
                               ).then_inc(sem("mod_ready"), 1)
        ada_part(ADA_GATES[0])
        ada_part(ADA_GATES[1])
        for j in ADA_GATES[:2]:
            ada_gate(j)
        dve.wait_ge(sem("hyb_const"), 1)
        for kv in range(2):
            moved(dve, f"cmp{kv}")
            for g in range(2):
                i = 2 * kv + g
                base = kcv[:, i, :].rearrange("p (n l e) -> p e l n", l=8, e=2)[:, 0, :, :]
                pc = N["posc"][:, kv, :]
                for hf in range(2):
                    ins = v.tensor_tensor(ckin[:, kv, hf * 8:hf * 8 + 8, g * CW:g * CW + NCMP], base[:, :, hf:hf + NCMP],
                                          pc[:, hf * 8:hf * 8 + 8].unsqueeze(2).broadcast_to([P, 8, NCMP]), ALU.add)
                    if (g, hf) != (1, 1):
                        step.go(ins)
            ins.then_inc(sem("ckin_ready"), 1)
        ps = full(dve, "vc")
        free(v.tensor_tensor(N["vcm"], ps[:, 0:HD].unsqueeze(1).broadcast_to([P, H, HD]),
                             N["m8"].unsqueeze(2).broadcast_to([P, H, HD]), ALU.mult), "vc")
        cE = N["cE"].rearrange("p b h n -> p (b h) n")
        cmx = N["cmx"].rearrange("p b h -> p (b h)")
        csm = N["csm"].rearrange("p b h -> p (b h)")
        crc = N["crc"].rearrange("p b h -> p (b h)")
        for e in range(2):
            ps = full(dve, f"cS{e}")
            free(v.scalar_tensor_tensor(N["cE"].rearrange("p b (i e) n -> p (b i) e n", e=2)[:, :, e, :],
                                        ps[:, 0:P].rearrange("p (i n) -> p i n", n=CW), SCALE,
                                        N["cb"].rearrange("p b (i e) n -> p (b i) e n", e=2)[:, :, e, :],
                                        ALU.mult, ALU.add), f"cS{e}")
        moved(dve, "cS0")
        moved(dve, "cS1")
        step(v.tensor_reduce(cmx, cE, AX, ALU.max))
        v.tensor_tensor(cE, cE, cmx.unsqueeze(2).broadcast_to([P, 16, CW]), ALU.subtract).then_inc(sem("c_arg"), 1)
        dve.wait_ge(sem("c_exp"), 1)
        step(v.tensor_reduce(csm, cE, AX, ALU.add))
        step(v.reciprocal(crc, csm))
        for tb in range(TB):
            moved(dve, f"vw{tb}")
            ga = N["ga"][:, tb, :].rearrange("p (h e) -> p h e", e=3)
            step(v.scalar_tensor_tensor(N["crc"][:, tb, :], N["crc"][:, tb, :], N["rv"][:, tb:tb + 1], ga[:, :, 0],
                                        ALU.mult, ALU.mult))
        v.tensor_tensor(cE, cE, crc.unsqueeze(2).broadcast_to([P, 16, CW]), ALU.mult).then_inc(sem("cprobs"), 1)

        for j in ADA_GATES[2:]:
            ada_part(j)
            ada_gate(j)

        def gcol(i):
            h, e = i // 2, i % 2
            return N["ga"][:, :, h * 3 + 1 + e]

        def n_item(i):
            h = i // 2
            dve.wait_ge(sem("bias_ready"), h + 1)
            sm_max(f"nS{i}", i, N["E"], SCALE, N["bh"][:, h % 2, :], "n_max", f"nT{i - 3}" if i >= 3 else None)
            if i % 2 == 1:
                dve.sem_inc(sem("bias_used"), 1)
            if i:
                sm_norm(i - 1, N["E"], "n_exp", "nprobs", gcol(i - 1))

        def nO(h):
            r = slice((h % 2) * 64, (h % 2) * 64 + 64)
            ps = full(dve, f"nO{h}")
            free(v.tensor_copy(N["oaT"][r, h // 2, :], ps[r, 0:T]), f"nO{h}")

        def mg(ch):
            ps = full(dve, f"mg{ch}")
            free(v.tensor_copy(N["sgm"][:, ch, :], ps[:, 0:T]), f"mg{ch}")

        def break_sums(h):
            z1 = sbp[:, h % 2, :]
            ps = full(dve, f"bL{h}")
            free(v.tensor_tensor(z1, z1, ps[:, 0:384], ALU.add), f"bL{h}")
            moved(dve, f"bL{h}")
            dve.sem_inc(sem("b_arg"), 1)

        def break_keep(h):
            z, z1, lk = sbk[:, 0, :], sbp[:, h % 2, :], sbk[:, 2 + h % 2, :]
            dve.wait_ge(sem("b_log"), h + 1)
            if h >= 2:
                full(dve, f"bO{h - 2}")
            step(v.scalar_tensor_tensor(z1, z, 0.0, sbk[:, 1, :], ALU.min, ALU.subtract))
            step.go(v.scalar_tensor_tensor(lk, z, -1.0, z1, ALU.mult, ALU.add))
            step.wait()
            step.go(v.tensor_tensor(z1, z1, maskS[:, :], ALU.add))
            v.tensor_tensor(lk, lk, keep[:, :], ALU.mult).then_inc(sem("keep"), 1)
            step.wait()

        for h in range(H):
            n_item(2 * h)
            if h:
                break_sums(h - 1)
                mg(2 * h - 1)
            if h >= 2:
                nO(h - 2)
            n_item(2 * h + 1)
            break_keep(h)
            mg(2 * h)
        sm_norm(2 * H - 1, N["E"], "n_exp", "nprobs", gcol(2 * H - 1))
        break_sums(H - 1)
        mg(2 * H - 1)
        nO(H - 2)
        nO(H - 1)

        for ch in range(KC):
            if ch % 4 == 0:
                dve.wait_ge(sem("merge_gates"), 3 + ch // 4)
            ps = full(dve, f"ya{ch}")
            free(v.tensor_tensor(N["sgm"][:, ch, :], N["sgm"][:, ch, :], ps[:, 0:T], ALU.mult), f"ya{ch}")
            ps = full(dve, f"yb{ch}")
            free(v.tensor_tensor(N["sgm"][:, KC + ch, :], N["sgm"][:, KC + ch, :], ps[:, 0:T], ALU.mult), f"yb{ch}")
            moved(dve, f"ya{ch}")
            moved(dve, f"yb{ch}")
            v.tensor_tensor(xT[:, ch, :], N["sgm"][:, ch, :], N["sgm"][:, KC + ch, :], ALU.add).then_inc(sem("yT"), 1)

        def gated_residual(name, g, then):
            for tb in range(TB):
                for half in range(2):
                    cs = slice(half * 512, half * 512 + 512)
                    nm = f"{name}_{tb}_{half}"
                    ps = full(dve, nm)
                    free(v.tensor_tensor(yt[:, tb, cs], ps[:, :], g[:, cs], ALU.mult), nm)
                    moved(dve, nm)
                v.tensor_tensor(xt[:, tb, :], xt[:, tb, :], yt[:, tb, :], ALU.add).then_inc(sem("x_ready"), 1)
                then(tb)

        def second_norm(tb):
            dve.wait_ge(sem("x_ready"), TB * 6 + tb + 1)
            rms_norm(tb)
        gated_residual("mix2", N["g1"], second_norm)
        for ch in range(FC):
            moved(dve, f"fg{ch}")
            ps = full(dve, f"fu{ch}")
            free(v.tensor_tensor(F["hid"][:, ch, :], F["hid"][:, ch, :], ps[:, 0:T], ALU.mult), f"fu{ch}")
            moved(dve, f"fu{ch}")
            dve.sem_inc(sem("hid"), 1)

        def final_norm(tb):
            dve.wait_ge(sem("x_ready"), TB * 7 + tb + 1)
            rms_rstd(tb)
            dve.wait_ge(sem("lnp"), 16 * 5)
            v.scalar_tensor_tensor(yt[:, tb, :], xt[:, tb, :], rstd[:, 0:1], lnp[:, 0, :], ALU.mult, ALU.mult
                                   ).then_inc(sem("out_ready"), 1)
        gated_residual("dn", N["g2"], final_norm)


def layouts(inputs):
    g = {k: np.asarray(v) for k, v in inputs.items()}
    bc = lambda v: np.ascontiguousarray(np.broadcast_to(v, (P,) + v.shape))
    cols = lambda v: np.ascontiguousarray(v.reshape(-1, P).T)
    d = {k: g[k] for k in ("a_w_in", "a_w_out", "kv_w_up", "b_w_dq", "b_w_out", "peer_w_q",
                           "ple_w_gate", "w_ada_2", "cmp_w1_k_2", "cmp_w1_v_2", "w_proj_a_2", "w_proj_b_2", "w_out_2", "w_ffn_gate_2", "w_ffn_up_2",
                           "w_ffn_down_2")}
    w = g["kv_w_down"]
    r1, r2 = w[:, KV_RANK:KV_RANK + RHALF], w[:, KV_RANK + RHALF:]
    d["kv_w_down_r"] = np.concatenate([w[:, :KV_RANK]] + [r1] * 4 + [r2] * 4, axis=1)
    w = g["b_w_uq"][0].reshape(Q_RANK, 2, 4, 192)
    d["b_w_uq_p"] = np.concatenate([w[..., :128].reshape(Q_RANK, 2, 512), w[..., 128:160].reshape(Q_RANK, 2, 128),
                                    w[..., 160:].reshape(Q_RANK, 2, 128)], axis=2).reshape(Q_RANK, 1536)
    w = g["w_in_2"][0]
    twice = lambda c0: [w[:, c0 + j * HD:c0 + (j + 1) * HD] for j in (0, 0, 1, 1)]
    d["w_in_2r"] = np.concatenate([w[:, :512]] + twice(512) + twice(640) + twice(768) + twice(1024)
                                   + [w[:, 896:1024], w[:, 1152:]], axis=1)
    d["cmp_w2"] = np.ascontiguousarray(np.stack([g["cmp_w2_k_2"][0]] * 2 + [g["cmp_w2_v_2"][0]], axis=1))
    d["x"] = g["x"][0]
    d["xTin"] = np.ascontiguousarray(g["x"][0].T)
    d["pT_wp"] = np.concatenate([g["p"][:, 0].transpose(0, 2, 1), g["ple_w_proj"]], axis=2)
    d["pos"] = bc(g["positions"][0])
    d["invf"] = np.tile((np.float32(THETA) ** (-np.arange(0, ROPE, 2, dtype=np.float32) / np.float32(ROPE))), 4)[:, None].astype(np.float32)
    gb = np.stack([g["ln_g"], g["ln_b"]], axis=2)
    d["lnp"] = np.ascontiguousarray(np.broadcast_to(gb[:, :, None], (DEPTH, 2, P, 2, D)))
    d["hng"] = bc(g["a_hn_g"][0])
    d["bif"] = np.ascontiguousarray(g["a_b_if"][0].T)
    d["kvg"] = bc(g["kv_norm_g"])
    d["qng"] = bc(g["b_q_norm_g"][0])
    d["keysT"] = np.ascontiguousarray(g["peer_sub_keys"].transpose(0, 4, 1, 2, 3).reshape(DEPTH, P, 2048))
    d["uv"] = np.concatenate([g["peer_u"], g["peer_v"]], axis=2).reshape(DEPTH * NEXP, 2 * D)
    d["cT"] = cols(g["c_2"][0])
    b = g["b_ada_2"][0].reshape(6, D)
    d["badaT"] = np.ascontiguousarray(np.stack([cols(b[i]) for i in (0, 1, 3, 4)], axis=1))
    d["bg1"], d["bg2"] = bc(b[2]), bc(b[5])
    d["ngT"] = np.ascontiguousarray(np.stack([cols(g["norm_mix_g_2"][0]), cols(g["norm_ffn_g_2"][0])], axis=1))
    d["nfg"] = bc(g["norm_final_g_2"])
    two = lambda v: v.reshape(16, 2, HD).transpose(1, 2, 0).reshape(P, 16)
    d["posc"] = np.ascontiguousarray(np.stack([two(g["cmp_pos_k_2"][0]), two(g["cmp_pos_v_2"][0])], axis=1))
    return d


def kernel(**inputs):
    import concourse.bacc as bacc
    from concourse.bass_utils import run_bass_kernel_spmd as run
    nc = bacc.Bacc("TRN2", target_bir_lowering=False, num_devices=1)
    d = layouts(inputs)
    aps = {k: nc.dram_tensor("in_" + k, v.shape, mybir.dt.from_np(v.dtype), kind="ExternalInput").ap()
           for k, v in d.items()}
    out = nc.dram_tensor("out", (T, D), F32, kind="ExternalOutput").ap()
    build(nc, aps, out)
    r = run(nc, [{"in_" + k: v for k, v in d.items()}], core_ids=[0])
    return r.results[0]["out"].reshape(1, T, D)
```
